# Optimizing a Trainium2 kernel written in Bass

```python
import jax, jax.numpy as jnp
from jax import lax
import numpy as np

D_MODEL = 1024
BATCH = 1
SEQ = 512
DEPTH = 2

N_A = DEPTH // 2
N_B = DEPTH - N_A
MEM_LEN = 256
MEM_HEADS = 4
MEM_DH = D_MODEL // (2 * MEM_HEADS)
MEM_WIDTH = MEM_HEADS * MEM_DH
GLA_HEADS = 4
GLA_DV = D_MODEL // (2 * GLA_HEADS)
GLA_DK = GLA_DV // 2
GLA_QK = GLA_HEADS * GLA_DK
GLA_V = GLA_HEADS * GLA_DV
GLA_RANK = 16
GLA_TAU = 16.0
GLA_CHUNK = 64
NSA_HEADS = 8
NSA_GROUPS = 2
NSA_HPG = NSA_HEADS // NSA_GROUPS
NSA_DH = D_MODEL // (2 * NSA_HEADS)
NSA_WIDTH = NSA_HEADS * NSA_DH
KV_WIDTH = NSA_GROUPS * NSA_DH
CMP_BLOCK = 32
CMP_STRIDE = 16
CMP_HIDDEN = 256
SEL_BLOCK = 64
SEL_TOPN = 16
WINDOW = 512
Q_BLOCK = 128
FFN_DIM = ((8 * D_MODEL // 3 + 127) // 128) * 128
CONV_WIDTH = 3
EPS = 1e-6
A_PROJ = 2 * GLA_QK + 2 * GLA_V + GLA_RANK + MEM_WIDTH
B_PROJ = NSA_WIDTH + 3 * NSA_HEADS + MEM_WIDTH
SHARED_KV_PROJ = 6 * KV_WIDTH


F32 = jnp.float32

def rmsnorm(x, g):
    xf = x.astype(F32)
    y = xf * lax.rsqrt(jnp.mean(xf * xf, axis=-1, keepdims=True) + EPS)
    return y.astype(x.dtype) * g

def split_cols(z, widths):
    idx = [int(i) for i in np.cumsum(widths)[:-1]]
    return jnp.split(z, idx, axis=-1)

def masked_softmax(s, mask):
    s = jnp.where(mask, s.astype(F32), -jnp.inf)
    m = jnp.max(s, axis=-1, keepdims=True)
    m = jnp.where(jnp.isfinite(m), m, 0.0)
    e = jnp.exp(s - m)
    return e / jnp.maximum(jnp.sum(e, axis=-1, keepdims=True), 1e-30)

def alibi_slopes(n):
    return jnp.exp2(-8.0 * jnp.arange(1, n + 1, dtype=F32) / n)

def mem_attend(mq, mem_k, mem_v):
    B, T, _ = mq.shape
    qh = mq.reshape(B, T, MEM_HEADS, MEM_DH) * (MEM_DH ** -0.5)
    s = jnp.einsum('bthd,bmhd->bhtm', qh, mem_k)
    p = jax.nn.softmax(s.astype(F32), axis=-1).astype(mem_v.dtype)
    return jnp.einsum('bhtm,bmhd->bthd', p, mem_v).reshape(B, T, MEM_WIDTH)

def gla_chunked(q, k, v, log_a):
    B, T, H, DK = q.shape
    DV = v.shape[-1]
    C = GLA_CHUNK
    NC = T // C

    def chunks(a):
        return a.astype(F32).reshape(B, NC, C, H, a.shape[-1]).transpose(1, 0, 3, 2, 4)

    causal = jnp.tril(jnp.ones((C, C), dtype=bool))[:, :, None]

    def step(S, inp):
        qc, kc, vc, gc = inp
        b = jnp.cumsum(gc, axis=2)
        b_last = b[:, :, -1:, :]
        o_inter = jnp.einsum('bhtd,bhde->bhte', qc * jnp.exp(b), S)
        decay = jnp.exp(jnp.where(causal, b[:, :, :, None, :] - b[:, :, None, :, :], -jnp.inf))
        attn = jnp.einsum('bhtd,bhsd,bhtsd->bhts', qc, kc, decay)
        o = o_inter + jnp.einsum('bhts,bhse->bhte', attn, vc)
        S = jnp.exp(b_last[:, :, 0, :])[..., None] * S + jnp.einsum('bhsd,bhse->bhde', kc * jnp.exp(b_last - b), vc)
        return S, o

    S0 = jnp.zeros((B, H, DK, DV), F32)
    _, o = lax.scan(step, S0, (chunks(q), chunks(k), chunks(v), chunks(log_a)))
    return o.transpose(1, 0, 3, 2, 4).reshape(B, T, H, DV)

def gla_layer_mix(h, mem_k, mem_v, w_in, w_alpha, b_alpha, g_head, w_out):
    B, T, _ = h.shape
    q, k, v, r, alr, mq = split_cols(h @ w_in, [GLA_QK, GLA_QK, GLA_V, GLA_V, GLA_RANK, MEM_WIDTH])
    q = q.reshape(B, T, GLA_HEADS, GLA_DK) * (GLA_DK ** -0.5)
    k = k.reshape(B, T, GLA_HEADS, GLA_DK)
    v = v.reshape(B, T, GLA_HEADS, GLA_DV)
    log_a = jax.nn.log_sigmoid((alr @ w_alpha + b_alpha).astype(F32)) / GLA_TAU
    log_a = log_a.reshape(B, T, GLA_HEADS, GLA_DK)
    o = gla_chunked(q, k, v, log_a).astype(h.dtype)
    o = rmsnorm(o, g_head).reshape(B, T, GLA_V) * jax.nn.silu(r)
    m = mem_attend(mq, mem_k, mem_v)
    return jnp.concatenate([o, m], axis=-1) @ w_out

def compress_blocks(a, pe, w1, w2):
    B, T, G, DH = a.shape
    n_sub = CMP_BLOCK // CMP_STRIDE
    sub = a.reshape(B, T // CMP_STRIDE, CMP_STRIDE, G, DH)
    ncmp = T // CMP_STRIDE - n_sub + 1
    blocks = jnp.concatenate([sub[:, i:i + ncmp] for i in range(n_sub)], axis=2)
    blocks = blocks + pe[:, None, :]
    flat = blocks.transpose(0, 1, 3, 2, 4).reshape(B, ncmp, G, CMP_BLOCK * DH)
    return jax.nn.gelu(flat @ w1) @ w2

def nsa_shared_kv(x, g_kv, w_kv, pe_k, pe_v, w_ck1, w_ck2, w_cv1, w_cv2):
    B, T, _ = x.shape
    kv = (rmsnorm(x, g_kv) @ w_kv).reshape(B, T, 6, NSA_GROUPS, NSA_DH)
    k_c, v_c, k_s, v_s, k_w, v_w = [kv[:, :, i] for i in range(6)]
    return (compress_blocks(k_c, pe_k, w_ck1, w_ck2), compress_blocks(v_c, pe_v, w_cv1, w_cv2),
            k_s, v_s, k_w, v_w)

def selection_overlap(ncmp, ns):
    cs = jnp.arange(ncmp) * CMP_STRIDE
    ss = jnp.arange(ns) * SEL_BLOCK
    ov = jnp.minimum(cs[:, None] + CMP_BLOCK, ss[None, :] + SEL_BLOCK) - jnp.maximum(cs[:, None], ss[None, :])
    return jnp.clip(ov, 0, None).astype(F32) / CMP_BLOCK

def nsa_attend(q, gates, k_cmp, v_cmp, k_slc, v_slc, k_win, v_win):
    B, T, H, DH = q.shape
    G, HPG = NSA_GROUPS, NSA_HPG
    nqb = T // Q_BLOCK
    ncmp = k_cmp.shape[1]
    ns = T // SEL_BLOCK
    n_sel = min(SEL_TOPN, ns)
    slope = alibi_slopes(H).reshape(G, HPG)[None, None, :, :, None]
    cmp_end = jnp.arange(ncmp) * CMP_STRIDE + CMP_BLOCK - 1
    overlap = selection_overlap(ncmp, ns)

    def to_blocks(a):
        return a.reshape(B, ns, SEL_BLOCK, G, DH).transpose(0, 3, 1, 2, 4)

    ks_b, vs_b = to_blocks(k_slc), to_blocks(v_slc)
    pad = ((0, 0), (WINDOW, 0), (0, 0), (0, 0))
    kw_pad, vw_pad = jnp.pad(k_win, pad), jnp.pad(v_win, pad)
    gather = jax.vmap(jax.vmap(lambda blocks, ix: blocks[ix]))
    sel_off = jnp.arange(SEL_BLOCK)
    win_off = jnp.arange(Q_BLOCK + WINDOW)
    blk = jnp.arange(ns)

    def one_block(inp):
        qi, gi, bi = inp
        t = bi * Q_BLOCK + jnp.arange(Q_BLOCK)
        dist_c = (t[:, None] - cmp_end[None, :])
        s = jnp.einsum('bqghd,bngd->bqghn', qi, k_cmp).astype(F32) - slope * dist_c.astype(F32)[None, :, None, None, :]
        p_c = masked_softmax(s, (dist_c >= 0)[None, :, None, None, :])
        o_c = jnp.einsum('bqghn,bngd->bqghd', p_c.astype(v_cmp.dtype), v_cmp)
        cur = t // SEL_BLOCK
        imp = jnp.einsum('bqghn,nj->bqgj', p_c, overlap)
        valid = (blk[None, :] <= cur[:, None])[None, :, None, :]
        forced = ((blk[None, :] == 0) | (blk[None, :] == cur[:, None]) | (blk[None, :] == cur[:, None] - 1))[None, :, None, :]
        imp = jnp.where(forced, jnp.inf, jnp.where(valid, imp, -jnp.inf))
        _, idx = lax.top_k(imp, n_sel)
        idx = idx.transpose(0, 2, 1, 3)
        kg = gather(ks_b, idx).reshape(B, G, Q_BLOCK, n_sel * SEL_BLOCK, DH)
        vg = gather(vs_b, idx).reshape(B, G, Q_BLOCK, n_sel * SEL_BLOCK, DH)
        pos = (idx[..., None] * SEL_BLOCK + sel_off).reshape(B, G, Q_BLOCK, n_sel * SEL_BLOCK)
        dist_s = (t[None, None, :, None] - pos).transpose(0, 2, 1, 3)[:, :, :, None, :]
        s = jnp.einsum('bqghd,bgqsd->bqghs', qi, kg).astype(F32) - slope * dist_s.astype(F32)
        p_s = masked_softmax(s, dist_s >= 0)
        o_s = jnp.einsum('bqghs,bgqsd->bqghd', p_s.astype(vg.dtype), vg)
        start = bi * Q_BLOCK
        kw = lax.dynamic_slice_in_dim(kw_pad, start, Q_BLOCK + WINDOW, axis=1)
        vw = lax.dynamic_slice_in_dim(vw_pad, start, Q_BLOCK + WINDOW, axis=1)
        kpos = start - WINDOW + win_off
        dist_w = t[:, None] - kpos[None, :]
        mask_w = ((dist_w >= 0) & (dist_w < WINDOW) & (kpos >= 0)[None, :])[None, :, None, None, :]
        s = jnp.einsum('bqghd,bkgd->bqghk', qi, kw).astype(F32) - slope * dist_w.astype(F32)[None, :, None, None, :]
        p_w = masked_softmax(s, mask_w)
        o_w = jnp.einsum('bqghk,bkgd->bqghd', p_w.astype(vw.dtype), vw)
        return gi[..., 0:1] * o_c + gi[..., 1:2] * o_s + gi[..., 2:3] * o_w

    qb = q.reshape(B, nqb, Q_BLOCK, G, HPG, DH).transpose(1, 0, 2, 3, 4, 5)
    gb = gates.reshape(B, nqb, Q_BLOCK, G, HPG, 3).transpose(1, 0, 2, 3, 4, 5).astype(q.dtype)
    out = lax.map(one_block, (qb, gb, jnp.arange(nqb)))
    return out.transpose(1, 0, 2, 3, 4, 5).reshape(B, T, H * DH)

def nsa_layer_mix(h, shared, mem_k, mem_v, w_in, w_out):
    B, T, _ = h.shape
    q, gl, mq = split_cols(h @ w_in, [NSA_WIDTH, 3 * NSA_HEADS, MEM_WIDTH])
    q = q.reshape(B, T, NSA_HEADS, NSA_DH) * (NSA_DH ** -0.5)
    gates = jax.nn.sigmoid(gl.reshape(B, T, NSA_HEADS, 3))
    o = nsa_attend(q, gates, *shared)
    m = mem_attend(mq, mem_k, mem_v)
    return jnp.concatenate([o, m], axis=-1) @ w_out

def conv_ffn(h, w_up, conv_w, conv_b, w_down):
    T = h.shape[1]
    a, b = jnp.split(h @ w_up, 2, axis=-1)
    a_pad = jnp.pad(a, ((0, 0), (CONV_WIDTH - 1, 0), (0, 0)))
    a = sum(a_pad[:, j:j + T] * conv_w[j] for j in range(CONV_WIDTH)) + conv_b
    return (jax.nn.silu(a) * b) @ w_down

def first_inputs(seed: int = 0) -> dict:
    key = jax.random.key(seed)
    ks = jax.random.split(key, 26)

    def nrm(k, shape, scale):
        return jax.random.normal(k, shape, F32) * scale

    def gain(k, shape):
        return 1.0 + 0.02 * jax.random.normal(k, shape, F32)

    D = D_MODEL
    return {
        'x': nrm(ks[0], (BATCH, SEQ, D), 1.0),
        'mem': nrm(ks[1], (BATCH, MEM_LEN, D), 1.0),
        'g_mix': gain(ks[2], (DEPTH, D)),
        'g_ffn': gain(ks[3], (DEPTH, D)),
        'g_mem': gain(ks[4], (DEPTH, D)),
        'w_mem_kv': nrm(ks[5], (DEPTH, D, 2 * MEM_WIDTH), D ** -0.5),
        'w_up': nrm(ks[6], (DEPTH, D, 2 * FFN_DIM), D ** -0.5),
        'conv_w': nrm(ks[7], (DEPTH, CONV_WIDTH, FFN_DIM), CONV_WIDTH ** -0.5),
        'conv_b': nrm(ks[8], (DEPTH, FFN_DIM), 0.01),
        'w_down': nrm(ks[9], (DEPTH, FFN_DIM, D), FFN_DIM ** -0.5),
        'a_w_in': nrm(ks[10], (N_A, D, A_PROJ), D ** -0.5),
        'a_w_alpha': nrm(ks[11], (N_A, GLA_RANK, GLA_QK), GLA_RANK ** -0.5),
        'a_b_alpha': nrm(ks[12], (N_A, GLA_QK), 0.01),
        'a_g_head': gain(ks[13], (N_A, GLA_DV)),
        'a_w_out': nrm(ks[14], (N_A, GLA_V + MEM_WIDTH, D), (GLA_V + MEM_WIDTH) ** -0.5),
        'g_kv': gain(ks[15], (D,)),
        'w_kv': nrm(ks[16], (D, SHARED_KV_PROJ), D ** -0.5),
        'pe_k': nrm(ks[17], (CMP_BLOCK, NSA_DH), 0.1),
        'pe_v': nrm(ks[18], (CMP_BLOCK, NSA_DH), 0.1),
        'w_ck1': nrm(ks[19], (CMP_BLOCK * NSA_DH, CMP_HIDDEN), (CMP_BLOCK * NSA_DH) ** -0.5),
        'w_ck2': nrm(ks[20], (CMP_HIDDEN, NSA_DH), CMP_HIDDEN ** -0.5),
        'w_cv1': nrm(ks[21], (CMP_BLOCK * NSA_DH, CMP_HIDDEN), (CMP_BLOCK * NSA_DH) ** -0.5),
        'w_cv2': nrm(ks[22], (CMP_HIDDEN, NSA_DH), CMP_HIDDEN ** -0.5),
        'b_w_in': nrm(ks[23], (N_B, D, B_PROJ), D ** -0.5),
        'b_w_out': nrm(ks[24], (N_B, NSA_WIDTH + MEM_WIDTH, D), (NSA_WIDTH + MEM_WIDTH) ** -0.5),
        'g_final': gain(ks[25], (D,)),
    }

def first_block(x, mem, g_mix, g_ffn, g_mem, w_mem_kv, w_up, conv_w, conv_b, w_down,
              a_w_in, a_w_alpha, a_b_alpha, a_g_head, a_w_out,
              g_kv, w_kv, pe_k, pe_v, w_ck1, w_ck2, w_cv1, w_cv2,
              b_w_in, b_w_out, g_final):
    B, M, _ = mem.shape
    shared = None
    for l in range(DEPTH):
        if l == N_A:
            shared = nsa_shared_kv(x, g_kv, w_kv, pe_k, pe_v, w_ck1, w_ck2, w_cv1, w_cv2)
        mkv = (rmsnorm(mem, g_mem[l]) @ w_mem_kv[l]).reshape(B, M, 2, MEM_HEADS, MEM_DH)
        mem_k, mem_v = mkv[:, :, 0], mkv[:, :, 1]
        h = rmsnorm(x, g_mix[l])
        if l < N_A:
            x = x + gla_layer_mix(h, mem_k, mem_v, a_w_in[l], a_w_alpha[l], a_b_alpha[l], a_g_head[l], a_w_out[l])
        else:
            j = l - N_A
            x = x + nsa_layer_mix(h, shared, mem_k, mem_v, b_w_in[j], b_w_out[j])
        x = x + conv_ffn(rmsnorm(x, g_ffn[l]), w_up[l], conv_w[l], conv_b[l], w_down[l])
    return rmsnorm(x, g_final)


DEPTH_2 = 1

D_MIX = D_MODEL
SC_WIDTH = D_MIX // 4
SC_GROUPS = 4
SC_KERNEL = 3
GDN_WIDTH = D_MIX // 2
GDN_HEADS = 4
GDN_HEAD_DIM = GDN_WIDTH // GDN_HEADS
GDN_CONV = 4
GDN_CHUNK = 64
SB_WIDTH = D_MIX - SC_WIDTH - GDN_WIDTH
SB_HEADS = 4
SB_HEAD_DIM = SB_WIDTH // SB_HEADS
SB_BLOCK = 128
D_FF = 256 * ((8 * D_MODEL // 3 + 255) // 256)
FFN_CONV = 3
NORM_EPS = 1e-6
SPLIT_SIZES = (SC_WIDTH, SC_WIDTH, SC_WIDTH,
               GDN_WIDTH, GDN_WIDTH, GDN_WIDTH, GDN_WIDTH, GDN_HEADS, GDN_HEADS,
               SB_WIDTH, SB_WIDTH, SB_WIDTH)
D_IN_PROJ = 3 * SC_WIDTH + 4 * GDN_WIDTH + 2 * GDN_HEADS + 3 * SB_WIDTH


def rmsnorm_2(x, w):
    xf = x.astype(jnp.float32)
    y = xf * lax.rsqrt(jnp.mean(xf * xf, axis=-1, keepdims=True) + NORM_EPS) * w.astype(jnp.float32)
    return y.astype(x.dtype)

def l2norm(x):
    xf = x.astype(jnp.float32)
    return xf * lax.rsqrt(jnp.sum(xf * xf, axis=-1, keepdims=True) + NORM_EPS)

def causal_dwconv(x, w):
    K, C = w.shape
    return lax.conv_general_dilated(
        x, w[:, None, :].astype(x.dtype), window_strides=(1,), padding=[(K - 1, 0)],
        dimension_numbers=('NWC', 'WIO', 'NWC'), feature_group_count=C)

def split_columns(proj):
    points = [int(p) for p in np.cumsum(np.array(SPLIT_SIZES))[:-1]]
    return jnp.split(proj, points, axis=-1)

def gated_delta_rule_chunked(q, k, v, g, beta):
    f32 = jnp.float32
    Bsz, L, H, Dk = q.shape
    Dv = v.shape[-1]
    N = L // GDN_CHUNK

    def to_chunks(t):
        t = t.reshape((Bsz, N, GDN_CHUNK, H) + t.shape[3:])
        return jnp.moveaxis(t, 3, 1)

    q = to_chunks(q.astype(f32)) * (Dk ** -0.5)
    k = to_chunks(k.astype(f32))
    v = to_chunks(v.astype(f32))
    beta = to_chunks(beta.astype(f32))
    g = jnp.cumsum(to_chunks(g.astype(f32)), axis=-1)
    idx = jnp.arange(GDN_CHUNK)
    causal = idx[:, None] >= idx[None, :]
    strict = idx[:, None] > idx[None, :]
    decay = jnp.exp(jnp.where(causal, g[..., :, None] - g[..., None, :], -jnp.inf))
    k_beta = k * beta[..., None]
    lower = jnp.where(strict, jnp.einsum('bhncd,bhnsd->bhncs', k_beta, k) * decay, 0.0)
    lhs = lower + jnp.eye(GDN_CHUNK, dtype=f32)
    rhs = jnp.concatenate([v * beta[..., None], k_beta * jnp.exp(g)[..., None]], axis=-1)
    sol = lax.linalg.triangular_solve(lhs, rhs, left_side=True, lower=True, unit_diagonal=True)
    u, w = sol[..., :Dv], sol[..., Dv:]
    attn_intra = jnp.where(causal, jnp.einsum('bhncd,bhnsd->bhncs', q, k) * decay, 0.0)

    def step(S, inp):
        q_i, k_i, u_i, w_i, g_i, a_i = inp
        v_new = u_i - jnp.einsum('bhcd,bhde->bhce', w_i, S)
        o = jnp.einsum('bhcd,bhde->bhce', q_i * jnp.exp(g_i)[..., None], S) + \
            jnp.einsum('bhcs,bhse->bhce', a_i, v_new)
        g_last = g_i[..., -1]
        S = S * jnp.exp(g_last)[..., None, None] + \
            jnp.einsum('bhcd,bhce->bhde', k_i * jnp.exp(g_last[..., None] - g_i)[..., None], v_new)
        return S, o

    xs = tuple(jnp.moveaxis(t, 2, 0) for t in (q, k, u, w, g, attn_intra))
    S0 = jnp.zeros((Bsz, H, Dk, Dv), f32)
    _, outs = lax.scan(step, S0, xs)
    return outs.transpose(1, 0, 3, 2, 4).reshape(Bsz, L, H, Dv)

def stick_breaking_attention(q, k, v):
    L, D = q.shape[1], q.shape[-1]
    scale = D ** -0.5
    q_off = jnp.arange(SB_BLOCK)
    outs = []
    for blk in range(L // SB_BLOCK):
        start, end = blk * SB_BLOCK, (blk + 1) * SB_BLOCK
        z = jnp.einsum('bqhd,bkhd->bhqk', q[:, start:end], k[:, :end]).astype(jnp.float32) * scale
        strict = jnp.arange(end)[None, :] < (start + q_off)[:, None]
        log_beta = jax.nn.log_sigmoid(z)
        log_one_minus = jnp.where(strict, jax.nn.log_sigmoid(-z), 0.0)
        tail = lax.cumsum(log_one_minus, axis=3, reverse=True) - log_one_minus
        A = jnp.where(strict, jnp.exp(log_beta + tail), 0.0)
        outs.append(jnp.einsum('bhqk,bkhd->bqhd', A.astype(v.dtype), v[:, :end]))
    return jnp.concatenate(outs, axis=1)

def second_inputs(seed: int = 0) -> dict:
    key = jax.random.key(seed)
    ks = jax.random.split(key, 16)
    f32 = jnp.float32
    nrm = lambda k, shape: jax.random.normal(k, shape, f32)
    dt = jnp.exp(jax.random.uniform(ks[6], (DEPTH_2, GDN_HEADS), f32, np.log(1e-3), np.log(1e-1)))
    return {
        'x': nrm(ks[0], (BATCH, SEQ, D_MODEL)),
        'w_norm_mix': 1.0 + 0.02 * nrm(ks[1], (DEPTH_2, D_MODEL)),
        'w_mix_in': nrm(ks[2], (DEPTH_2, D_MODEL, D_IN_PROJ)) * D_MODEL ** -0.5,
        'w_sconv': nrm(ks[3], (DEPTH_2, SC_KERNEL, SC_WIDTH)) * SC_KERNEL ** -0.5,
        'w_gdn_conv': nrm(ks[4], (DEPTH_2, GDN_CONV, 3 * GDN_WIDTH)) * GDN_CONV ** -0.5,
        'gdn_a_log': jnp.log(jax.random.uniform(ks[5], (DEPTH_2, GDN_HEADS), f32, 1.0, 16.0)),
        'gdn_dt_bias': dt + jnp.log(-jnp.expm1(-dt)),
        'w_gdn_norm': 1.0 + 0.02 * nrm(ks[7], (DEPTH_2, GDN_HEAD_DIM)),
        'w_mix_out': nrm(ks[8], (DEPTH_2, D_MIX, D_MODEL)) * D_MIX ** -0.5,
        'w_norm_ffn': 1.0 + 0.02 * nrm(ks[9], (DEPTH_2, D_MODEL)),
        'w_ffn_up': nrm(ks[10], (DEPTH_2, D_MODEL, 2 * D_FF)) * D_MODEL ** -0.5,
        'w_ffn_conv': nrm(ks[11], (DEPTH_2, FFN_CONV, 2 * D_FF)) * FFN_CONV ** -0.5,
        'w_ffn_down': nrm(ks[12], (DEPTH_2, D_FF, D_MODEL)) * D_FF ** -0.5,
        'w_norm_final': 1.0 + 0.02 * nrm(ks[13], (D_MODEL,)),
    }

def second_block(x, w_norm_mix, w_mix_in, w_sconv, w_gdn_conv, gdn_a_log, gdn_dt_bias, w_gdn_norm,
              w_mix_out, w_norm_ffn, w_ffn_up, w_ffn_conv, w_ffn_down, w_norm_final):
    Bsz, L, _ = x.shape
    f32 = jnp.float32
    for l in range(DEPTH_2):
        h = rmsnorm_2(x, w_norm_mix[l])
        proj = h @ w_mix_in[l]
        (sc_b, sc_c, sc_h, gq, gk, gv, gz, ga, gb, sq, sk, sv) = split_columns(proj)

        y_sc = sc_b * causal_dwconv(sc_c * sc_h, w_sconv[l])

        qkv = jax.nn.silu(causal_dwconv(jnp.concatenate([gq, gk, gv], axis=-1), w_gdn_conv[l]))
        gq, gk, gv = jnp.split(qkv, 3, axis=-1)
        heads = lambda t: t.reshape(Bsz, L, GDN_HEADS, GDN_HEAD_DIM)
        beta = jax.nn.sigmoid(gb.astype(f32))
        g = -jnp.exp(gdn_a_log[l].astype(f32)) * jax.nn.softplus(ga.astype(f32) + gdn_dt_bias[l].astype(f32))
        o = gated_delta_rule_chunked(l2norm(heads(gq)), l2norm(heads(gk)), heads(gv), g, beta)
        o = rmsnorm_2(o, w_gdn_norm[l]) * jax.nn.silu(heads(gz).astype(f32))
        y_gdn = o.reshape(Bsz, L, GDN_WIDTH).astype(x.dtype)

        sb_heads = lambda t: t.reshape(Bsz, L, SB_HEADS, SB_HEAD_DIM)
        y_sb = stick_breaking_attention(sb_heads(sq), sb_heads(sk), sb_heads(sv)).reshape(Bsz, L, SB_WIDTH)

        x = x + jnp.concatenate([y_sc, y_gdn, y_sb], axis=-1) @ w_mix_out[l]

        h = rmsnorm_2(x, w_norm_ffn[l])
        u = causal_dwconv(h @ w_ffn_up[l], w_ffn_conv[l])
        gate, val = jnp.split(u, 2, axis=-1)
        x = x + (jax.nn.silu(gate) * val) @ w_ffn_down[l]
    return rmsnorm_2(x, w_norm_final)


def setup_inputs(seed=0):
    out = dict(first_inputs(seed))
    for name, value in second_inputs(seed + 1).items():
        if name != "x":
            out[name + "_2"] = value
    return out


def reference(
    x, mem, g_mix, g_ffn, g_mem, w_mem_kv, w_up, conv_w, conv_b, w_down, a_w_in, a_w_alpha,
    a_b_alpha, a_g_head, a_w_out, g_kv, w_kv, pe_k, pe_v, w_ck1, w_ck2, w_cv1, w_cv2, b_w_in,
    b_w_out, g_final, w_norm_mix_2, w_mix_in_2, w_sconv_2, w_gdn_conv_2, gdn_a_log_2,
    gdn_dt_bias_2, w_gdn_norm_2, w_mix_out_2, w_norm_ffn_2, w_ffn_up_2, w_ffn_conv_2,
    w_ffn_down_2, w_norm_final_2,
):
    x = first_block(
        x, mem, g_mix, g_ffn, g_mem, w_mem_kv, w_up, conv_w, conv_b, w_down, a_w_in, a_w_alpha,
        a_b_alpha, a_g_head, a_w_out, g_kv, w_kv, pe_k, pe_v, w_ck1, w_ck2, w_cv1, w_cv2,
        b_w_in, b_w_out, g_final,
    )
    return second_block(
        x, w_norm_mix_2, w_mix_in_2, w_sconv_2, w_gdn_conv_2, gdn_a_log_2, gdn_dt_bias_2,
        w_gdn_norm_2, w_mix_out_2, w_norm_ffn_2, w_ffn_up_2, w_ffn_conv_2, w_ffn_down_2,
        w_norm_final_2,
    )


_drawn_inputs = setup_inputs


def setup_inputs(seed=0):
    import zlib

    import numpy as np

    out = dict(_drawn_inputs(seed))
    spreads = {}
    factors = {'g_mem': 8.0,
     'conv_b': 6.011,
     'a_b_alpha': 8.0,
     'a_g_head': 4.194,
     'g_kv': 8.0,
     'pe_k': 8.0,
     'w_norm_mix_2': 2.681,
     'w_gdn_norm_2': 28.567,
     'w_norm_ffn_2': 12.223,
     'w_norm_final_2': 7.743,
     'g_ffn': 3.217,
     'pe_v': 8.0}
    for name, (base, spread) in spreads.items():
        noise = np.random.default_rng([zlib.crc32(name.encode()), seed]).standard_normal(out[name].shape)
        drawn = base * np.exp(spread * noise) if base else spread * noise
        out[name] = __import__('jax').numpy.asarray(drawn.astype(out[name].dtype))
    for name, factor in factors.items():
        out[name] = (out[name] * factor).astype(out[name].dtype)
    return out
```

```python
from contextlib import ExitStack

import concourse.bass as bass
from concourse import mybir

F32 = mybir.dt.float32
I32 = mybir.dt.int32
ALU = mybir.AluOpType
ACT = mybir.ActivationFunctionType
AX = mybir.AxisListType

P = 128
RING = 4
SLOT = 2048
BIG = 1e30
BATCH_LOADS = 2


class Signal:

    def __init__(self, sem):
        self.sem = sem
        self.base = 0

    def at(self, n):
        return self.base + n


class Chain:

    def __init__(self, sem):
        self.sem = sem
        self.n = 0
        self.reg = None
        self.per = 0

    def link(self, eng, ins):
        self.n += 1
        ins.then_inc(self.sem, 1)
        eng.wait_ge(self.sem, self.n if self.reg is None else self.n + self.reg * self.per)


class Ring:

    def __init__(self, landed, used, loads):
        self.landed = landed
        self.used = used
        self.loads = loads
        self.out = 0
        self.took = 0

    def full(self, n):
        return 16 * sum(self.loads[m] for m in range(n % RING, n + 1, RING))


class K:
    pass


def bank(k, i):
    return k.psum[i % 8]


def load_chunk(k, sp, n, pieces, reg=None):
    r = k.ring
    if reg is not None:
        sp.wait_ge(r.used, reg * RING + (n - RING + 1))
    elif n >= RING:
        sp.wait_ge(r.used, n - RING + 1)
    for dst, src in pieces:
        sp.dma_start(dst, src).then_inc(r.landed[n % RING], 16)


def slot(k, n, kt, cols):
    return k.slots[n % RING][:, 0:kt * cols].rearrange("p (k n) -> p k n", k=kt)


def chunks_of(k, w, cols, width=512, kt=4):
    rows = w.shape[0] // P
    wv = w.rearrange("(k p) n -> p k n", p=P)
    out = []
    for k0 in range(0, rows, kt):
        out.append(lambda n, k0=k0: [(slot(k, n, kt, width)[:, a:a + kt // 2, :],
                                      wv[:, k0 + a:k0 + a + kt // 2, cols:cols + width]) for a in (0, kt // 2)])
    return out


def take_chunk(k, pe):
    n = k.ring.took
    k.ring.took += 1
    pe.wait_ge(k.ring.landed[n % RING], k.ring.full(n))
    return n


def stream(k, sp, upto):
    end = min(upto + RING, len(k.plan))
    while k.ring.out < end:
        n = k.ring.out
        load_chunk(k, sp, n, k.plan[n](n))
        k.ring.out += 1


def pe_wait_bank(k, pe, t):
    if t >= 8:
        pe.wait_ge(k.tile_free.sem, k.tile_free.at(t - 7))


def pe_feature_tiles(k, pe, t, acts, n_cols, col0s, chunks):
    for c0 in col0s:
        pe_wait_bank(k, pe, t)
        for kk in range(8):
            w = slot(k, chunks[kk // 4], 4, 512)[:, kk % 4, c0:c0 + P]
            mm = pe.matmul(bank(k, t)[:, 0:n_cols], w, acts(kk), start=(kk == 0), stop=(kk == 7))
        mm.then_inc(k.tile_full.sem, 1)
        t += 1
    return t


def pe_token_tiles(k, pe, t, stat, tiles, rhs_of, width):
    for tt in range(tiles):
        pe_wait_bank(k, pe, t)
        for kk in range(8):
            mm = pe.matmul(bank(k, t)[:, 0:width], stat(kk, tt), rhs_of(kk), start=(kk == 0), stop=(kk == 7))
        mm.then_inc(k.tile_full.sem, 1)
        t += 1
    return t


def pe_used(k, pe, chunks):
    pe.drain().then_inc(k.ring.used, chunks)


def act_squares(k, act, src, n):
    for kk in range(8):
        act.activation(k.sq[:, kk, 0:n], src(kk), ACT.Square).then_inc(k.sq_ready.sem, 1)


def pe_norm_sums(k, pe, n, b=7):
    for kk in range(8):
        pe.wait_ge(k.sq_ready.sem, k.sq_ready.at(kk + 1))
        mm = pe.matmul(bank(k, b)[:, 0:n], k.ones[:, :], k.sq[:, kk, 0:n], start=(kk == 0), stop=(kk == 7))
    mm.then_inc(k.sums_full.sem, 1)


def act_rstd(k, act, n, b=7, dim=1024, out=None, eps=1e-6):
    act.wait_ge(k.sums_full.sem, k.sums_full.at(1))
    k.act_chain.link(act, act.activation(k.rstd[:, 0:n], bank(k, b)[:, 0:n], ACT.Ln, bias=k.eps[:, 0:1], scale=1.0 / dim))
    act.activation(k.rstd[:, 0:n], k.rstd[:, 0:n], ACT.Exp, scale=-0.5).then_inc(k.rstd_ready.sem, 1)


def dve_norm(k, dve, dst, src, gain, n):
    for kk in range(8):
        dve.scalar_tensor_tensor(dst(kk), src(kk), k.vec(gain + kk), k.rstd[:, 0:n], ALU.mult, ALU.mult)\
            .then_inc(k.h_ready.sem, 1)


VEC_ROWS = {}


def vector_tiles(a):
    rows = []

    def put(name, tile, at, src):
        rows.append((tile, at, src))
        VEC_ROWS[name] = tile * P + at
        return at + src.shape[0]

    r = lambda v: v.rearrange("(n p) -> n p", p=P)
    at = 0
    for l in range(2):
        at = put(f"g_mix{l}", 0, at, r(a["g_mix"][l]))
        at = put(f"g_ffn{l}", 0, at, r(a["g_ffn"][l]))
        at = put(f"g_mem{l}", 0, at, r(a["g_mem"][l]))
    for name in ("g_kv", "g_final"):
        at = put(name, 0, at, r(a[name]))
    at = put("w_norm_mix_2", 0, at, r(a["w_norm_mix_2"][0]))
    at = put("w_norm_ffn_2", 0, at, r(a["w_norm_ffn_2"][0]))
    at = put("w_norm_final_2", 0, at, r(a["w_norm_final_2"]))
    at = put("a_g_head", 0, at, r(a["a_g_head"][0]))
    at = put("w_gdn_norm_2", 0, at, r(a["w_gdn_norm_2"][0]))
    conv = a["conv_w"].rearrange("l j (n p) -> l (j n) p", p=P)
    at = put("conv_w0", 1, 0, conv[0])
    at = put("conv_b0", 1, at, r(a["conv_b"][0]))
    at = put("conv_b1", 1, at, r(a["conv_b"][1]))
    at = put("conv_w1", 2, 0, conv[1])
    at = put("w_sconv_2", 2, at, a["w_sconv_2"][0].rearrange("j (n p) -> (j n) p", p=P))
    at = put("w_gdn_conv_2", 2, at, a["w_gdn_conv_2"][0].rearrange("j (n p) -> (j n) p", p=P))
    fc = a["w_ffn_conv_2"][0].rearrange("j (n p) -> j n p", p=P)
    at = put("ffn_conv2_0", 3, 0, fc[0])
    at = put("ffn_conv2_1", 3, at, fc[1])
    at = put("ffn_conv2_2", 4, 0, fc[2])
    at = put("pe_k", 4, at, a["pe_k"].rearrange("(j q) d -> j (q d)", q=2))
    at = put("pe_v", 4, at, a["pe_v"].rearrange("(j q) d -> j (q d)", q=2))
    return rows


VEC_TILES = 5


def stage_setup(k, a):
    rows = vector_tiles(a)
    x_rows = k.carve(0, (4, 1024))
    mem_rows = k.carve(4096, (2, 1024))
    v_rows = k.carve(6144, (VEC_TILES, P))
    iota_f = k.carve(7168, (512,)).bitcast(I32)
    iota_c = k.carve(7680, (4 * 31,)).bitcast(I32)
    ip = k.carve(7808, (P,)).bitcast(I32)
    ic = k.carve(7936, (P,)).bitcast(I32)
    xo = k.carve(8064, (P,)).bitcast(I32)
    sh = k.carve(8192, (7 * P,)).bitcast(I32)
    x_in, mem_in, v_in = k.sem("x_in"), k.sem("mem_in"), k.sem("vectors_in")
    rows_clear, consts, iotas = k.sem("rows_clear"), k.sem("constants"), k.sem("iotas")
    turned, out = k.sem("turned"), k.sem("turned_out")
    jobs = [("x", tt, m) for m in range(8) for tt in range(4)] + [("mem", tt, m) for m in range(8) for tt in range(2)]

    with k.nc.Block() as block:
        @block.sync
        def _(sp):
            for tt in range(4):
                sp.dma_start(x_rows[:, tt, :], a["x"][0, tt * P:(tt + 1) * P, :]).then_inc(x_in, 16)
            for tt in range(2):
                sp.dma_start(mem_rows[:, tt, :], a["mem"][0, tt * P:(tt + 1) * P, :]).then_inc(mem_in, 16)
            stream(k, sp, 0)

        @block.scalar
        def _(act):
            act.wait_ge(rows_clear, 1)
            for tile, at, src in rows:
                act.dma_start(v_rows[at:at + src.shape[0], tile, :], src).then_inc(v_in, 16)

        @block.gpsimd
        def _(pool):
            k.pool_chain.link(pool, pool.memset(k.ones[:, :], 1.0))
            k.pool_chain.link(pool, pool.affine_select(k.triu[:, :], k.ones[:, :], [[1, P]], ALU.is_ge, 0.0,
                                                       base=0, channel_multiplier=-1))
            k.pool_chain.link(pool, pool.affine_select(k.ident[:, :], k.triu[:, :], [[1, P]], ALU.is_equal, 0.0,
                                                       base=0, channel_multiplier=-1))
            pool.affine_select(k.triu_strict[:, :], k.triu[:, :], [[1, P]], ALU.not_equal, 0.0,
                               base=0, channel_multiplier=-1).then_inc(consts, 1)
            k.pool_chain.link(pool, pool.affine_select(k.tril[:, :], k.ones[:, :], [[-1, P]], ALU.is_ge, 0.0,
                                                       base=0, channel_multiplier=1))
            pool.iota(iota_f, [[-1, 512]], base=384, channel_multiplier=1).then_inc(iotas, 1)
            pool.iota(iota_c, [[P, 4], [-16, 31]], base=-31, channel_multiplier=1).then_inc(iotas, 1)
            pool.iota(ip, [[0, P]], base=0, channel_multiplier=1).then_inc(iotas, 1)
            pool.iota(ic, [[1, P]], base=0, channel_multiplier=0).then_inc(iotas, 1)

        @block.vector
        def _(dve):
            L = lambda ins: k.dve_chain.link(dve, ins)
            dve.memset(v_rows[:, :, :], 0.0).then_inc(rows_clear, 1)
            L(dve.memset(k.eps[:, :], 1e-6))
            dve.wait_ge(iotas, 4)
            dve.wait_ge(consts, 1)
            L(dve.tensor_copy(k.dist[:, :], iota_f))
            L(dve.tensor_copy(k.dist_cmp[:, :], iota_c))
            L(dve.tensor_scalar(k.valid[:, :], k.dist_cmp[:, 0:1], 0.0, None, ALU.is_ge))
            L(dve.tensor_tensor(xo, ip, ic, ALU.bitwise_xor))
            for lg in range(7):
                piece = sh[:, lg * P:(lg + 1) * P]
                L(dve.tensor_scalar(piece, xo, lg, None, ALU.logical_shift_right))
                L(dve.scalar_tensor_tensor(k.level[:, lg, :], piece, 1.0, k.triu[:, :], ALU.is_equal, ALU.mult))
            for n, (what, tt, m) in enumerate(jobs):
                dve.wait_ge(turned, n + 1)
                dst = k.xT[:, m, tt * P:(tt + 1) * P] if what == "x" else k.memT[:, m, tt * P:(tt + 1) * P]
                dve.tensor_copy(dst, bank(k, n)[:, 0:P]).then_inc(out, 1)
            for t in range(VEC_TILES):
                dve.wait_ge(turned, len(jobs) + t + 1)
                dve.tensor_copy(k.vecs[:, t * P:(t + 1) * P], bank(k, len(jobs) + t)[:, 0:P]).then_inc(out, 1)

        @block.tensor
        def _(pe):
            pe.wait_ge(consts, 1)
            pe.wait_ge(x_in, 64)
            for n, (what, tt, m) in enumerate(jobs):
                if n == 32:
                    pe.wait_ge(mem_in, 32)
                if n >= 8:
                    pe.wait_ge(out, n - 7)
                src = (x_rows if what == "x" else mem_rows)[:, tt, m * P:(m + 1) * P]
                pe.transpose(bank(k, n)[:, 0:P], src, k.ident[:, :]).then_inc(turned, 1)
            pe.wait_ge(v_in, 16 * len(rows))
            for t in range(VEC_TILES):
                n = len(jobs) + t
                pe.wait_ge(out, n - 7)
                pe.transpose(bank(k, n)[:, 0:P], v_rows[:, t, :], k.ident[:, :]).then_inc(turned, 1)

    masked = k.sem("masked")
    with k.nc.Block() as block:
        @block.gpsimd
        def _(pool):
            pool.affine_select(k.dist[:, :], k.dist[:, :], [[-1, 512]], ALU.is_ge, BIG, base=384,
                               channel_multiplier=1).then_inc(masked, 1)
            pool.affine_select(k.dist_cmp[:, :], k.dist_cmp[:, :], [[P, 4], [-16, 31]], ALU.is_ge, BIG, base=-31,
                               channel_multiplier=1).then_inc(masked, 1)
            pool.wait_ge(masked, 2)


def stage_memory(k, a):
    M = 256
    chunks = 8
    first = k.ring.took
    mn = k.carve(4096, (8, M))
    with k.nc.Block() as block:
        @block.sync
        def _(sp):
            stream(k, sp, first + chunks)

        @block.scalar
        def _(act):
            act_squares(k, act, lambda kk: k.memT[:, kk, :], M)
            act_rstd(k, act, M)
            for t in range(12):
                l, m = divmod(t, 6)
                act.wait_ge(k.tile_full.sem, k.tile_full.at(t + 1))
                dst = k.mkT[:, l, m, :] if m < 4 else k.mv[:, l, m - 4, :]
                act.copy(dst, bank(k, t)[:, 0:M if m < 4 else 512]).then_inc(k.tile_free.sem, 1)

        @block.vector
        def _(dve):
            dve.wait_ge(k.rstd_ready.sem, k.rstd_ready.at(1))
            for l in range(2):
                if l == 1:
                    dve.wait_ge(k.tile_full.sem, k.tile_full.at(6))
                dve_norm(k, dve, lambda kk: mn[:, kk, :], lambda kk: k.memT[:, kk, :], VEC_ROWS[f"g_mem{l}"], M)

        @block.tensor
        def _(pe):
            pe_norm_sums(k, pe, M)
            t = 0
            for l in range(2):
                pe.wait_ge(k.h_ready.sem, k.h_ready.at(8 * (l + 1)))
                cs = [take_chunk(k, pe), take_chunk(k, pe)]
                t = pe_feature_tiles(k, pe, t, lambda kk: mn[:, kk, :], M, [m * P for m in range(4)], cs)
                pe_used(k, pe, 2)
                cs = [take_chunk(k, pe), take_chunk(k, pe)]
                t = pe_token_tiles(k, pe, t, lambda kk, tt: mn[:, kk, tt * P:(tt + 1) * P], 2,
                                   lambda kk: slot(k, cs[kk // 4], 4, 512)[:, kk % 4, :], 512)
                pe_used(k, pe, 2)
    k.advance(sq_ready=8, sums_full=1, rstd_ready=1, h_ready=16, tile_full=12, tile_free=12)


def stage_gla_in(k, a):
    k.qT, k.kT = k.carve(0, (2, 512)), k.carve(1024, (2, 512))
    k.v = k.carve(2048, (4, 512))
    k.rT = k.carve(4096, (4, 512))
    k.mqT = k.carve(6144, (4, 512))
    k.alrT = k.carve(8192, (512,))
    w_alr = k.carve(8704, (8, 16))
    alr_in, ones_row = k.sem("alr_in"), k.sem("ones_row")
    first = k.ring.took
    with k.nc.Block() as block:
        @block.sync
        def _(sp):
            sp.dma_start(w_alr[:, :, :], a["a_w_in"][0].rearrange("(k p) n -> p k n", p=P)[:, :, 1536:1552]).then_inc(alr_in, 16)
            stream(k, sp, first + 8)

        @block.gpsimd
        def _(pool):
            pool.memset(k.alrT[0:32, :], 1.0).then_inc(ones_row, 1)

        @block.scalar
        def _(act):
            act_squares(k, act, lambda kk: k.xT[:, kk, :], 512)
            act_rstd(k, act, 512)

            def tile(t):
                act.wait_ge(k.tile_full.sem, k.tile_full.at(t + 1))
                return bank(k, t)[:, :]

            for t in range(17):
                src = tile(t)
                if t < 2:
                    ins = act.mul(k.qT[:, t, :], src, 64 ** -0.5)
                elif t < 4:
                    ins = act.copy(k.kT[:, t - 2, :], src)
                elif t < 8:
                    ins = act.copy(k.v[:, t - 4, :], src)
                elif t < 12:
                    ins = act.activation(k.rT[:, t - 8, :], src, ACT.Silu)
                elif t < 16:
                    ins = act.mul(k.mqT[:, t - 12, :], src, -(128 ** -0.5))
                else:
                    act.wait_ge(ones_row, 1)
                    ins = act.copy(k.alrT[0:16, :], src[0:16, :])
                ins.then_inc(k.tile_free.sem, 1)

        @block.vector
        def _(dve):
            dve.wait_ge(k.rstd_ready.sem, k.rstd_ready.at(1))
            dve_norm(k, dve, lambda kk: k.hT[:, kk, :], lambda kk: k.xT[:, kk, :], VEC_ROWS["g_mix0"], 512)

        @block.tensor
        def _(pe):
            pe_norm_sums(k, pe, 512)
            pe.wait_ge(k.h_ready.sem, k.h_ready.at(8))
            t = 0
            for group in range(4):
                cs = [take_chunk(k, pe), take_chunk(k, pe)]
                if group == 1:
                    t = pe_token_tiles(k, pe, t, lambda kk, tt: k.hT[:, kk, tt * P:(tt + 1) * P], 4,
                                       lambda kk: slot(k, cs[kk // 4], 4, 512)[:, kk % 4, :], 512)
                else:
                    t = pe_feature_tiles(k, pe, t, lambda kk: k.hT[:, kk, :], 512, [m * P for m in range(4)], cs)
                pe_used(k, pe, 2)
            pe.wait_ge(alr_in, 16)
            pe_wait_bank(k, pe, t)
            for kk in range(8):
                mm = pe.matmul(bank(k, t)[0:16, :], w_alr[:, kk, :], k.hT[:, kk, :], start=(kk == 0), stop=(kk == 7))
            mm.then_inc(k.tile_full.sem, 1)
    k.advance(sq_ready=8, sums_full=1, rstd_ready=1, h_ready=8, tile_full=17, tile_free=17)


def stage_mem_attention(k, layer, out_of):
    prob = [k.carve(k.ma + i * 1024, (4, 256)) for i in range(2)]
    probT = [k.carve(k.ma + 2048 + i * 1024, (2, 512)) for i in range(2)]
    low, tot, inv = (k.carve(k.ma + 4096 + i * 16, (4, 4)) for i in range(3))
    z_full, low_ready, e_ready, p_ready, t_full, t_out, o_full, o_out = k.ma_sig
    with k.nc.Block() as block:
        @block.tensor
        def _(pe):
            def scores(h):
                if h >= 1:
                    pe.wait_ge(e_ready.sem, e_ready.at(4 * h))
                for tt in range(4):
                    mm = pe.matmul(bank(k, tt // 2)[:, (tt % 2) * 256:(tt % 2) * 256 + 256],
                                   k.mqT[:, h, tt * P:(tt + 1) * P], k.mkT[:, layer, h, :], start=True, stop=True)
                mm.then_inc(z_full.sem, 1)

            scores(0)
            for h in range(4):
                if h < 3:
                    scores(h + 1)
                pe.wait_ge(p_ready.sem, p_ready.at(h + 1))
                if h >= 1:
                    pe.wait_ge(t_out.sem, t_out.at(2 * h))
                for mt in range(2):
                    for tt in range(4):
                        mm = pe.transpose(bank(k, 2 + mt)[:, tt * P:(tt + 1) * P],
                                          prob[h % 2][:, tt, mt * P:(mt + 1) * P], k.ident[:, :])
                    mm.then_inc(t_full.sem, 1)
                if h >= 2:
                    pe.wait_ge(o_out.sem, o_out.at(h - 1))
                for mt in range(2):
                    pe.wait_ge(t_out.sem, t_out.at(2 * h + mt + 1))
                    mm = pe.matmul(bank(k, 4 + h % 2)[:, :], k.mv[:, layer, mt, h * P:(h + 1) * P],
                                   probT[h % 2][:, mt, :], start=(mt == 0), stop=(mt == 1))
                mm.then_inc(o_full.sem, 1)

        @block.vector
        def _(dve):
            def lows(h):
                dve.wait_ge(z_full.sem, z_full.at(h + 1))
                for b in range(2):
                    dve.tensor_reduce(low[:, h, 2 * b:2 * b + 2],
                                      bank(k, b)[:, :].rearrange("p (a n) -> p a n", a=2), AX.X, ALU.min)\
                        .then_inc(low_ready.sem, 1)

            lows(0)
            for h in range(4):
                dve.wait_ge(e_ready.sem, e_ready.at(4 * (h + 1)))
                k.dve_chain.link(dve, dve.reciprocal(inv[:, h, :], tot[:, h, :]))
                dve.tensor_tensor(prob[h % 2][:, :, :], prob[h % 2][:, :, :],
                                  inv[:, h, :].unsqueeze(2).broadcast_to([P, 4, 256]), ALU.mult)\
                    .then_inc(p_ready.sem, 1)
                if h < 3:
                    lows(h + 1)

        @block.scalar
        def _(act):
            for h in range(4):
                act.wait_ge(low_ready.sem, low_ready.at(2 * (h + 1)))
                if h >= 2:
                    act.wait_ge(t_full.sem, t_full.at(2 * (h - 1)))
                for tt in range(4):
                    act.activation(prob[h % 2][:, tt, :], bank(k, tt // 2)[:, (tt % 2) * 256:(tt % 2) * 256 + 256],
                                   ACT.Exp, bias=low[:, h, tt:tt + 1], scale=-1.0,
                                   accum_out=tot[:, h, tt:tt + 1]).then_inc(e_ready.sem, 1)
                for mt in range(2):
                    act.wait_ge(t_full.sem, t_full.at(2 * h + mt + 1))
                    if h >= 2:
                        act.wait_ge(o_full.sem, o_full.at(h - 1))
                    act.copy(probT[h % 2][:, mt, :], bank(k, 2 + mt)[:, :]).then_inc(t_out.sem, 1)
                act.wait_ge(o_full.sem, o_full.at(h + 1))
                act.copy(out_of(h), bank(k, 4 + h % 2)[:, :]).then_inc(o_out.sem, 1)
    for s, n in zip(k.ma_sig, (4, 8, 16, 4, 8, 8, 4, 4)):
        s.base += n


def stage_out_projection(k):
    first = k.ring.took
    with k.nc.Block() as block:
        @block.sync
        def _(sp):
            stream(k, sp, first + 4)

        @block.tensor
        def _(pe):
            t = 0
            for group in range(2):
                cs = [take_chunk(k, pe), take_chunk(k, pe)]
                t = pe_feature_tiles(k, pe, t, lambda kk: k.catT[:, kk, :], 512, [m * P for m in range(4)], cs)
                pe_used(k, pe, 2)

        @block.vector
        def _(dve):
            for t in range(8):
                dve.wait_ge(k.tile_full.sem, k.tile_full.at(t + 1))
                dve.tensor_tensor(k.xT[:, t, :], k.xT[:, t, :], bank(k, t)[:, :], ALU.add).then_inc(k.tile_free.sem, 1)
    k.advance(tile_full=8, tile_free=8)


def stage_gla(k, a):
    C = 4
    base = k.ma
    w_alpha = k.carve(base, (256,))
    g = k.carve(base + 256, (C, 256))
    tmp = k.carve(base + 1280, (C, 256))
    b = k.carve(base + 2304, (2, 512))
    eb = k.carve(base + 3328, (2, 512))
    qe = k.carve(base + 4352, (2, 512))
    kbar = k.carve(base + 5376, (2, 512))
    kbar_tok = k.carve(base + 6400, (C, 2, P))
    diff = [k.carve(base + 7424 + i * 1024, (1024,)) for i in range(2)]
    ql = [k.carve(base + 9472 + i * 1024, (2, 512)) for i in range(2)]
    kl = [k.carve(base + 11520 + i * 1024, (2, 512)) for i in range(2)]
    A = k.carve(base + 13568, (4, 512))
    Ss = [k.carve(base + 15616 + i * 512, (2, 256)) for i in range(2)]
    last = lambda t: t[:, :, :].rearrange("p i (c n) -> p (i c) n", c=C)
    w_in, y_full, ls_ready, b_full, b_ready = (k.sem(n) for n in ("w_alpha_in", "alpha_full", "decay_ready", "cum_full", "cum_ready"))
    logs = k.sem("alpha_logs")
    kb_ready, kb_turned, kb_out = k.sem("kbar_ready"), k.sem("kbar_turned"), k.sem("kbar_out")
    with k.nc.Block() as block:
        @block.sync
        def _(sp):
            sp.dma_start(w_alpha[0:16, :], a["a_w_alpha"][0]).then_inc(w_in, 16)
            sp.dma_start(w_alpha[16:17, :], a["a_b_alpha"]).then_inc(w_in, 16)

        @block.tensor
        def _(pe):
            pe.wait_ge(w_in, 32)
            for c in range(C):
                mm = pe.matmul(bank(k, c // 2)[:, (c % 2) * 256:(c % 2) * 256 + 256], k.alrT[0:17, c * P:(c + 1) * P],
                               w_alpha[0:17, :], start=True, stop=True)
            mm.then_inc(y_full, 1)
            pe.wait_ge(ls_ready, 1)
            for i in range(2):
                for c in range(C):
                    mm = pe.matmul(bank(k, 2 + i)[:, c * P:(c + 1) * P], g[:, c, i * P:(i + 1) * P], k.triu[:, :],
                                   start=True, stop=True)
            mm.then_inc(b_full, 1)
            pe.wait_ge(kb_ready, 1)
            for c in range(C):
                for i in range(2):
                    mm = pe.transpose(bank(k, 4 + c // 2)[:, ((c % 2) * 2 + i) * P:((c % 2) * 2 + i + 1) * P],
                                      kbar[:, i, c * P:(c + 1) * P], k.ident[:, :])
            mm.then_inc(kb_turned, 1)

        @block.scalar
        def _(act):
            L = lambda ins: k.act_chain.link(act, ins)
            act.wait_ge(y_full, 1)
            for h in range(2):
                src = bank(k, h)[:, :].rearrange("p (c n) -> p c n", c=2)
                L(act.activation(tmp[:, 2 * h:2 * h + 2, :], src, ACT.Abs))
                L(act.activation(tmp[:, 2 * h:2 * h + 2, :], tmp[:, 2 * h:2 * h + 2, :], ACT.Exp, scale=-1.0))
                act.activation(tmp[:, 2 * h:2 * h + 2, :], tmp[:, 2 * h:2 * h + 2, :], ACT.Ln, bias=1.0)\
                    .then_inc(logs, 1)
            act.wait_ge(b_full, 1)
            for i in range(2):
                act.mul(b[:, i, :], bank(k, 2 + i)[:, :], 1.0 / 16).then_inc(b_ready, 1)
            act.wait_ge(b_ready, 2)
            L(act.activation(eb[:, :, :], b[:, :, :], ACT.Exp))
            act.wait_ge(b_ready, 3)
            L(act.activation(kbar[:, :, :], kbar[:, :, :], ACT.Exp))
            act.sem_inc(b_ready, 1)
            act.wait_ge(kb_turned, 1)
            for h in range(2):
                act.copy(kbar_tok[:, 2 * h:2 * h + 2, :, :].rearrange("p c i n -> p (c i n)"),
                         bank(k, 4 + h)[:, :]).then_inc(kb_out, 1)

        @block.vector
        def _(dve):
            L = lambda ins: k.dve_chain.link(dve, ins)
            dve.wait_ge(logs, 2)
            for h in range(2):
                ins = dve.scalar_tensor_tensor(g[:, 2 * h:2 * h + 2, :], bank(k, h)[:, :].rearrange("p (c n) -> p c n", c=2),
                                               0.0, tmp[:, 2 * h:2 * h + 2, :], ALU.min, ALU.subtract)
                if h == 0:
                    L(ins)
            ins.then_inc(ls_ready, 1)
            dve.wait_ge(b_ready, 2)
            dve.tensor_tensor(last(kbar), last(b)[:, :, P - 1:P].broadcast_to([P, 8, P]), last(b), ALU.subtract)\
                .then_inc(b_ready, 1)
            dve.wait_ge(b_ready, 4)
            L(dve.tensor_tensor(qe[:, :, :], k.qT[:, :, :], eb[:, :, :], ALU.mult))
            dve.tensor_tensor(kbar[:, :, :], k.kT[:, :, :], kbar[:, :, :], ALU.mult).then_inc(kb_ready, 1)

    d_ready, dl_ready, e_done, qk_ready = (k.sem(n) for n in ("diff_ready", "diff_left", "level_exp", "level_qk"))
    s_full, s_done = k.sem("level_full"), k.sem("level_done")
    halves = lambda t, n: t.rearrange("p (m two n) -> p m two n", two=2, n=n)
    with k.nc.Block() as block:
        @block.vector
        def _(dve):
            L = lambda ins: k.dve_chain.link(dve, ins)
            L(dve.memset(A[:, :, :], 0.0))

            def differences(lv):
                n = 1 << lv
                m = 1024 // (2 * n)
                bv = halves(b[:, :, :].rearrange("p i n -> p (i n)"), n)
                dv = halves(diff[lv % 2], n)
                ref = bv[:, :, 0, n - 1:n].broadcast_to([P, m, n])
                if lv >= 2:
                    dve.wait_ge(qk_ready, lv - 1)
                dve.tensor_tensor(dv[:, :, 0, :], ref, bv[:, :, 0, :], ALU.subtract).then_inc(dl_ready, 1)
                dve.tensor_tensor(dv[:, :, 1, :], bv[:, :, 1, :], ref, ALU.subtract).then_inc(d_ready, 1)

            def products(lv):
                if lv == 7:
                    return
                dve.wait_ge(e_done, lv + 1)
                if lv >= 2:
                    dve.wait_ge(s_full, 4 * (lv - 1))
                e = diff[lv % 2].rearrange("p (i n) -> p i n", i=2)
                L(dve.tensor_tensor(ql[lv % 2][:, :, :], k.qT[:, :, :], e, ALU.mult))
                dve.tensor_tensor(kl[lv % 2][:, :, :], k.kT[:, :, :], e, ALU.mult).then_inc(qk_ready, 1)

            def place(lv):
                mask = (k.level[:, lv, :] if lv < 7 else k.ident[:, :]).bitcast(I32)
                for h in range(4):
                    dve.wait_ge(s_full, 4 * lv + h + 1)
                    if lv >= 1:
                        dve.wait_ge(s_done, 4 * (lv - 1) + h + 1)
                    dve.copy_predicated(A[:, h, :].rearrange("p (c n) -> p c n", c=C),
                                        mask.unsqueeze(1).broadcast_to([P, C, P]),
                                        bank(k, 4 * (lv % 2) + h)[:, :].rearrange("p (c n) -> p c n", c=C))\
                        .then_inc(s_done, 1)

            differences(0)
            for lv in range(8):
                if lv < 6:
                    differences(lv + 1)
                products(lv)
                if lv >= 1:
                    place(lv - 1)
            place(7)

        @block.scalar
        def _(act):
            for lv in range(7):
                act.wait_ge(d_ready, lv + 1)
                act.wait_ge(dl_ready, lv + 1)
                act.activation(diff[lv % 2], diff[lv % 2], ACT.Exp).then_inc(e_done, 1)

        @block.tensor
        def _(pe):
            for lv in range(8):
                q, kk = (ql[lv % 2], kl[lv % 2]) if lv < 7 else (k.qT, k.kT)
                if lv < 7:
                    pe.wait_ge(qk_ready, lv + 1)
                for h in range(4):
                    if lv >= 2:
                        pe.wait_ge(s_done, 4 * (lv - 2) + h + 1)
                    r0 = (h % 2) * 64
                    for c in range(C):
                        cs = slice(c * P, (c + 1) * P)
                        mm = pe.matmul(bank(k, 4 * (lv % 2) + h)[:, cs], kk[r0:r0 + 64, h // 2, cs], q[r0:r0 + 64, h // 2, cs],
                                       start=True, stop=True)
                    mm.then_inc(s_full, 1)

    u_full, S_ready, o_full = k.sem("gla_update_full"), k.sem("gla_state_ready"), k.sem("gla_out_full")
    o_out, sq, nf, rs = k.sem("gla_out"), k.sem("gla_squares"), k.sem("gla_sums"), k.sem("gla_rstd")
    o = A
    o_sb, osq, rstd = k.carve(base + 7424, (4, 512)), k.carve(base + 9472, (4, 512)), k.carve(base + 11520, (4, 512))
    with k.nc.Block() as block:
        @block.tensor
        def _(pe):
            for c in range(C):
                cs = slice(c * P, (c + 1) * P)
                if c < C - 1:
                    for i in range(2):
                        if c >= 1:
                            pe.wait_ge(S_ready, 2 * (c - 1) + i + 1)
                        pe.matmul(bank(k, 4 + i)[:, 0:256], kbar_tok[:, c, i, :], k.v[:, c, i * 256:(i + 1) * 256],
                                  start=True, stop=True).then_inc(u_full, 1)
                for h in range(4):
                    r0 = (h % 2) * 64
                    if c >= 1:
                        pe.wait_ge(S_ready, 2 * c)
                        pe.matmul(bank(k, h)[:, cs], Ss[(c - 1) % 2][r0:r0 + 64, h // 2, (h % 2) * P:(h % 2 + 1) * P],
                                  qe[r0:r0 + 64, h // 2, cs], start=True, stop=False)
                    mm = pe.matmul(bank(k, h)[:, cs], k.v[:, c, h * P:(h + 1) * P], A[:, h, cs], start=(c == 0), stop=True)
            mm.then_inc(o_full, 1)
            for h in range(4):
                pe.wait_ge(sq, h + 1)
                pe.matmul(bank(k, 4 + h)[:, :], k.ones[:, :], osq[:, h, :], start=True, stop=True).then_inc(nf, 1)

        @block.vector
        def _(dve):
            L = lambda ins: k.dve_chain.link(dve, ins)
            for c in range(C - 1):
                for i in range(2):
                    dve.wait_ge(u_full, 2 * c + i + 1)
                    col = eb[:, i, c * P + P - 1:c * P + P]
                    if c == 0:
                        ins = dve.tensor_copy(Ss[0][:, i, :], bank(k, 4 + i)[:, 0:256])
                    else:
                        dve.wait_ge(S_ready, 2 * c)
                        if c >= 2:
                            dve.wait_ge(u_full, 2 * c + 2)
                        ins = dve.scalar_tensor_tensor(Ss[c % 2][:, i, :], Ss[(c - 1) % 2][:, i, :], col,
                                                       bank(k, 4 + i)[:, 0:256], ALU.mult, ALU.add)
                    ins.then_inc(S_ready, 1)
            for h in range(4):
                dve.wait_ge(rs, h + 1)
                L(dve.scalar_tensor_tensor(o_sb[:, h, :], o_sb[:, h, :], k.vec(VEC_ROWS["a_g_head"]), rstd[:, h, :],
                                           ALU.mult, ALU.mult))
                L(dve.tensor_tensor(k.catT[:, h, :], o_sb[:, h, :], k.rT[:, h, :], ALU.mult))

        @block.scalar
        def _(act):
            L = lambda ins: k.act_chain.link(act, ins)
            act.wait_ge(o_full, 1)
            for h in range(4):
                act.copy(o_sb[:, h, :], bank(k, h)[:, :]).then_inc(o_out, 1)
                act.activation(osq[:, h, :], bank(k, h)[:, :], ACT.Square).then_inc(sq, 1)
            act.wait_ge(o_out, 4)
            for h in range(4):
                act.wait_ge(nf, h + 1)
                L(act.activation(rstd[:, h, :], bank(k, 4 + h)[:, :], ACT.Ln, bias=k.eps[:, 0:1], scale=1.0 / P))
            for h in range(4):
                act.activation(rstd[:, h, :], rstd[:, h, :], ACT.Exp, scale=-0.5).then_inc(rs, 1)


FF = 2816
FT = FF // P


def ffn_chunks(k, w_up, w_down):
    up = w_up.rearrange("(k p) n -> p k n", p=P)
    down = w_down.rearrange("(k p) n -> p k n", p=P)
    out = []
    for grp in range(FT // 2):
        for half in range(2):
            out.append(lambda n, grp=grp, half=half: [
                (slot(k, n, 4, 512)[:, :, s * 256:(s + 1) * 256],
                 up[:, 4 * half:4 * half + 4, s * FF + grp * 256:s * FF + (grp + 1) * 256]) for s in range(2)])
    for kk in range(0, FT, 2):
        out.append(lambda n, kk=kk: [(slot(k, n, 2, 1024)[:, s, :], down[:, kk + s, :]) for s in range(2)])
    return out


def stage_ffn(k, w_up, w_down, gain, taps, bias, both):
    LOOPS = FT // 4
    act_t = k.carve(0, (FT * 512,))
    pad = [[k.carve(FT * 512 + (2 * s + i) * 516, (516,)) for i in range(2)] for s in range(2)]
    acc = [[k.carve(FT * 512 + 2064 + (2 * s + i) * 512, (512,)) for i in range(2)] for s in range(2)]
    first = k.ring.took
    up_all, total = FT, FT + FT // 2
    up = w_up.rearrange("(k p) n -> p k n", p=P)
    down = w_down.rearrange("(k p) n -> p k n", p=P)
    PAIR = 3 if both else 1
    padded, conv_a, conv_b, silu, done, cleared = k.ffn_sig
    f_tiles = FT
    bank_of = lambda f, s: bank(k, 2 * (f % 4) + s)

    with k.nc.Block() as block:
        @block.sync
        def _(sp):
            with sp.Fori(0, (up_all - RING) // RING) as i:
                for j in range(RING):
                    n = first + RING + j
                    grp2, half = j // 2, j % 2
                    src = up[:, 4 * half:4 * half + 4, :]
                    pieces = [(slot(k, n, 4, 512)[:, :, s * 256:(s + 1) * 256],
                               src[:, :, bass.ds(i * 512 + (s * FF + (2 + grp2) * 256), 256)]) for s in range(2)]
                    load_chunk(k, sp, n, pieces, i)
            k.ring.out = first + RING + (up_all - RING) // RING * RING
            stream(k, sp, first + total)

        @block.tensor
        def _(pe):
            pe_norm_sums(k, pe, 512)

            def group(n0, f0, reg, wait_bank):
                for f in range(2):
                    for s in range(2):
                        for kk in range(8):
                            n = n0 + kk // 4
                            if f == 0 and s == 0 and kk % 4 == 0:
                                full = k.ring.full(n)
                                pe.wait_ge(k.ring.landed[n % RING], full if reg is None else full + reg * (16 * BATCH_LOADS))
                            if kk == 0 and wait_bank:
                                need = f0 + f - 3
                                pe.wait_ge(done.sem, done.at(need) if reg is None else reg * 4 + done.at(need))
                            col = s * 256 + f * P
                            mm = pe.matmul(bank_of(f0 + f, s)[:, :], slot(k, n, 4, 512)[:, kk % 4, col:col + P],
                                           k.hT[:, kk, :], start=(kk == 0), stop=(kk == 7))
                        mm.then_inc(k.tile_full.sem, 1)
                pe_used(k, pe, 2)

            pe.wait_ge(k.h_ready.sem, k.h_ready.at(8))
            pe.wait_ge(k.rstd_ready.sem, k.rstd_ready.at(1))
            group(first, 0, None, False)
            group(first + 2, 2, None, False)
            with pe.Fori(0, LOOPS - 1) as i:
                group(first + 4, 4, i, True)
                group(first + 6, 6, i, True)
            n = first + 4 * LOOPS
            group(n, 4 * LOOPS, None, True)
            n += 2
            full = lambda m: k.ring.full(m)

            def rows(m, reg, kk0, wait, f_lo, last_rows=False):
                pe.wait_ge(k.ring.landed[m % RING], full(m) if reg is None else full(m) + reg * (16 * BATCH_LOADS))
                for r in range(2):
                    for o in range(8):
                        rhs = act_t[:, bass.ds(reg * (8 * 512) + (kk0 + r) * 512, 512)] if reg is not None \
                            else act_t[:, (kk0 + r) * 512:(kk0 + r + 1) * 512]
                        mm = pe.matmul(bank(k, o)[:, :], slot(k, m, 2, 1024)[:, r, o * P:(o + 1) * P], rhs,
                                       start=(kk0 + r == 0 and reg is None), stop=last_rows and r == 1)
                        if last_rows and r == 1:
                            mm.then_inc(k.tile_full.sem, 1)
                pe_used(k, pe, 1)

            pe.wait_ge(done.sem, done.at(FT))
            rows(n, None, 0, True, 0)
            with pe.Fori(0, 2) as i:
                for j in range(4):
                    rows(n + 1 + j, i, 2 + 2 * j, False, 0)
            rows(n + 9, None, 18, False, 0)
            rows(n + 10, None, 20, False, 0, True)
        k.ring.took = first + total

        @block.gpsimd
        def _(pool):
            for s in range(2):
                for i in range(2):
                    pool.memset(pad[s][i][:, 0:2], 0.0).then_inc(cleared.sem, 1)

        @block.scalar
        def _(act):
            act_squares(k, act, lambda kk: k.xT[:, kk, :], 512)
            act_rstd(k, act, 512)
            act.wait_ge(cleared.sem, cleared.at(4))

            def copies(f, reg, early):
                at = lambda sig, v: sig.at(v) if reg is None else reg * 4 + sig.at(v)
                for s in range(2 if both else 1):
                    tf = 2 * f + s + 1
                    act.wait_ge(k.tile_full.sem, k.tile_full.at(tf) if reg is None else reg * 8 + k.tile_full.at(tf))
                    if not early:
                        act.wait_ge((conv_a, conv_b)[s].sem, at((conv_a, conv_b)[s], f - 1))
                    act.copy(pad[s][f % 2][:, 2:514], bank_of(f, s)[:, :])\
                        .then_inc(padded.sem, 1)

            def gate(f, reg):
                at = lambda sig, v: sig.at(v) if reg is None else reg * 4 + sig.at(v)
                act.wait_ge(conv_a.sem, at(conv_a, f + 1))
                act.activation(acc[0][f % 2], acc[0][f % 2], ACT.Silu).then_inc(silu.sem, 1)

            for f in range(4):
                copies(f, None, f < 2)
                if f >= 1:
                    gate(f - 1, None)
            with act.Fori(0, LOOPS - 1) as i:
                for f in range(4, 8):
                    copies(f, i, False)
                    gate(f - 1, i)
            for f in range(4 * LOOPS, FT):
                copies(f, None, False)
                gate(f - 1, None)
            gate(FT - 1, None)

        @block.vector
        def _(dve):
            dve.wait_ge(k.rstd_ready.sem, k.rstd_ready.at(1))
            dve_norm(k, dve, lambda kk: k.hT[:, kk, :], lambda kk: k.xT[:, kk, :], gain, 512)

            def conv(f, reg):
                at = lambda sig, v, per=4: sig.at(v) if reg is None else reg * per + sig.at(v)
                vec = lambda c: k.vecs[:, c + f:c + f + 1] if reg is None else k.vecs[:, bass.ds(reg * 4 + (c + f), 1)]
                n_pad = (2 if both else 1)
                for s in range(n_pad):
                    dve.wait_ge(padded.sem, at(padded, n_pad * f + s + 1, 4 * n_pad))
                    dst, src = acc[s][f % 2], pad[s][f % 2]
                    t0, t1, t2 = (taps(j) + s * FT for j in range(3))
                    if bias is None:
                        k.dve_chain.link(dve, dve.tensor_scalar(dst, src[:, 2:514], vec(t2), None, ALU.mult))
                    else:
                        k.dve_chain.link(dve, dve.tensor_scalar(dst, src[:, 2:514], vec(t2), vec(bias), ALU.mult, ALU.add))
                    k.dve_chain.link(dve, dve.scalar_tensor_tensor(dst, src[:, 1:513], vec(t1), dst, ALU.mult, ALU.add))
                    dve.scalar_tensor_tensor(dst, src[:, 0:512], vec(t0), dst, ALU.mult, ALU.add)\
                        .then_inc((conv_a, conv_b)[s].sem, 1)

            def gated(f, reg):
                at = lambda sig, v, per=4: sig.at(v) if reg is None else reg * per + sig.at(v)
                dve.wait_ge(silu.sem, at(silu, f + 1))
                if both:
                    dve.wait_ge(conv_b.sem, at(conv_b, f + 1))
                else:
                    dve.wait_ge(k.tile_full.sem, at(k.tile_full, 2 * f + 2, 8))
                other = acc[1][f % 2] if both else bank_of(f, 1)[:, :]
                dst = act_t[:, f * 512:(f + 1) * 512] if reg is None else act_t[:, bass.ds(reg * 2048 + f * 512, 512)]
                dve.tensor_tensor(dst, acc[0][f % 2], other, ALU.mult).then_inc(done.sem, 1)

            per = 2 * (2 if both else 1)
            for f in range(4):
                if f >= 2:
                    dve.wait_ge(done.sem, done.at(f - 1))
                conv(f, None)
                if f >= 1:
                    gated(f - 1, None)
            k.dve_chain.per = 4 * per
            with dve.Fori(0, LOOPS - 1) as i:
                k.dve_chain.reg = i
                n0 = k.dve_chain.n
                for f in range(4, 8):
                    dve.wait_ge(done.sem, i * 4 + done.at(f - 1))
                    conv(f, i)
                    gated(f - 1, i)
                assert k.dve_chain.n - n0 == k.dve_chain.per
            k.dve_chain.reg = None
            k.dve_chain.n = n0 + k.dve_chain.per * (LOOPS - 1)
            for f in range(4 * LOOPS, FT):
                dve.wait_ge(done.sem, done.at(f - 1))
                conv(f, None)
                gated(f - 1, None)
            gated(FT - 1, None)
            for o in range(8):
                dve.wait_ge(k.tile_full.sem, k.tile_full.at(2 * FT + o + 1))
                dve.tensor_tensor(k.xT[:, o, :], k.xT[:, o, :], bank(k, o)[:, :], ALU.add).then_inc(k.tile_free.sem, 1)
    k.advance(sq_ready=8, sums_full=1, rstd_ready=1, h_ready=8, tile_full=2 * FT + 8, tile_free=8)
    for s, n in zip(k.ffn_sig, (FT * (2 if both else 1), FT, FT * (1 if both else 0), FT, FT, 4)):
        s.base += n


NCMP = 31


def kv_chunks(k, w_kv):
    wv = w_kv.rearrange("(k p) n -> p k n", p=P)
    out = []
    for half in range(2):
        out.append(lambda n, half=half: [
            (slot(k, n, 4, 512)[:, kk, :].rearrange("p (c two d) -> p c two d", c=4, two=2)[:, :, two, :],
             wv[:, 4 * half + kk, 0:256].rearrange("p (c d) -> p c d", c=4)) for kk in range(4) for two in range(2)])
    return out


def paired_query_chunks(k, w):
    wv = w.rearrange("(k p) n -> p k n", p=P)
    return [lambda n, k0=k0: [
        (slot(k, n, 4, 512)[:, kk, :].rearrange("p (j g d) -> p j g d", j=4, g=2)[:, :, g, :],
         wv[:, k0 + kk, g * 256:(g + 1) * 256].rearrange("p (j d) -> p j d", j=4)) for kk in range(4) for g in range(2)]
        for k0 in (0, 4)]


def paired_out_chunks(k, w, cols):
    first = lambda n: [(slot(k, n, 4, 512)[g * 64:(g + 1) * 64, :, :],
                        w[g * 256:(g + 1) * 256, cols:cols + 512].rearrange("(j p) n -> p j n", p=64)) for g in range(2)]
    return [first, chunks_of(k, w, cols)[1]]


def stage_nsa_in(k, a):
    k.qT, k.mqT = k.carve(0, (4, 512)), k.carve(2048, (4, 512))
    k.ksT, k.kwT = k.carve(4096, (512,)), k.carve(4608, (512,))
    k.vsw = k.carve(5120, (4, 256))
    kv2 = [k.carve(6144, (2, 512)), k.carve(7168, (2, 512))]
    k.kcT, k.vc = k.carve(8192, (32,)), k.carve(8224, (P,))
    k.gates = k.carve(8352, (4, 24))
    hid = [[k.carve(8448 + (2 * s + ht) * 62, (62,)) for ht in range(2)] for s in range(2)]
    cb = k.carve(8696, (4,))
    w2k, w2v = k.carve(8704, (2, P)), k.carve(8960, (2, 64))
    wg = k.carve(9088, (8, 24))
    h2 = k.carve(9280, (8, 512))
    k.bias_of, k.bias_cmp = k.carve(13376, (8, 512)), k.carve(17472, (8, 124))
    small_in, slopes = k.sem("nsa_small_in"), k.sem("alibi_ready")
    first = k.ring.took
    gates_ready = k.sem("gates_ready")
    with k.nc.Block() as block:
        @block.sync
        def _(sp):
            w2 = a["w_ck2"].rearrange("(k p) n -> p k n", p=P)
            for two in range(2):
                sp.dma_start(w2k[:, :, two * 64:(two + 1) * 64], w2).then_inc(small_in, 16)
            sp.dma_start(w2v[:, :, :], a["w_cv2"].rearrange("(k p) n -> p k n", p=P)).then_inc(small_in, 16)
            sp.dma_start(wg[:, :, :], a["b_w_in"][0].rearrange("(k p) n -> p k n", p=P)[:, :, 512:536]).then_inc(small_in, 16)
            stream(k, sp, first + 12)

        @block.gpsimd
        def _(pool):
            for h in range(8):
                pool.tensor_scalar(k.bias_of[:, h, :], k.dist[:, :], 2.0 ** -(h + 1), None, ALU.mult).then_inc(slopes, 1)
                pool.tensor_scalar(k.bias_cmp[:, h, :], k.dist_cmp[:, :], 2.0 ** -(h + 1), None, ALU.mult).then_inc(slopes, 1)
            pool.wait_ge(slopes, 16)

        @block.vector
        def _(dve):
            dve.wait_ge(k.rstd_ready.sem, k.rstd_ready.at(1))
            x = lambda kk: k.xT[:, kk, :]
            dve_norm(k, dve, lambda kk: k.hT[:, kk, :], x, VEC_ROWS["g_kv"], 512)
            dve_norm(k, dve, lambda kk: h2[:, kk, :], x, VEC_ROWS["g_mix1"], 512)
            dve.wait_ge(gates_ready, 1)
            first_rows = k.gates[:, 0, :].rearrange("p (h b) -> p h b", b=3)[:, :, 0]
            k.dve_chain.link(dve, dve.tensor_scalar(first_rows, first_rows, k.valid[:, 0:1], None, ALU.mult))

        @block.scalar
        def _(act):
            act_squares(k, act, lambda kk: k.xT[:, kk, :], 512)
            act_rstd(k, act, 512)
            for t in range(25):
                act.wait_ge(k.tile_full.sem, k.tile_full.at(t + 1))
                src = bank(k, t)
                if t < 4:
                    dst = kv2[t // 2][:, t % 2, :]
                    k.act_chain.link(act, act.copy(dst[0:64, :], src[0:64, :]))
                    ins = act.copy(dst[64:P, 0:511], src[64:P, 1:512])
                elif t < 6:
                    ins = act.copy(k.ksT if t == 4 else k.kwT, src[:, :])
                elif t < 10:
                    ins = act.copy(k.vsw[:, t - 6, :], src[:, 0:256])
                elif t < 14:
                    s, ht = divmod(t - 10, 2)
                    col = cb[:, t - 10:t - 9]
                    k.act_chain.link(act, act.copy(col, src[:, 64:65]))
                    ins = act.activation(hid[s][ht], src[:, 0:62], ACT.Gelu_apprx_tanh, bias=col)
                elif t == 14:
                    k.act_chain.link(act, act.copy(k.kcT[0:64, 0:NCMP], src[0:64, 0:NCMP]))
                    ins = act.copy(k.kcT[64:P, 0:NCMP], src[64:P, NCMP:2 * NCMP])
                elif t == 15:
                    ins = act.copy(k.vc[0:NCMP, :], src[0:NCMP, 0:P])
                elif t < 20:
                    ins = act.mul(k.qT[:, t - 16, :], src[:, :], -(64 ** -0.5))
                elif t == 20:
                    k.act_chain.link(act, act.activation(k.gates[:, :, :].rearrange("p a b -> p (a b)"), src[:, 0:96], ACT.Sigmoid))
                    act.sem_inc(gates_ready, 1)
                    act.sem_inc(k.tile_free.sem, 1)
                    continue
                else:
                    ins = act.mul(k.mqT[:, t - 21, :], src[:, :], -(128 ** -0.5))
                ins.then_inc(k.tile_free.sem, 1)

        @block.tensor
        def _(pe):
            pe_norm_sums(k, pe, 512)
            pe.wait_ge(k.h_ready.sem, k.h_ready.at(8))
            h = lambda kk: k.hT[:, kk, :]
            cs = [take_chunk(k, pe), take_chunk(k, pe)]
            t = pe_feature_tiles(k, pe, 0, h, 512, [m * P for m in range(4)], cs)
            pe_used(k, pe, 2)
            cs = [take_chunk(k, pe), take_chunk(k, pe)]
            t = pe_feature_tiles(k, pe, t, h, 512, [0, 256], cs)
            t = pe_token_tiles(k, pe, t, lambda kk, tt: k.hT[:, kk, tt * P:(tt + 1) * P], 4,
                               lambda kk: slot(k, cs[kk // 4], 4, 512)[:, kk % 4, :]
                               .rearrange("p (b two n) -> p b two n", b=2, two=2)[:, :, 1, :], 256)
            pe_used(k, pe, 2)
            for s in range(2):
                cs = [take_chunk(k, pe), take_chunk(k, pe)]
                if s == 0:
                    pe.wait_ge(k.tile_free.sem, k.tile_free.at(4))
                for ht in range(2):
                    pe_wait_bank(k, pe, t)
                    for part in range(2):
                        for j in range(16):
                            w = slot(k, cs[j // 8], 8, 256)[:, j % 8, ht * P:(ht + 1) * P]
                            if part == 0:
                                rhs = kv2[s][:, :, 2 * j:2 * j + 16 * (NCMP - 1) + 1:16]
                                mm = pe.matmul(bank(k, t)[:, 0:2 * NCMP], w, rhs, start=(j == 0), stop=(j == 15))
                            else:
                                c = VEC_ROWS["pe_v" if s else "pe_k"] + j
                                mm = pe.matmul(bank(k, t)[:, 64:65], w, k.vec(c), start=(j == 0), stop=(j == 15))
                    mm.then_inc(k.tile_full.sem, 1)
                    t += 1
                pe_used(k, pe, 2)
            pe.wait_ge(small_in, 64)
            pe.wait_ge(k.tile_free.sem, k.tile_free.at(14))
            for ht in range(2):
                mm = pe.matmul(bank(k, t)[:, 0:62], w2k[:, ht, :], hid[0][ht], start=(ht == 0), stop=(ht == 1))
            mm.then_inc(k.tile_full.sem, 1)
            t += 1
            for g in range(2):
                for ht in range(2):
                    mm = pe.matmul(bank(k, t)[0:NCMP, g * 64:(g + 1) * 64], hid[1][ht][:, g * NCMP:(g + 1) * NCMP], w2v[:, ht, :],
                                   start=(ht == 0), stop=(ht == 1))
            mm.then_inc(k.tile_full.sem, 1)
            t += 1
            pe.wait_ge(k.h_ready.sem, k.h_ready.at(16))
            hh = lambda kk: h2[:, kk, :]
            cs = [take_chunk(k, pe), take_chunk(k, pe)]
            t = pe_feature_tiles(k, pe, t, hh, 512, [m * P for m in range(4)], cs)
            pe_used(k, pe, 2)
            pe_wait_bank(k, pe, t)
            for tt in range(4):
                for kk in range(8):
                    mm = pe.matmul(bank(k, t)[:, tt * 24:(tt + 1) * 24], h2[:, kk, tt * P:(tt + 1) * P], wg[:, kk, :],
                                   start=(kk == 0), stop=(kk == 7))
            mm.then_inc(k.tile_full.sem, 1)
            t += 1
            cs = [take_chunk(k, pe), take_chunk(k, pe)]
            t = pe_feature_tiles(k, pe, t, hh, 512, [m * P for m in range(4)], cs)
            pe_used(k, pe, 2)
    k.advance(sq_ready=8, sums_full=1, rstd_ready=1, h_ready=16, tile_full=25, tile_free=25)
    k.ma = 9280


def stage_nsa(k):
    prob = [[[k.carve(18464 + par * 2688 + br * 1280 + 64 * i * (i + 1), ((i + 1) * P,)) for i in range(4)]
             for br in range(2)] for par in range(2)]
    pcmp = [k.carve(18464 + par * 2688 + 2560, (4, NCMP)) for par in range(2)]
    at = [9280, 23840]
    offs = [0, 512, 896, 1152]
    pT = [[[k.carve(at[par] + br * 1280 + offs[j], (512 - j * P,)) for j in range(4)] for br in range(2)] for par in range(2)]
    pcT = [k.carve(at[par] + 2560, (512,)) for par in range(2)]
    low, tot, coef = (k.carve(26912 + i * 96, (8, 12)) for i in range(3))
    s_full, z_ready, e_done, p_ready = (k.sem(n) for n in ("nsa_scores", "nsa_lows", "nsa_exps", "nsa_probs"))
    t_full, t_out_a, t_out_v, o_full, o_out = (k.sem(n) for n in ("nsa_turned", "nsa_turned_act", "nsa_turned_dve", "nsa_full", "nsa_out"))
    zc_ready, lc_ready = k.sem("nsa_cmp_added"), k.sem("nsa_cmp_low")
    by_vector = lambda n: (n % 9) % 2 == 1
    copies_by = lambda which, n: sum(by_vector(m) == bool(which) for m in range(n))
    copied = lambda n: (int(by_vector(n)), copies_by(int(by_vector(n)), n + 1))
    units = [(i, br) for i in range(4) for br in range(2)]

    with k.nc.Block() as block:
        @block.tensor
        def _(pe):
            def scores(h):
                j, g = h % 4, h // 4
                r = slice(g * 64, (g + 1) * 64)
                for u, (i, br) in enumerate(units):
                    n = 8 * h + u
                    if n >= 3:
                        pe.wait_ge(z_ready, n - 2)
                    keys = (k.ksT, k.kwT)[br]
                    pe.matmul(bank(k, n % 3)[:, 0:(i + 1) * P], k.qT[r, j, i * P:(i + 1) * P], keys[r, 0:(i + 1) * P],
                              start=True, stop=True).then_inc(s_full, 1)
                if h >= 1:
                    pe.wait_ge(zc_ready, h)
                for i in range(4):
                    mm = pe.matmul(bank(k, 3)[:, i * 32:i * 32 + NCMP], k.qT[r, j, i * P:(i + 1) * P], k.kcT[r, 0:NCMP],
                                   start=True, stop=True)
                mm.then_inc(s_full, 1)

            def turn(h):
                pe.wait_ge(p_ready, 9 * (h + 1))
                for m in range(9):
                    n = 9 * h + m
                    if n >= 2:
                        which, count = copied(n - 2)
                        pe.wait_ge((t_out_a, t_out_v)[which], count)
                    b = bank(k, 4 + n % 2)
                    if m < 8:
                        br, j = divmod(m, 4)
                        for i in range(j, 4):
                            mm = pe.transpose(b[:, (i - j) * P:(i - j + 1) * P], prob[h % 2][br][i][:, j * P:(j + 1) * P], k.ident[:, :])
                    else:
                        for i in range(4):
                            mm = pe.transpose(b[0:NCMP, i * P:(i + 1) * P], pcmp[h % 2][:, i, :], k.ident[:, :])
                    mm.then_inc(t_full, 1)

            def values(h):
                if h >= 2:
                    pe.wait_ge(o_out, h - 1)
                o = bank(k, 6 + h % 2)
                for which in range(2):
                    pe.wait_ge((t_out_a, t_out_v)[which], copies_by(which, 9 * (h + 1)))
                pe.matmul(o[:, :], k.vc[0:NCMP, :], pcT[h % 2][0:NCMP, :], start=True, stop=False)
                for br in range(2):
                    for j in range(4):
                        mm = pe.matmul(o[:, j * P:512], k.vsw[:, j, br * P:(br + 1) * P], pT[h % 2][br][j],
                                       start=False, stop=(br == 1 and j == 3))
                mm.then_inc(o_full, 1)

            scores(0)
            for h in range(8):
                if h < 7:
                    scores(h + 1)
                turn(h)
                if h >= 1:
                    values(h - 1)
            values(7)

        def copy_turned(copy, eng, h, m):
            n = 9 * h + m
            eng.wait_ge(t_full, n + 1)
            if h >= 2:
                eng.wait_ge(o_full, h - 1)
            b = bank(k, 4 + n % 2)
            if m == 8:
                return copy(pcT[h % 2][0:NCMP, :], b[0:NCMP, :])
            br, j = divmod(m, 4)
            return copy(pT[h % 2][br][j], b[:, 0:512 - j * P])

        @block.vector
        def _(dve):
            L = lambda ins: k.dve_chain.link(dve, ins)

            def lows(h):
                if h >= 2:
                    dve.wait_ge(t_full, 9 * (h - 1))
                for u, (i, br) in enumerate(units):
                    dve.wait_ge(s_full, 9 * h + u + 1)
                    n = (i + 1) * P
                    dve.tensor_tensor_reduce(prob[h % 2][br][i], bank(k, (8 * h + u) % 3)[:, 0:n],
                                             k.bias_of[:, h, 384 - i * P:512], 1.0, 3e38, ALU.add, ALU.min,
                                             low[:, h, 4 * br + i:4 * br + i + 1]).then_inc(z_ready, 1)
                dve.wait_ge(s_full, 9 * (h + 1))
                dve.tensor_tensor(pcmp[h % 2][:, :, :], bank(k, 3)[:, 0:P].rearrange("p (i n) -> p i n", i=4)[:, :, 0:NCMP],
                                  k.bias_cmp[:, h, :].rearrange("p (i n) -> p i n", i=4), ALU.add).then_inc(zc_ready, 1)
                dve.wait_ge(zc_ready, h + 1)
                dve.tensor_reduce(low[:, h, 8:12], pcmp[h % 2][:, :, :], AX.X, ALU.min).then_inc(lc_ready, 1)

            def weigh(h):
                dve.wait_ge(e_done, 12 * (h + 1))
                L(dve.reciprocal(coef[:, h, :], tot[:, h, :]))
                gates = k.gates[:, :, 3 * h:3 * h + 3].rearrange("p i b -> p b i")
                cv = coef[:, h, :].rearrange("p (b i) -> p b i", b=3)
                L(dve.tensor_tensor(cv[:, 0:2, :], cv[:, 0:2, :], gates[:, 1:3, :], ALU.mult))
                L(dve.tensor_tensor(cv[:, 2, :], cv[:, 2, :], gates[:, 0, :], ALU.mult))
                for br in range(2):
                    for i in range(4):
                        p = prob[h % 2][br][i]
                        dve.tensor_scalar(p, p, coef[:, h, 4 * br + i:4 * br + i + 1], None, ALU.mult).then_inc(p_ready, 1)
                dve.tensor_tensor(pcmp[h % 2][:, :, :], pcmp[h % 2][:, :, :],
                                  coef[:, h, 8:12].unsqueeze(2).broadcast_to([P, 4, NCMP]), ALU.mult).then_inc(p_ready, 1)

            def turned(h):
                for m in range(9):
                    if by_vector(9 * h + m):
                        copy_turned(dve.tensor_copy, dve, h, m).then_inc(t_out_v, 1)

            lows(0)
            for h in range(8):
                if h >= 1:
                    turned(h - 1)
                weigh(h)
                if h < 7:
                    lows(h + 1)
            turned(7)

        @block.scalar
        def _(act):
            def exps(h):
                for u, (i, br) in enumerate(units):
                    act.wait_ge(z_ready, 8 * h + u + 1)
                    p, c = prob[h % 2][br][i], 4 * br + i
                    act.activation(p, p, ACT.Exp, bias=low[:, h, c:c + 1], scale=-1.0,
                                   accum_out=tot[:, h, c:c + 1]).then_inc(e_done, 1)
                act.wait_ge(lc_ready, h + 1)
                for i in range(4):
                    act.activation(pcmp[h % 2][:, i, :], pcmp[h % 2][:, i, :], ACT.Exp, bias=low[:, h, 8 + i:9 + i], scale=-1.0,
                                   accum_out=tot[:, h, 8 + i:9 + i]).then_inc(e_done, 1)

            def finish(h):
                act.wait_ge(o_full, h + 1)
                r = slice(h // 4 * 64, (h // 4 + 1) * 64)
                act.copy(k.catT[r, h % 4, :], bank(k, 6 + h % 2)[r, :]).then_inc(o_out, 1)

            exps(0)
            for h in range(8):
                if h < 7:
                    exps(h + 1)
                for m in range(9):
                    if not by_vector(9 * h + m):
                        copy_turned(act.copy, act, h, m).then_inc(t_out_a, 1)
                if h >= 1:
                    finish(h - 1)
            finish(7)


def mixed_chunks(k, w, parts):
    wv = w.rearrange("(k p) n -> p k n", p=P)
    return [lambda n, k0=k0: [(slot(k, n, 4, 512)[:, :, s * 256:(s + 1) * 256], wv[:, k0:k0 + 4, c:c + 256])
                              for s, c in enumerate(parts)] for k0 in (0, 4)]


def stage_mix_in(k, a):
    k.scb, k.scc, k.prod = k.carve(0, (2, 512)), k.carve(1024, (2, 512)), k.carve(2048, (2, 516))
    k.qkv = k.carve(3080, (12, 512))
    k.zT = k.carve(9224, (4, 512))
    k.sbq, k.sbk, k.sbv = k.carve(11272, (2, 512)), k.carve(12296, (2, 512)), k.carve(13320, (4, 256))
    k.gab = k.carve(14344, (32,))
    w_ab = k.carve(14376, (8, 8))
    raw = [k.carve(14640 + i * 516, (516,)) for i in range(2)]
    acc = [k.carve(15680 + i * 512, (512,)) for i in range(2)]
    k.decay_row = k.carve(16720, (8,))
    k.decay_all = k.carve(14568, (8,))
    k.silu_done = k.sem("mix_silu_done")
    small_in, cleared, raw_in, conv_done = (k.sem(n) for n in ("mix_small_in", "mix_cleared", "mix_raw_in", "mix_conv_done"))
    first = k.ring.took
    taps = VEC_ROWS["w_gdn_conv_2"]
    CONV0 = 10
    with k.nc.Block() as block:
        @block.sync
        def _(sp):
            sp.dma_start(w_ab[:, :, :], a["w_mix_in_2"][0].rearrange("(k p) n -> p k n", p=P)[:, :, 2816:2824]).then_inc(small_in, 16)
            sp.dma_start(k.decay_row[0:1, 0:4], a["gdn_a_log_2"]).then_inc(small_in, 16)
            sp.dma_start(k.decay_row[0:1, 4:8], a["gdn_dt_bias_2"]).then_inc(small_in, 16)
            stream(k, sp, first + 14)

        @block.gpsimd
        def _(pool):
            for i in range(2):
                pool.memset(raw[i][:, 0:3], 0.0).then_inc(cleared, 1)
                pool.memset(k.prod[:, i, 0:2], 0.0).then_inc(cleared, 1)

        @block.vector
        def _(dve):
            L = lambda ins: k.dve_chain.link(dve, ins)
            x = lambda kk: k.xT[:, kk, :]
            dve.wait_ge(k.rstd_ready.sem, k.rstd_ready.at(1))
            dve_norm(k, dve, x, x, VEC_ROWS["g_final"], 512)
            dve.wait_ge(k.rstd_ready.sem, k.rstd_ready.at(2))
            dve_norm(k, dve, lambda kk: k.hT[:, kk, :], x, VEC_ROWS["w_norm_mix_2"], 512)
            for i in range(2):
                dve.wait_ge(k.tile_free.sem, k.tile_free.at(5 + i))
                p = k.prod[:, i, 2:514]
                L(dve.tensor_tensor(p, p, k.scc[:, i, :], ALU.mult))
            for n in range(12):
                dve.wait_ge(raw_in, n + 1)
                if n >= 2:
                    dve.wait_ge(k.silu_done, n - 1)
                dst, src = acc[n % 2], raw[n % 2]
                L(dve.tensor_scalar(dst, src[:, 3:515], k.vec(taps + 36 + n), None, ALU.mult))
                for j in (2, 1):
                    L(dve.scalar_tensor_tensor(dst, src[:, j:j + 512], k.vec(taps + 12 * j + n), dst, ALU.mult, ALU.add))
                dve.scalar_tensor_tensor(dst, src[:, 0:512], k.vec(taps + n), dst, ALU.mult, ALU.add).then_inc(conv_done, 1)

        @block.scalar
        def _(act):
            act_squares(k, act, lambda kk: k.xT[:, kk, :], 512)
            act_rstd(k, act, 512)
            k.sums_full.base += 1
            for kk in range(8):
                act.wait_ge(k.h_ready.sem, k.h_ready.at(kk + 1))
                act.activation(k.sq[:, kk, :], k.xT[:, kk, :], ACT.Square).then_inc(k.sq_ready.sem, 1)
            act_rstd(k, act, 512)
            k.sums_full.base -= 1
            act.wait_ge(cleared, 4)

            def silu(n):
                act.wait_ge(conv_done, n + 1)
                act.activation(k.qkv[:, n, :], acc[n % 2], ACT.Silu).then_inc(k.silu_done, 1)

            for t in range(31):
                act.wait_ge(k.tile_full.sem, k.tile_full.at(t + 1))
                src = bank(k, t)
                if t < 2:
                    ins = act.copy(k.scb[:, t, :], src[:, :])
                elif t < 4:
                    ins = act.copy(k.scc[:, t - 2, :], src[:, :])
                elif t < 6:
                    ins = act.copy(k.prod[:, t - 4, 2:514], src[:, :])
                elif t < 10:
                    ins = act.copy(k.sbv[:, t - 6, :], src[:, 0:256])
                elif t < 22:
                    n = t - CONV0
                    if n >= 2:
                        act.wait_ge(conv_done, n - 1)
                    k.act_chain.link(act, act.copy(raw[n % 2][:, 3:515], src[:, :]))
                    act.sem_inc(raw_in, 1)
                    act.sem_inc(k.tile_free.sem, 1)
                    if n >= 1:
                        silu(n - 1)
                    continue
                elif t < 26:
                    if t == 22:
                        silu(11)
                    ins = act.activation(k.zT[:, t - 22, :], src[:, :], ACT.Silu)
                elif t < 28:
                    ins = act.mul(k.sbq[:, t - 26, :], src[:, :], 64 ** -0.5)
                elif t < 30:
                    ins = act.copy(k.sbk[:, t - 28, :], src[:, :])
                else:
                    k.act_chain.link(act, act.copy(k.decay_all[:, :], src[:, 64:72]))
                    ins = act.copy(k.gab[:, :], src[:, 0:32])
                ins.then_inc(k.tile_free.sem, 1)

        @block.tensor
        def _(pe):
            pe_norm_sums(k, pe, 512)
            k.sq_ready.base += 8
            pe_norm_sums(k, pe, 512)
            k.sq_ready.base -= 8
            pe.wait_ge(k.h_ready.sem, k.h_ready.at(16))
            h = lambda kk: k.hT[:, kk, :]
            t = 0
            for group in range(7):
                cs = [take_chunk(k, pe), take_chunk(k, pe)]
                t = pe_feature_tiles(k, pe, t, h, 512, [m * P for m in range(2 if group == 1 else 4)], cs)
                if group == 1:
                    t = pe_token_tiles(k, pe, t, lambda kk, tt: k.hT[:, kk, tt * P:(tt + 1) * P], 4,
                                       lambda kk: slot(k, cs[kk // 4], 4, 512)[:, kk % 4, 256:512], 256)
                pe_used(k, pe, 2)
            pe.wait_ge(small_in, 48)
            pe_wait_bank(k, pe, t)
            for tt in range(4):
                for kk in range(8):
                    pe.matmul(bank(k, t)[:, tt * 8:(tt + 1) * 8], k.hT[:, kk, tt * P:(tt + 1) * P], w_ab[:, kk, :],
                              start=(kk == 0), stop=(kk == 7))
            pe.matmul(bank(k, t)[:, 64:72], k.ones[0:1, :], k.decay_row[0:1, :], start=True, stop=True)\
                .then_inc(k.tile_full.sem, 1)
    k.advance(sq_ready=16, sums_full=2, rstd_ready=2, h_ready=16, tile_full=31, tile_free=31)


def stage_delta(k, a):
    H, C = 4, 4
    cq, ck, cv = k.qkv[:, 0:4, :], k.qkv[:, 4:8, :], k.qkv[:, 8:12, :]
    small = lambda i: k.carve(14440 + 16 * i, (C, H))
    g, beta, G, expG, bexp, tail, tmp = (small(i) for i in range(7))
    EG = k.carve(14720, (H, 512))
    D = k.carve(16768, (H, 512))
    LT = k.carve(18816, (H, 512))
    attn = k.carve(20864, (H, 512))
    Kb, Kbar, Vb = k.carve(22912, (H, 512)), k.carve(24960, (H, 512)), k.carve(27008, (H, 512))
    X = k.carve(29056, (H, 512))
    g_wide, beta_wide = k.carve(20864, (16, P)), k.carve(22912, (16, P))
    sqs = k.carve(24960, (8, 512))
    rs = k.carve(16768, (8, 512))
    chunk = lambda t: t.rearrange("p h (c n) -> p h c n", c=C)
    by_head = lambda t: t[:, :, :].rearrange("p c h -> p h c")
    k.last_decay = k.carve(14600, (H, C))
    conv = k.prod
    sq, nf, rd = k.sem("delta_squares"), k.sem("delta_sums"), k.sem("delta_rstd")
    gates, wide, cum = k.sem("delta_gates"), k.sem("delta_wide"), k.sem("delta_cum")

    with k.nc.Block() as block:
        @block.scalar
        def _(act):
            L = lambda ins: k.act_chain.link(act, ins)
            gab = k.gab.rearrange("p (c n) -> p c n", c=C)
            L(act.activation(beta[:, :, :], gab[:, :, 4:8], ACT.Sigmoid))
            for n in range(8):
                act.activation(sqs[:, n, :], k.qkv[:, n, :], ACT.Square).then_inc(sq, 1)
            act.wait_ge(gates, 1)
            L(act.activation(tmp[:, :, :], g[:, :, :], ACT.Abs))
            L(act.activation(tmp[:, :, :], tmp[:, :, :], ACT.Exp, scale=-1.0))
            L(act.activation(k.decay_all[:, 0:4], k.decay_all[:, 0:4], ACT.Exp))
            L(act.activation(tmp[:, :, :], tmp[:, :, :], ACT.Ln, bias=1.0))
            act.sem_inc(gates, 1)
            for n in range(8):
                act.wait_ge(nf, n + 1)
                L(act.activation(rs[:, n, :], bank(k, n)[:, :], ACT.Ln, bias=k.eps[:, 0:1]))
                act.activation(rs[:, n, :], rs[:, n, :], ACT.Exp, scale=-0.5).then_inc(rd, 1)

        @block.tensor
        def _(pe):
            for n in range(8):
                pe.wait_ge(sq, n + 1)
                pe.matmul(bank(k, n)[:, :], k.ones[:, :], sqs[:, n, :], start=True, stop=True).then_inc(nf, 1)

        @block.vector
        def _(dve):
            L = lambda ins: k.dve_chain.link(dve, ins)
            gab = k.gab.rearrange("p (c n) -> p c n", c=C)
            head_row = lambda cols: k.decay_all[:, cols:cols + 4].unsqueeze(1).broadcast_to([P, C, H])
            dve.tensor_tensor(g[:, :, :], gab[:, :, 0:4], head_row(4), ALU.add).then_inc(gates, 1)
            taps = VEC_ROWS["w_sconv_2"]
            for i in range(2):
                y = k.scc[:, i, :]
                L(dve.tensor_scalar(y, conv[:, i, 2:514], k.vec(taps + 4 + i), None, ALU.mult))
                L(dve.scalar_tensor_tensor(y, conv[:, i, 1:513], k.vec(taps + 2 + i), y, ALU.mult, ALU.add))
                L(dve.scalar_tensor_tensor(y, conv[:, i, 0:512], k.vec(taps + i), y, ALU.mult, ALU.add))
                L(dve.tensor_tensor(k.catT[:, i, :], y, k.scb[:, i, :], ALU.mult))
            dve.wait_ge(gates, 2)
            L(dve.scalar_tensor_tensor(g[:, :, :], g[:, :, :], 0.0, tmp[:, :, :], ALU.max, ALU.add))
            L(dve.scalar_tensor_tensor(g[:, :, :], g[:, :, :], -1.0, head_row(0), ALU.mult, ALU.mult))
            flat = lambda t: t[:, :, :].rearrange("p c h -> p (c h)").unsqueeze(2).broadcast_to([P, 16, P])
            ones = k.ones[:, :].unsqueeze(1).broadcast_to([P, 16, P])
            L(dve.tensor_tensor(g_wide[:, :, :], ones, flat(g), ALU.mult))
            L(dve.tensor_tensor(beta_wide[:, :, :], ones, flat(beta), ALU.mult))
            for n in range(8):
                dve.wait_ge(rd, n + 1)
                dst = k.qkv[:, n, :]
                dve.scalar_tensor_tensor(dst, dst, 128 ** -0.5 if n < 4 else 1.0, rs[:, n, :], ALU.mult, ALU.mult).then_inc(wide, 1)
            dve.wait_ge(wide, 8)

    gb, bb, st, ex, dc = (k.sem(n) for n in ("delta_G_wide", "delta_beta_wide", "delta_steps", "delta_exps", "delta_decay"))
    with k.nc.Block() as block:
        @block.tensor
        def _(pe):
            for h in range(H):
                for c in range(C):
                    mm = pe.matmul(bank(k, h)[:, c * P:(c + 1) * P], g_wide[:, c * H + h, :], k.triu[:, :], start=True, stop=True)
                mm.then_inc(gb, 1)
            pe.matmul(bank(k, 4)[:, 0:16], k.triu[:, :], g[:, :, :].rearrange("p c h -> p (c h)"), start=True, stop=True)\
                .then_inc(cum, 1)
            pe.wait_ge(st, 1)
            for h in range(H):
                for c in range(C):
                    mm = pe.matmul(bank(k, 4 + h)[:, c * P:(c + 1) * P], beta_wide[:, c * H + h, :], k.ident[:, :], start=True, stop=True)
                mm.then_inc(bb, 1)

        @block.vector
        def _(dve):
            L = lambda ins: k.dve_chain.link(dve, ins)
            dve.wait_ge(cum, 1)
            dve.tensor_copy(G[:, :, :].rearrange("p c h -> p (c h)"), bank(k, 4)[:, 0:16]).then_inc(st, 1)
            dve.wait_ge(st, 1)
            for h in range(H):
                dve.wait_ge(ex, h + 1)
                for c in range(C):
                    ins = dve.tensor_scalar(D[:, h, c * P:(c + 1) * P], bank(k, h)[:, c * P:(c + 1) * P], G[:, c, h:h + 1], 0.0,
                                            ALU.subtract, ALU.min)
                    ins.then_inc(dc, 1)
                dve.tensor_tensor(tail[:, :, h], bank(k, h)[:, P - 1:512:P], G[:, :, h], ALU.subtract).then_inc(dc, 1)
            dve.wait_ge(ex, 7)
            L(dve.tensor_tensor(bexp[:, :, :], beta[:, :, :], expG[:, :, :], ALU.mult))
            mask = lambda m: m[:, :].unsqueeze(1).broadcast_to([P, C, P])
            for h in range(H):
                L(dve.tensor_tensor(chunk(D)[:, h], chunk(D)[:, h], mask(k.triu), ALU.mult))
                dve.wait_ge(bb, h + 1)
                L(dve.tensor_tensor(LT[:, h, :], D[:, h, :], bank(k, 4 + h)[:, :], ALU.mult))
                L(dve.tensor_tensor(chunk(LT)[:, h], chunk(LT)[:, h], mask(k.triu_strict), ALU.mult))

        @block.scalar
        def _(act):
            for h in range(H):
                act.wait_ge(gb, h + 1)
                act.activation(EG[:, h, :], bank(k, h)[:, :], ACT.Exp).then_inc(ex, 1)
            act.wait_ge(st, 1)
            act.activation(expG[:, :, :], G[:, :, :], ACT.Exp).then_inc(ex, 1)
            act.wait_ge(dc, 20)
            act.activation(tail[:, :, :], tail[:, :, :], ACT.Exp).then_inc(ex, 1)
            act.activation(D[:, :, :], D[:, :, :], ACT.Exp).then_inc(ex, 1)

    turned, used, prod_f, prod_r, qe_ready = (k.sem(n) for n in ("delta_turned", "delta_turned_used", "delta_prod", "delta_prod_used", "delta_qe"))
    with k.nc.Block() as block:
        @block.tensor
        def _(pe):
            for n in range(8):
                src = (ck, cv)[n % 2][:, n // 2, :]
                if n >= 4:
                    pe.wait_ge(used, n - 3)
                for c in range(C):
                    mm = pe.transpose(bank(k, n % 4)[:, c * P:(c + 1) * P], src[:, c * P:(c + 1) * P], k.ident[:, :])
                mm.then_inc(turned, 1)
            for n in range(8):
                h = n // 2
                if n >= 4:
                    pe.wait_ge(prod_r, n - 3)
                for c in range(C):
                    cs = slice(c * P, (c + 1) * P)
                    mm = pe.matmul(bank(k, 4 + n % 4)[:, cs], ck[:, h, cs], (ck, cq)[n % 2][:, h, cs], start=True, stop=True)
                mm.then_inc(prod_f, 1)

        @block.vector
        def _(dve):
            for n in range(8):
                h = n // 2
                dve.wait_ge(turned, n + 1)
                src = bank(k, n % 4)[:, :].rearrange("p (c n) -> p c n", c=C)
                wide_of = lambda t: by_head(t)[:, h, :].unsqueeze(2).broadcast_to([P, C, P])
                if n % 2 == 0:
                    k.dve_chain.link(dve, dve.tensor_tensor(chunk(Kbar)[:, h], src, wide_of(tail), ALU.mult))
                    dve.tensor_tensor(chunk(Kb)[:, h], src, wide_of(bexp), ALU.mult).then_inc(used, 1)
                else:
                    dve.tensor_tensor(chunk(Vb)[:, h], src, wide_of(beta), ALU.mult).then_inc(used, 1)
            for n in range(8):
                h = n // 2
                dve.wait_ge(prod_f, n + 1)
                dst, w = (LT, LT) if n % 2 == 0 else (attn, D)
                dve.tensor_tensor(dst[:, h, :], bank(k, 4 + n % 4)[:, :], w[:, h, :], ALU.mult).then_inc(prod_r, 1)

        @block.gpsimd
        def _(pool):
            k.pool_chain.link(pool, pool.tensor_copy(k.last_decay[:, :, :], EG[:, :, P - 1:512:P]))
            for h in range(H):
                pool.tensor_tensor(EG[:, h, :], EG[:, h, :], cq[:, h, :], ALU.mult).then_inc(qe_ready, 1)
            pool.wait_ge(qe_ready, H)

    R = cv
    Y = k.carve(3080, (H, 512))
    Lm = k.carve(16768, (4, 512))
    lm, yf, yr, xf, xr, rf, rr = (k.sem(n) for n in ("inv_masked", "inv_y", "inv_y_out", "inv_x", "inv_x_out", "inv_r", "inv_r_out"))
    eye = k.sem("inv_eye")
    with k.nc.Block() as block:
        @block.gpsimd
        def _(pool):
            mask = lambda lv: k.level[:, lv, :].unsqueeze(1).broadcast_to([P, C, P])
            for lv in range(7):
                for h in range(H):
                    n = lv * H + h
                    if n >= 4:
                        pool.wait_ge(yf, n - 3)
                    pool.tensor_tensor(chunk(Lm)[:, n % 4], chunk(LT)[:, h], mask(lv), ALU.mult).then_inc(lm, 1)

        @block.tensor
        def _(pe):
            blocks = [slice(c * P, (c + 1) * P) for c in range(C)]
            pe.wait_ge(eye, 8)
            for lv in range(7):
                def first(h):
                    n = lv * H + h
                    pe.wait_ge(lm, n + 1)
                    if lv:
                        pe.wait_ge(xr, (lv - 1) * H + h + 1)
                    if n >= 2:
                        pe.wait_ge(yr, n - 1)
                    for cs in blocks:
                        mm = pe.matmul(bank(k, n % 2)[:, cs], Lm[:, n % 4, cs], X[:, h, cs], start=True, stop=True)
                    mm.then_inc(yf, 1)

                def second(h):
                    n = lv * H + h
                    pe.wait_ge(yr, n + 1)
                    if lv:
                        pe.wait_ge(rr, (lv - 1) * H + h + 1)
                    if n >= 2:
                        pe.wait_ge(rr, n - 1)
                    if lv < 6:
                        if n >= 2:
                            pe.wait_ge(xr, n - 1)
                        for cs in blocks:
                            mm = pe.matmul(bank(k, 2 + n % 2)[:, cs], R[:, h, cs], Y[:, h, cs], start=True, stop=True)
                        mm.then_inc(xf, 1)
                    for cs in blocks:
                        mm = pe.matmul(bank(k, 4 + n % 2)[:, cs], Y[:, h, cs], R[:, h, cs], start=True, stop=True)
                    mm.then_inc(rf, 1)

                first(0)
                for h in range(H):
                    if h < 3:
                        first(h + 1)
                    second(h)

        @block.scalar
        def _(act):
            for n in range(7 * H):
                act.wait_ge(yf, n + 1)
                if n >= H:
                    act.wait_ge(rf, n - H + 1)
                act.copy(Y[:, n % H, :], bank(k, n % 2)[:, :]).then_inc(yr, 1)

        @block.vector
        def _(dve):
            eyes = k.ident[:, :].unsqueeze(1).broadcast_to([P, C, P])
            for h in range(H):
                dve.tensor_copy(chunk(X)[:, h], eyes).then_inc(eye, 1)
                dve.tensor_copy(chunk(R)[:, h], eyes).then_inc(eye, 1)
            dve.wait_ge(eye, 8)
            for n in range(7 * H):
                h = n % H
                if n < 6 * H:
                    dve.wait_ge(xf, n + 1)
                    if n >= H:
                        dve.wait_ge(xr, n - H + 1)
                    dve.tensor_tensor(X[:, h, :], X[:, h, :], bank(k, 2 + n % 2)[:, :], ALU.subtract).then_inc(xr, 1)
                dve.wait_ge(rf, n + 1)
                if n >= H:
                    dve.wait_ge(rr, n - H + 1)
                dve.tensor_tensor(R[:, h, :], R[:, h, :], bank(k, 4 + n % 2)[:, :], ALU.subtract).then_inc(rr, 1)

    S = [k.carve(5128 + i * 512, (H, P)) for i in range(2)]
    vn = [k.carve(6152 + i * 512, (H, P)) for i in range(2)]
    uw, uo = k.sem("delta_uw"), k.sem("delta_uw_out")
    with k.nc.Block() as block:
        @block.tensor
        def _(pe):
            for n in range(8):
                h = n // 2
                for c in range(C):
                    cs = slice(c * P, (c + 1) * P)
                    l, r = (R, Vb) if n % 2 == 0 else (Kb, R)
                    mm = pe.matmul(bank(k, n)[:, cs], l[:, h, cs], r[:, h, cs], start=True, stop=True)
                mm.then_inc(uw, 1)

        @block.scalar
        def _(act):
            for n in range(1, 8, 2):
                act.wait_ge(uw, n + 1)
                act.copy(Kb[:, n // 2, :], bank(k, n)[:, :]).then_inc(uo, 1)

        @block.vector
        def _(dve):
            for n in range(0, 8, 2):
                dve.wait_ge(uw, n + 1)
                dve.tensor_copy(Vb[:, n // 2, :], bank(k, n)[:, :]).then_inc(uo, 1)

    ws, vr, of, df, sr = (k.sem(n) for n in ("delta_ws", "delta_v_new", "delta_out", "delta_update", "delta_state"))
    o_sq, o_nf, o_rd, o_cp = (k.sem(n) for n in ("delta_out_sq", "delta_out_sums", "delta_out_rstd", "delta_out_copied"))
    o_sb, osq, rstd = k.carve(16768, (H, 512)), k.carve(18816, (H, 512)), k.carve(29056, (H, 512))
    with k.nc.Block() as block:
        @block.tensor
        def _(pe):
            for c in range(C):
                cs = slice(c * P, (c + 1) * P)
                s = S[(c - 1) % 2]
                if c:
                    pe.wait_ge(sr, c)
                    for h in range(H):
                        mm = pe.matmul(bank(k, 4)[:, h * P:(h + 1) * P], Kb[:, h, cs], s[:, h, :], start=True, stop=True)
                    mm.then_inc(ws, 1)
                    for h in range(H):
                        pe.matmul(bank(k, h)[:, cs], s[:, h, :], EG[:, h, cs], start=True, stop=False)
                pe.wait_ge(vr, c + 1)
                if c < C - 1:
                    for h in range(H):
                        mm = pe.matmul(bank(k, 5)[:, h * P:(h + 1) * P], Kbar[:, h, cs], vn[c % 2][:, h, :], start=True, stop=True)
                    mm.then_inc(df, 1)
                for h in range(H):
                    mm = pe.matmul(bank(k, h)[:, cs], vn[c % 2][:, h, :], attn[:, h, cs], start=(c == 0), stop=True)
            mm.then_inc(of, 1)
            for h in range(H):
                pe.wait_ge(o_sq, h + 1)
                pe.matmul(bank(k, 4 + h)[:, :], k.ones[:, :], osq[:, h, :], start=True, stop=True).then_inc(o_nf, 1)

        @block.vector
        def _(dve):
            L = lambda ins: k.dve_chain.link(dve, ins)
            for c in range(C):
                u = chunk(Vb)[:, :, c, :]
                if c == 0:
                    dve.tensor_copy(vn[0][:, :, :], u).then_inc(vr, 1)
                else:
                    dve.wait_ge(ws, c)
                    dve.tensor_tensor(vn[c % 2][:, :, :], u, bank(k, 4)[:, :].rearrange("p (h n) -> p h n", h=H), ALU.subtract)\
                        .then_inc(vr, 1)
                if c < C - 1:
                    dve.wait_ge(df, c + 1)
                    d = bank(k, 5)[:, :].rearrange("p (h n) -> p h n", h=H)
                    if c == 0:
                        dve.tensor_copy(S[0][:, :, :], d).then_inc(sr, 1)
                    else:
                        L(dve.tensor_tensor(S[c % 2][:, :, :], S[(c - 1) % 2][:, :, :],
                                            k.last_decay[:, :, c].unsqueeze(2).broadcast_to([P, H, P]), ALU.mult))
                        dve.tensor_tensor(S[c % 2][:, :, :], S[c % 2][:, :, :], d, ALU.add).then_inc(sr, 1)
            for h in range(H):
                dve.wait_ge(o_rd, h + 1)
                L(dve.scalar_tensor_tensor(o_sb[:, h, :], o_sb[:, h, :], k.vec(VEC_ROWS["w_gdn_norm_2"]), rstd[:, h, :],
                                           ALU.mult, ALU.mult))
                L(dve.tensor_tensor(k.catT[:, 2 + h, :], o_sb[:, h, :], k.zT[:, h, :], ALU.mult))

        @block.scalar
        def _(act):
            act.wait_ge(of, 1)
            for h in range(H):
                act.copy(o_sb[:, h, :], bank(k, h)[:, :]).then_inc(o_cp, 1)
                act.activation(osq[:, h, :], bank(k, h)[:, :], ACT.Square).then_inc(o_sq, 1)
            act.wait_ge(o_cp, 4)
            for h in range(H):
                act.wait_ge(o_nf, h + 1)
                k.act_chain.link(act, act.activation(rstd[:, h, :], bank(k, 4 + h)[:, :], ACT.Ln, bias=k.eps[:, 0:1], scale=1.0 / P))
            for h in range(H):
                act.activation(rstd[:, h, :], rstd[:, h, :], ACT.Exp, scale=-0.5).then_inc(o_rd, 1)


def stage_stick(k):
    z = [[k.carve(14720 + par * 2560 + off, (512 - j * P,)) for j, off in enumerate((0, 512, 896, 1152))] for par in range(2)]
    sp_ = [[k.carve(16000 + par * 2560 + off, (512 - j * P,)) for j, off in enumerate((0, 512, 896, 1152))] for par in range(2)]
    zf, zc, zl, spr, tf, wr, ar, am, of, oc = (k.sem(n) for n in (
        "stick_z", "stick_z_copied", "stick_logs", "stick_softplus", "stick_tail", "stick_exponent", "stick_exp", "stick_masked",
        "stick_full", "stick_out"))
    with k.nc.Block() as block:
        @block.tensor
        def _(pe):
            def scores(h):
                r = slice(h % 2 * 64, h % 2 * 64 + 64)
                for m, j in enumerate((3, 2, 1, 0)):
                    n = 4 * h + m
                    if n >= 2:
                        pe.wait_ge(spr, n - 1)
                    pe.matmul(bank(k, n % 2)[:, 0:512 - j * P], k.sbk[r, h // 2, j * P:(j + 1) * P], k.sbq[r, h // 2, j * P:512],
                              start=True, stop=True).then_inc(zf, 1)

            def tails(h):
                for m, j in enumerate((3, 2, 1, 0)):
                    n = 4 * h + m
                    pe.wait_ge(spr, n + 1)
                    if n >= 2:
                        pe.wait_ge(wr, n - 1)
                    b = bank(k, 2 + n % 2)
                    mm = pe.matmul(b[:, 0:512 - j * P], k.tril[:, :], sp_[h % 2][j], start=True, stop=(j == 3))
                    for jj in range(j + 1, 4):
                        mm = pe.matmul(b[:, (jj - j) * P:512 - j * P], k.ones[:, :], sp_[h % 2][jj], start=False, stop=(jj == 3))
                    mm.then_inc(tf, 1)

            def values(h):
                if h >= 2:
                    pe.wait_ge(oc, h - 1)
                pe.wait_ge(am, 4 * (h + 1))
                for j in range(4):
                    mm = pe.matmul(bank(k, 4 + h % 2)[:, j * P:512], k.sbv[:, j, (h // 2) * P:(h // 2 + 1) * P], z[h % 2][j],
                                   start=(j == 0), stop=(j == 3))
                mm.then_inc(of, 1)

            scores(0)
            for h in range(4):
                if h < 3:
                    scores(h + 1)
                tails(h)
                values(h)

        @block.scalar
        def _(act):
            L = lambda ins: k.act_chain.link(act, ins)

            def logs(h):
                if h >= 2:
                    act.wait_ge(of, h - 1)
                for m, j in enumerate((3, 2, 1, 0)):
                    n = 4 * h + m
                    act.wait_ge(zf, n + 1)
                    src, s = bank(k, n % 2)[:, 0:512 - j * P], sp_[h % 2][j]
                    act.copy(z[h % 2][j], src).then_inc(zc, 1)
                    L(act.activation(s, src, ACT.Abs))
                    L(act.activation(s, s, ACT.Exp, scale=-1.0))
                    act.activation(s, s, ACT.Ln, bias=1.0).then_inc(zl, 1)

            logs(0)
            for h in range(4):
                if h < 3:
                    logs(h + 1)
                for m, j in enumerate((3, 2, 1, 0)):
                    act.wait_ge(wr, 4 * h + m + 1)
                    act.activation(z[h % 2][j], z[h % 2][j], ACT.Exp).then_inc(ar, 1)
                act.wait_ge(of, h + 1)
                r = slice(h % 2 * 64, h % 2 * 64 + 64)
                act.copy(k.catT[r, 6 + h // 2, :], bank(k, 4 + h % 2)[r, :]).then_inc(oc, 1)

        @block.vector
        def _(dve):
            L = lambda ins: k.dve_chain.link(dve, ins)

            def softplus(h):
                for m, j in enumerate((3, 2, 1, 0)):
                    n = 4 * h + m
                    dve.wait_ge(zl, n + 1)
                    s = sp_[h % 2][j]
                    L(dve.scalar_tensor_tensor(s, bank(k, n % 2)[:, 0:512 - j * P], 0.0, s, ALU.max, ALU.add))
                    dve.tensor_tensor(s[:, 0:P], s[:, 0:P], k.triu_strict[:, :], ALU.mult).then_inc(spr, 1)

            def exponents(h):
                for m, j in enumerate((3, 2, 1, 0)):
                    n = 4 * h + m
                    dve.wait_ge(tf, n + 1)
                    dve.wait_ge(zc, n + 1)
                    w = z[h % 2][j]
                    L(dve.tensor_tensor(w, w, bank(k, 2 + n % 2)[:, 0:512 - j * P], ALU.subtract))
                    dve.tensor_scalar(w[:, 0:P], w[:, 0:P], 0.0, None, ALU.min).then_inc(wr, 1)

            def mask(h):
                for m, j in enumerate((3, 2, 1, 0)):
                    dve.wait_ge(ar, 4 * h + m + 1)
                    w = z[h % 2][j][:, 0:P]
                    dve.tensor_tensor(w, w, k.triu_strict[:, :], ALU.mult).then_inc(am, 1)

            softplus(0)
            for h in range(4):
                if h < 3:
                    softplus(h + 1)
                exponents(h)
                mask(h)


def stage_final(k, out):
    rows = k.carve(0, (4, 1024))
    turned, copied, stored = k.sem("final_turned"), k.sem("final_copied"), k.sem("final_stored")
    with k.nc.Block() as block:
        @block.scalar
        def _(act):
            act_squares(k, act, lambda kk: k.xT[:, kk, :], 512)
            act_rstd(k, act, 512)
            for n in range(8):
                act.wait_ge(turned, n + 1)
                act.copy(rows[:, n // 2, (n % 2) * 512:(n % 2 + 1) * 512], bank(k, n)[:, :]).then_inc(copied, 1)

        @block.vector
        def _(dve):
            dve.wait_ge(k.rstd_ready.sem, k.rstd_ready.at(1))
            dve_norm(k, dve, lambda kk: k.hT[:, kk, :], lambda kk: k.xT[:, kk, :], VEC_ROWS["w_norm_final_2"], 512)

        @block.tensor
        def _(pe):
            pe_norm_sums(k, pe, 512)
            for n in range(8):
                pe.wait_ge(k.h_ready.sem, k.h_ready.at(4 * (n % 2 + 1)))
                for m in range(4):
                    kk = (n % 2) * 4 + m
                    mm = pe.transpose(bank(k, n)[:, m * P:(m + 1) * P], k.hT[:, kk, (n // 2) * P:(n // 2 + 1) * P], k.ident[:, :])
                mm.then_inc(turned, 1)

        @block.sync
        def _(sp):
            for n in range(8):
                sp.wait_ge(copied, n + 1)
                half = slice((n % 2) * 512, (n % 2 + 1) * 512)
                sp.dma_start(out[0, (n // 2) * P:(n // 2 + 1) * P, half], rows[:, n // 2, half]).then_inc(stored, 16)
            sp.wait_ge(stored, 128)


ARENA = 33000


def make_plan(k, a, plan):
    for l in range(2):
        for cols in (0, 512):
            plan(chunks_of(k, a["w_mem_kv"][l], cols))
    for cols in (0, 512, 1024, 1552):
        plan(chunks_of(k, a["a_w_in"][0], cols))
    for cols in (0, 512):
        plan(chunks_of(k, a["a_w_out"][0], cols))
    plan(ffn_chunks(k, a["w_up"][0], a["w_down"][0]))
    plan(kv_chunks(k, a["w_kv"]), 8)
    plan(chunks_of(k, a["w_kv"], 256))
    plan(chunks_of(k, a["w_ck1"], 0, 256, 8))
    plan(chunks_of(k, a["w_cv1"], 0, 256, 8))
    plan(paired_query_chunks(k, a["b_w_in"][0]), 8)
    plan(chunks_of(k, a["b_w_in"][0], 536))
    for cols in (0, 512):
        plan(paired_out_chunks(k, a["b_w_out"][0], cols))
    plan(ffn_chunks(k, a["w_up"][1], a["w_down"][1]))
    w = a["w_mix_in_2"][0]
    plan(chunks_of(k, w, 0))
    plan(mixed_chunks(k, w, (512, 3336)))
    for cols in (768, 1280, 1792, 2304, 2824):
        plan(chunks_of(k, w, cols))
    for cols in (0, 512):
        plan(chunks_of(k, a["w_mix_out_2"][0], cols))
    plan(ffn_chunks(k, a["w_ffn_up_2"][0], a["w_ffn_down_2"][0]))


def program(k, a, out):
    conv = lambda name: (lambda j: VEC_ROWS[name] + j * FT)
    return [
        lambda: stage_setup(k, a),
        lambda: stage_memory(k, a),
        lambda: stage_gla_in(k, a),
        lambda: stage_gla(k, a),
        lambda: stage_mem_attention(k, 0, lambda h: k.catT[:, 4 + h, :]),
        lambda: stage_out_projection(k),
        lambda: stage_ffn(k, a["w_up"][0], a["w_down"][0], VEC_ROWS["g_ffn0"], conv("conv_w0"), VEC_ROWS["conv_b0"], False),
        lambda: stage_nsa_in(k, a),
        lambda: stage_nsa(k),
        lambda: stage_mem_attention(k, 1, lambda h: k.catT[:, 4 + h, :]),
        lambda: stage_out_projection(k),
        lambda: stage_ffn(k, a["w_up"][1], a["w_down"][1], VEC_ROWS["g_ffn1"], conv("conv_w1"), VEC_ROWS["conv_b1"], False),
        lambda: stage_mix_in(k, a),
        lambda: stage_delta(k, a),
        lambda: stage_stick(k),
        lambda: stage_out_projection(k),
        lambda: stage_ffn(k, a["w_ffn_up_2"][0], a["w_ffn_down_2"][0], VEC_ROWS["w_norm_ffn_2"],
                          lambda j: VEC_ROWS[f"ffn_conv2_{j}"], None, True),
        lambda: stage_final(k, out),
    ]


def build(nc, a, out, until=99, debug=None):
    k = K()
    k.nc = nc
    ctx = ExitStack()
    with ctx:
        def sb(name, shape):
            return ctx.enter_context(nc.sbuf_tensor(name, shape, F32))

        k.sem = lambda name: ctx.enter_context(nc.semaphore(name))
        k.xT, k.hT = sb("xT", [P, 8, 512]), sb("hT", [P, 8, 512])
        k.slots = [sb(f"weights{i}", [P, SLOT]) for i in range(RING)]
        k.vecs = sb("vecs", [P, VEC_TILES * P])
        k.ident, k.ones, k.triu, k.triu_strict = (sb(n, [P, P]) for n in ("ident", "ones", "triu", "triu_strict"))
        k.tril = sb("tril", [P, P])
        k.level = sb("level", [P, 7, P])
        k.eps, k.valid = sb("eps", [P, 1]), sb("valid", [P, 1])
        k.rstd = sb("rstd", [P, 512])
        k.dist, k.dist_cmp = sb("dist", [P, 512]), sb("dist_cmp", [P, 4 * 31])
        k.arena = sb("arena", [P, ARENA])
        k.psum = [ctx.enter_context(nc.psum_tensor(f"bank{i}", [P, 512], F32)) for i in range(8)]
        k.vec = lambda c: k.vecs[:, c:c + 1]

        def carve(at, shape):
            n = 1
            for s in shape:
                n *= s
            assert at + n <= ARENA, (at, shape)
            ap = k.arena[:, at:at + n]
            if len(shape) == 2:
                return ap.rearrange("p (a b) -> p a b", a=shape[0])
            if len(shape) == 3:
                return ap.rearrange("p (a b c) -> p a b c", a=shape[0], b=shape[1])
            return ap

        k.carve = carve
        k.sq = carve(ARENA - 8192, (8, 512))
        k.mkT = carve(ARENA - 4096, (2, 4, 256))
        k.mv = carve(ARENA - 2048, (2, 2, 512))
        k.memT = carve(9216, (8, 256))
        k.catT = k.hT
        k.ma = 8832
        signals = {name: Signal(k.sem(name)) for name in
                   ("tile_full", "tile_free", "sq_ready", "sums_full", "rstd_ready", "h_ready")}
        k.tile_full, k.tile_free = signals["tile_full"], signals["tile_free"]
        k.sq_ready, k.sums_full = signals["sq_ready"], signals["sums_full"]
        k.rstd_ready, k.h_ready = signals["rstd_ready"], signals["h_ready"]
        k.ma_sig = [Signal(k.sem("mem_" + n)) for n in ("scores", "lows", "exps", "probs", "turned", "turned_out", "full", "out")]
        k.ffn_sig = [Signal(k.sem("ffn_" + n)) for n in ("padded", "conv_a", "conv_b", "silu", "done", "cleared")]

        def advance(**counts):
            for name, n in counts.items():
                signals[name].base += n

        k.advance = advance
        k.dve_chain, k.act_chain, k.pool_chain = (Chain(k.sem(n)) for n in ("vector_order", "scalar_order", "pool_order"))
        k.plan = []
        loads = []

        def plan(chunks, n=BATCH_LOADS):
            k.plan.extend(chunks)
            loads.extend([n] * len(chunks))

        make_plan(k, a, plan)
        k.ring = Ring([k.sem(f"weights_in{i}") for i in range(RING)], k.sem("weights_used"), loads)
        stages = program(k, a, out)
        for n, stage in enumerate(stages):
            if n >= until:
                break
            stage()
        if debug:
            debug(k, ctx)


_INS = ['x', 'mem', 'g_mix', 'g_ffn', 'g_mem', 'w_mem_kv', 'w_up', 'conv_w', 'conv_b', 'w_down', 'a_w_in', 'a_w_alpha',
        'a_b_alpha', 'a_g_head', 'a_w_out', 'g_kv', 'w_kv', 'pe_k', 'pe_v', 'w_ck1', 'w_ck2', 'w_cv1', 'w_cv2', 'b_w_in',
        'b_w_out', 'g_final', 'w_norm_mix_2', 'w_mix_in_2', 'w_sconv_2', 'w_gdn_conv_2', 'gdn_a_log_2', 'gdn_dt_bias_2',
        'w_gdn_norm_2', 'w_mix_out_2', 'w_norm_ffn_2', 'w_ffn_up_2', 'w_ffn_conv_2', 'w_ffn_down_2', 'w_norm_final_2']
_OUT = ((1, 512, 1024), 'float32')


def kernel(**inputs):
    import numpy as _np
    import concourse.bacc as _bacc
    from concourse import mybir as _mybir
    from concourse.bass_utils import run_bass_kernel_spmd as _run

    nc = _bacc.Bacc("TRN2", target_bir_lowering=False, num_devices=1)
    arrays, args = {}, {}
    for name in _INS:
        v = _np.ascontiguousarray(inputs[name])
        arrays[f"in_{name}"] = v
        args[name] = nc.dram_tensor(f"in_{name}", v.shape, _mybir.dt.from_np(v.dtype), kind="ExternalInput").ap()
    out = nc.dram_tensor("out", _OUT[0], _mybir.dt.from_np(_np.dtype(_OUT[1])), kind="ExternalOutput").ap()
    build(nc, args, out)
    r = _run(nc, [arrays], core_ids=[0])
    return r.results[0]["out"]
```

```python
from contextlib import ExitStack

import concourse.bass as bass
from concourse import mybir

F32 = mybir.dt.float32
F32R = mybir.dt.float32r
I32 = mybir.dt.int32
ALU = mybir.AluOpType
ACT = mybir.ActivationFunctionType
AX = mybir.AxisListType

P = 128
RING = 4
SLOT = 1024
BIG = 1e30


class Signal:

    def __init__(self, sem):
        self.sem = sem
        self.base = 0

    def at(self, n):
        return self.base + n


class Chain:

    def __init__(self, sem):
        self.sem = sem
        self.n = 0
        self.reg = None
        self.per = 0

    def link(self, eng, ins):
        self.n += 1
        ins.then_inc(self.sem, 1)
        eng.wait_ge(self.sem, self.n if self.reg is None else self.n + self.reg * self.per)


class Ring:

    def __init__(self, landed, hi, lo, used, loads):
        self.landed = landed
        self.hi = hi
        self.lo = lo
        self.used = used
        self.loads = loads
        self.out = 0
        self.hi_at = 0
        self.lo_at = 0
        self.took = 0
        self.owed = 0

    def full(self, n):
        return 16 * sum(self.loads[m] for m in range(n % RING, n + 1, RING))


class K:
    pass


def bank(k, i):
    return k.psum[i % 8]


def plus(count, reg, per):
    return count if reg is None else reg * per + count


def load_chunk(k, sp, n, pieces, reg=None, per=8):
    r = k.ring
    if n >= RING:
        sp.wait_ge(r.lo, plus(n - RING + 1, reg, per))
    for dst, src in pieces:
        sp.dma_start(dst, src).then_inc(r.landed[n % RING], 16)


def raw_slot(k, n, kt, cols):
    return k.raw[n % RING][:, :].rearrange("p (k n) -> p k n", k=kt)


def parts(k, n, kt):
    return [w[n % RING][:, :].rearrange("p (k n) -> p k n", k=kt) for w in (k.w_hi, k.w_lo)]


def chunks_of(k, w, cols, width=512, kt=2):
    wv = w.rearrange("(k p) n -> p k n", p=P)
    return [lambda n, k0=k0: [(raw_slot(k, n, kt, width)[:, :, :], wv[:, k0:k0 + kt, cols:cols + width])]
            for k0 in range(0, w.shape[0] // P, kt)]


def stream(k, sp, upto):
    end = min(upto + RING, k.phase_end)
    while k.ring.out < end:
        n = k.ring.out
        load_chunk(k, sp, n, k.plan[n](n))
        k.ring.out += 1


def split_hi_chunk(k, act, n, reg=None, loads=2, per=8):
    r = k.ring
    act.wait_ge(r.landed[n % RING], plus(r.full(n), reg, 16 * loads * per // RING))
    if n >= RING:
        act.wait_ge(r.used, plus(n - RING + 1, reg, per))
    act.copy(k.w_hi[n % RING][:, :], k.raw[n % RING][:, :]).then_inc(r.hi, 1)


def split_lo_chunk(k, dve, n, reg=None, per=8):
    r = k.ring
    dve.wait_ge(r.hi, plus(n + 1, reg, per))
    dve.tensor_tensor(k.w_lo[n % RING][:, :], k.raw[n % RING][:, :], k.w_hi[n % RING][:, :].bitcast(F32), ALU.subtract)\
        .then_inc(r.lo, 1)


def split_hi(k, act, upto):
    while k.ring.hi_at < min(upto, k.phase_end):
        split_hi_chunk(k, act, k.ring.hi_at)
        k.ring.hi_at += 1


def split_lo(k, dve, upto):
    while k.ring.lo_at < min(upto, k.phase_end):
        split_lo_chunk(k, dve, k.ring.lo_at)
        k.ring.lo_at += 1


def pe_used(k, pe):
    if k.ring.owed:
        pe.drain().then_inc(k.ring.used, 1)
        k.ring.owed = 0


def pe_three(k, pe, out, stat, mov, first, last):
    (sh, sl), (mh, ml) = stat, mov
    a = pe.matmul(out, sh, mh, start=first, stop=False)
    pe.matmul(out, sh, ml, start=False, stop=False)
    c = pe.matmul(out, sl, mh, start=False, stop=last)
    return a, c


def pe_chunk(k, pe, n, tiles, rows, total, reg=None, per=8, before=None):
    pe.wait_ge(k.ring.lo, plus(n + 1, reg, per))
    w = parts(k, n, len(rows))
    for r, kk in enumerate(rows):
        for i, (out, operands) in enumerate(tiles):
            if before is not None:
                before(i, kk)
            stat, mov = operands(kk, [x[:, r, :] for x in w])
            a, c = pe_three(k, pe, out, stat, mov, kk == 0, kk == total - 1)
            if r == 0 and i == 0 and k.ring.owed:
                a.then_inc(k.ring.used, 1)
            if kk == total - 1:
                c.then_inc(k.tile_full.sem, 1)
    k.ring.owed = 1


def pe_group(k, pe, t, tiles, h_from=None):
    def before(i, kk):
        if kk == 0 and t + i >= 8:
            pe.wait_ge(k.tile_free.sem, k.tile_free.at(t + i - 7))
        if h_from is not None and i == 0:
            pe.wait_ge(k.h_ready.sem, k.h_ready.at(h_from + kk + 1))

    outs = [(out(bank(k, t + i)), operands) for i, (out, operands) in enumerate(tiles)]
    for c in range(4):
        n = k.ring.took
        k.ring.took += 1
        pe_chunk(k, pe, n, outs, [2 * c, 2 * c + 1], 8, before=before)
    return t + len(tiles)


def feature_tile(k, c0, tokens=slice(0, 512)):
    n = tokens.stop - tokens.start
    return (lambda b: b[:, 0:n],
            lambda kk, w: ([x[:, c0:c0 + P] for x in w], [k.h_hi[:, kk, tokens], k.h_lo[:, kk, tokens]]))


def token_tile(k, tt, view, width, at=0):
    ts = slice(at + tt * P, at + (tt + 1) * P)
    return (lambda b: b[:, 0:width],
            lambda kk, w: ([k.h_hi[:, kk, ts], k.h_lo[:, kk, ts]], [view(x) for x in w]))


def act_squares(k, act, src, n):
    for kk in range(8):
        act.activation(k.sq[:, kk, 0:n], src(kk), ACT.Square).then_inc(k.sq_ready.sem, 1)


def pe_norm_sums(k, pe, n, b=7):
    for kk in range(8):
        pe.wait_ge(k.sq_ready.sem, k.sq_ready.at(kk + 1))
        mm = pe.matmul(bank(k, b)[:, 0:n], k.ones[:, :], k.sq[:, kk, 0:n], start=(kk == 0), stop=(kk == 7))
    mm.then_inc(k.sums_full.sem, 1)


def act_rstd(k, act, n, b=7, dim=1024):
    act.wait_ge(k.sums_full.sem, k.sums_full.at(1))
    k.act_chain.link(act, act.activation(k.rstd[:, 0:n], bank(k, b)[:, 0:n], ACT.Ln, bias=k.eps[:, 0:1], scale=1.0 / dim))
    act.activation(k.rstd[:, 0:n], k.rstd[:, 0:n], ACT.Exp, scale=-0.5).then_inc(k.rstd_ready.sem, 1)


def dve_normed(k, dve, dst, src, gain, n):
    for kk in range(8):
        dve.scalar_tensor_tensor(dst(kk), src(kk), k.vec(gain + kk), k.rstd[:, 0:n], ALU.mult, ALU.mult)\
            .then_inc(k.normed.sem, 1)


def act_split(k, act, value, at, tokens=slice(0, 512), tiles=range(8)):
    for i, kk in enumerate(tiles):
        if at is not None:
            act.wait_ge(k.normed.sem, k.normed.at(at + i + 1))
        act.copy(k.h_hi[:, kk, tokens], value(kk)).then_inc(k.h_rounded.sem, 1)


def dve_split(k, dve, value, at=0, tokens=slice(0, 512), tiles=range(8)):
    for i, kk in enumerate(tiles):
        dve.wait_ge(k.h_rounded.sem, k.h_rounded.at(at + i + 1))
        dve.tensor_tensor(k.h_lo[:, kk, tokens], value(kk), k.h_hi[:, kk, tokens].bitcast(F32), ALU.subtract)\
            .then_inc(k.h_ready.sem, 1)


def act_norm(k, act):
    act_squares(k, act, lambda kk: k.xT[:, kk, :], 512)
    act_rstd(k, act, 512)
    act_split(k, act, lambda kk: k.sq[:, kk, :], 0)


def dve_norm(k, dve, gain):
    dve.wait_ge(k.rstd_ready.sem, k.rstd_ready.at(1))
    dve_normed(k, dve, lambda kk: k.sq[:, kk, :], lambda kk: k.xT[:, kk, :], gain, 512)
    dve_split(k, dve, lambda kk: k.sq[:, kk, :])


NORM = dict(sq_ready=8, sums_full=1, rstd_ready=1, normed=8, h_rounded=8, h_ready=8)


def act_groups(k, act, first, sizes, read_out):
    t = 0
    for g, size in enumerate(sizes):
        split_hi(k, act, first + 4 * g + 7)
        for _ in range(size):
            act.wait_ge(k.tile_full.sem, k.tile_full.at(t + 1))
            read_out(t, bank(k, t))
            t += 1
        split_hi(k, act, first + 4 * g + 8)
    return t


def dve_groups(k, dve, first, groups, each=None):
    for g in range(groups):
        split_lo(k, dve, first + 4 * g + 8)
        if each is not None:
            each(g)


VEC_ROWS = {}


def vector_tiles(a):
    rows = []

    def put(name, tile, at, src):
        rows.append((tile, at, src))
        VEC_ROWS[name] = tile * P + at
        return at + src.shape[0]

    r = lambda v: v.rearrange("(n p) -> n p", p=P)
    at = 0
    for l in range(2):
        at = put(f"g_mix{l}", 0, at, r(a["g_mix"][l]))
        at = put(f"g_ffn{l}", 0, at, r(a["g_ffn"][l]))
        at = put(f"g_mem{l}", 0, at, r(a["g_mem"][l]))
    for name in ("g_kv", "g_final"):
        at = put(name, 0, at, r(a[name]))
    at = put("w_norm_mix_2", 0, at, r(a["w_norm_mix_2"][0]))
    at = put("w_norm_ffn_2", 0, at, r(a["w_norm_ffn_2"][0]))
    at = put("w_norm_final_2", 0, at, r(a["w_norm_final_2"]))
    at = put("a_g_head", 0, at, r(a["a_g_head"][0]))
    at = put("w_gdn_norm_2", 0, at, r(a["w_gdn_norm_2"][0]))
    conv = a["conv_w"].rearrange("l j (n p) -> l (j n) p", p=P)
    at = put("conv_w0", 1, 0, conv[0])
    at = put("conv_b0", 1, at, r(a["conv_b"][0]))
    at = put("conv_b1", 1, at, r(a["conv_b"][1]))
    at = put("conv_w1", 2, 0, conv[1])
    at = put("w_sconv_2", 2, at, a["w_sconv_2"][0].rearrange("j (n p) -> (j n) p", p=P))
    at = put("w_gdn_conv_2", 2, at, a["w_gdn_conv_2"][0].rearrange("j (n p) -> (j n) p", p=P))
    fc = a["w_ffn_conv_2"][0].rearrange("j (n p) -> j n p", p=P)
    at = put("ffn_conv2_0", 3, 0, fc[0])
    at = put("ffn_conv2_1", 3, at, fc[1])
    at = put("ffn_conv2_2", 4, 0, fc[2])
    at = put("pe_k", 4, at, a["pe_k"].rearrange("(j q) d -> j (q d)", q=2))
    at = put("pe_v", 4, at, a["pe_v"].rearrange("(j q) d -> j (q d)", q=2))
    return rows


VEC_TILES = 5


def stage_setup(k, a):
    rows = vector_tiles(a)
    x_rows = k.carve(0, (4, 1024))
    mem_rows = k.carve(4096, (2, 1024))
    v_rows = k.carve(6144, (VEC_TILES, P))
    iota_f = k.carve(7168, (512,)).bitcast(I32)
    iota_c = k.carve(7680, (4 * 31,)).bitcast(I32)
    ip = k.carve(7808, (P,)).bitcast(I32)
    ic = k.carve(7936, (P,)).bitcast(I32)
    xo = k.carve(8064, (P,)).bitcast(I32)
    sh = k.carve(8192, (7 * P,)).bitcast(I32)
    x_in, mem_in, v_in = k.sem("x_in"), k.sem("mem_in"), k.sem("vectors_in")
    rows_clear, consts, iotas = k.sem("rows_clear"), k.sem("constants"), k.sem("iotas")
    turned, out = k.sem("turned"), k.sem("turned_out")
    jobs = [("x", tt, m) for m in range(8) for tt in range(4)] + [("mem", tt, m) for m in range(8) for tt in range(2)]

    with k.nc.Block() as block:
        @block.sync
        def _(sp):
            for tt in range(4):
                sp.dma_start(x_rows[:, tt, :], a["x"][0, tt * P:(tt + 1) * P, :]).then_inc(x_in, 16)
            for tt in range(2):
                sp.dma_start(mem_rows[:, tt, :], a["mem"][0, tt * P:(tt + 1) * P, :]).then_inc(mem_in, 16)
            stream(k, sp, 0)

        @block.scalar
        def _(act):
            act.wait_ge(rows_clear, 1)
            for tile, at, src in rows:
                act.dma_start(v_rows[at:at + src.shape[0], tile, :], src).then_inc(v_in, 16)

        @block.gpsimd
        def _(pool):
            k.pool_chain.link(pool, pool.memset(k.ones[:, :], 1.0))
            k.pool_chain.link(pool, pool.affine_select(k.triu[:, :], k.ones[:, :], [[1, P]], ALU.is_ge, 0.0,
                                                       base=0, channel_multiplier=-1))
            k.pool_chain.link(pool, pool.affine_select(k.ident[:, :], k.triu[:, :], [[1, P]], ALU.is_equal, 0.0,
                                                       base=0, channel_multiplier=-1))
            pool.affine_select(k.triu_strict[:, :], k.triu[:, :], [[1, P]], ALU.not_equal, 0.0,
                               base=0, channel_multiplier=-1).then_inc(consts, 1)
            k.pool_chain.link(pool, pool.affine_select(k.tril[:, :], k.ones[:, :], [[-1, P]], ALU.is_ge, 0.0,
                                                       base=0, channel_multiplier=1))
            pool.iota(iota_f, [[-1, 512]], base=384, channel_multiplier=1).then_inc(iotas, 1)
            pool.iota(iota_c, [[P, 4], [-16, 31]], base=-31, channel_multiplier=1).then_inc(iotas, 1)
            pool.iota(ip, [[0, P]], base=0, channel_multiplier=1).then_inc(iotas, 1)
            pool.iota(ic, [[1, P]], base=0, channel_multiplier=0).then_inc(iotas, 1)

        @block.vector
        def _(dve):
            L = lambda ins: k.dve_chain.link(dve, ins)
            dve.memset(v_rows[:, :, :], 0.0).then_inc(rows_clear, 1)
            L(dve.memset(k.eps[:, :], 1e-6))
            dve.wait_ge(iotas, 4)
            dve.wait_ge(consts, 1)
            L(dve.tensor_copy(k.dist[:, :], iota_f))
            L(dve.tensor_copy(k.dist_cmp[:, :], iota_c))
            L(dve.tensor_scalar(k.valid[:, :], k.dist_cmp[:, 0:1], 0.0, None, ALU.is_ge))
            L(dve.tensor_tensor(xo, ip, ic, ALU.bitwise_xor))
            for lg in range(7):
                piece = sh[:, lg * P:(lg + 1) * P]
                L(dve.tensor_scalar(piece, xo, lg, None, ALU.logical_shift_right))
                L(dve.scalar_tensor_tensor(k.level[:, lg, :], piece, 1.0, k.triu[:, :], ALU.is_equal, ALU.mult))
            for n, (what, tt, m) in enumerate(jobs):
                dve.wait_ge(turned, n + 1)
                dst = k.xT[:, m, tt * P:(tt + 1) * P] if what == "x" else k.memT[:, m, tt * P:(tt + 1) * P]
                dve.tensor_copy(dst, bank(k, n)[:, 0:P]).then_inc(out, 1)
            for t in range(VEC_TILES):
                dve.wait_ge(turned, len(jobs) + t + 1)
                dve.tensor_copy(k.vecs[:, t * P:(t + 1) * P], bank(k, len(jobs) + t)[:, 0:P]).then_inc(out, 1)

        @block.tensor
        def _(pe):
            pe.wait_ge(consts, 1)
            pe.wait_ge(x_in, 64)
            for n, (what, tt, m) in enumerate(jobs):
                if n == 32:
                    pe.wait_ge(mem_in, 32)
                if n >= 8:
                    pe.wait_ge(out, n - 7)
                src = (x_rows if what == "x" else mem_rows)[:, tt, m * P:(m + 1) * P]
                pe.transpose(bank(k, n)[:, 0:P], src, k.ident[:, :]).then_inc(turned, 1)
            pe.wait_ge(v_in, 16 * len(rows))
            for t in range(VEC_TILES):
                n = len(jobs) + t
                pe.wait_ge(out, n - 7)
                pe.transpose(bank(k, n)[:, 0:P], v_rows[:, t, :], k.ident[:, :]).then_inc(turned, 1)

    masked = k.sem("masked")
    with k.nc.Block() as block:
        @block.gpsimd
        def _(pool):
            pool.affine_select(k.dist[:, :], k.dist[:, :], [[-1, 512]], ALU.is_ge, BIG, base=384,
                               channel_multiplier=1).then_inc(masked, 1)
            pool.affine_select(k.dist_cmp[:, :], k.dist_cmp[:, :], [[P, 4], [-16, 31]], ALU.is_ge, BIG, base=-31,
                               channel_multiplier=1).then_inc(masked, 1)
            pool.wait_ge(masked, 2)


def stage_memory(k, a):
    M = 256
    first = k.ring.took
    cols = [slice(0, M), slice(M, 2 * M)]
    value = [lambda kk: k.sq[:, kk, M:2 * M], lambda kk: k.sq[:, kk, 0:M]]
    sizes = [4, 2, 4, 2]
    with k.nc.Block() as block:
        @block.sync
        def _(sp):
            stream(k, sp, first + 16)

        @block.scalar
        def _(act):
            act_squares(k, act, lambda kk: k.memT[:, kk, :], M)
            split_hi(k, act, first + 4)
            act_rstd(k, act, M)
            for l in range(2):
                act_split(k, act, value[l], 8 * l, cols[l])

            def read_out(t, src):
                l, m = divmod(t, 6)
                dst = k.mkT[:, l, m, :] if m < 4 else k.mv[:, l, m - 4, :]
                act.copy(dst, src[:, 0:M if m < 4 else 512]).then_inc(k.tile_free.sem, 1)

            act_groups(k, act, first, sizes, read_out)

        @block.vector
        def _(dve):
            split_lo(k, dve, first + 4)
            dve.wait_ge(k.rstd_ready.sem, k.rstd_ready.at(1))
            for l in range(2):
                dve_normed(k, dve, value[l], lambda kk: k.memT[:, kk, :], VEC_ROWS[f"g_mem{l}"], M)
                dve_split(k, dve, value[l], 8 * l, cols[l])
            dve_groups(k, dve, first, 4)

        @block.tensor
        def _(pe):
            pe_norm_sums(k, pe, M)
            t = 0
            for l in range(2):
                pe.wait_ge(k.h_ready.sem, k.h_ready.at(8 * (l + 1)))
                t = pe_group(k, pe, t, [feature_tile(k, m * P, cols[l]) for m in range(4)])
                t = pe_group(k, pe, t, [token_tile(k, tt, lambda w: w[:, :], 512, l * M) for tt in range(2)])
            pe_used(k, pe)
    k.advance(sq_ready=8, sums_full=1, rstd_ready=1, normed=16, h_rounded=16, h_ready=16, tile_full=12, tile_free=12)


def small_weights(k, name, kt, n, pad=0):
    raw = k.scope(f"{name}_raw", [P, kt, n], F32)
    return raw, k.scope(f"{name}_hi", [P, kt, max(n, pad)], F32R), k.scope(f"{name}_lo", [P, kt, max(n, pad)], F32R)


def stage_gla_in(k, a):
    k.qT, k.kT = k.carve(0, (2, 512)), k.carve(1024, (2, 512))
    k.v = k.carve(2048, (4, 512))
    k.rT = k.carve(4096, (4, 512))
    k.mqT = k.carve(6144, (4, 512))
    k.alrT = k.carve(8192, (512,))
    w_alr, alr_hi, alr_lo = small_weights(k, "w_alr", 8, 16, P)
    alr_in, ones_row, alr_split = k.sem("alr_in"), k.sem("ones_row"), k.sem("alr_split")
    first = k.ring.took
    with k.nc.Block() as block:
        @block.sync
        def _(sp):
            sp.dma_start(w_alr[:, :, :], a["a_w_in"][0].rearrange("(k p) n -> p k n", p=P)[:, :, 1536:1552]).then_inc(alr_in, 16)
            stream(k, sp, first + 16)

        @block.gpsimd
        def _(pool):
            pool.memset(k.alrT[0:32, :], 1.0).then_inc(ones_row, 1)
            for part in (alr_hi, alr_lo):
                pool.memset(part[:, :, :].bitcast(F32), 0.0).then_inc(ones_row, 1)

        @block.scalar
        def _(act):
            act_norm(k, act)
            act.wait_ge(alr_in, 16)
            act.wait_ge(ones_row, 3)
            act.copy(alr_hi[:, :, 0:16], w_alr[:, :, :]).then_inc(alr_split, 1)

            def read_out(t, src):
                if t < 2:
                    ins = act.mul(k.qT[:, t, :], src[:, :], 64 ** -0.5)
                elif t < 4:
                    ins = act.copy(k.kT[:, t - 2, :], src[:, :])
                elif t < 8:
                    ins = act.copy(k.v[:, t - 4, :], src[:, :])
                elif t < 12:
                    ins = act.activation(k.rT[:, t - 8, :], src[:, :], ACT.Silu)
                elif t < 16:
                    ins = act.mul(k.mqT[:, t - 12, :], src[:, :], -(128 ** -0.5))
                else:
                    ins = act.copy(k.alrT[0:16, :], src[0:16, :])
                ins.then_inc(k.tile_free.sem, 1)

            t = act_groups(k, act, first, [4] * 4, read_out)
            act.wait_ge(k.tile_full.sem, k.tile_full.at(t + 1))
            read_out(t, bank(k, t))

        @block.vector
        def _(dve):
            dve_norm(k, dve, VEC_ROWS["g_mix0"])
            dve.wait_ge(alr_split, 1)
            dve.tensor_tensor(alr_lo[:, :, 0:16], w_alr[:, :, :], alr_hi[:, :, 0:16].bitcast(F32), ALU.subtract)\
                .then_inc(alr_split, 1)
            dve_groups(k, dve, first, 4)

        @block.tensor
        def _(pe):
            pe_norm_sums(k, pe, 512)
            t = 0
            for group in range(4):
                if group == 1:
                    tiles = [token_tile(k, tt, lambda w: w[:, :], 512) for tt in range(4)]
                else:
                    tiles = [feature_tile(k, m * P) for m in range(4)]
                t = pe_group(k, pe, t, tiles, 0 if group == 0 else None)
            pe_used(k, pe)
            pe.wait_ge(alr_split, 2)
            pe.wait_ge(k.tile_free.sem, k.tile_free.at(t - 7))
            for kk in range(8):
                _, mm = pe_three(k, pe, bank(k, t)[:, :], (alr_hi[:, kk, :], alr_lo[:, kk, :]),
                                 (k.h_hi[:, kk, :], k.h_lo[:, kk, :]), kk == 0, kk == 7)
            mm.then_inc(k.tile_full.sem, 1)
    k.advance(**NORM, tile_full=17, tile_free=17)


def stage_mem_attention(k, layer):
    prob = [k.scr(k.ma + i * 1024, (4, 256)) for i in range(2)]
    probT = [k.scr(k.ma + 2048 + i * 1024, (2, 512)) for i in range(2)]
    low, tot, inv = (k.scr(k.ma + 4096 + i * 16, (4, 4)) for i in range(3))
    z_full, low_ready, e_ready, p_ready, t_full, t_out, o_full, o_out = k.ma_sig
    with k.nc.Block() as block:
        @block.tensor
        def _(pe):
            def scores(h):
                if h >= 1:
                    pe.wait_ge(e_ready.sem, e_ready.at(4 * h))
                for tt in range(4):
                    mm = pe.matmul(bank(k, tt // 2)[:, (tt % 2) * 256:(tt % 2) * 256 + 256],
                                   k.mqT[:, h, tt * P:(tt + 1) * P], k.mkT[:, layer, h, :], start=True, stop=True)
                mm.then_inc(z_full.sem, 1)

            scores(0)
            for h in range(4):
                if h < 3:
                    scores(h + 1)
                pe.wait_ge(p_ready.sem, p_ready.at(h + 1))
                if h >= 1:
                    pe.wait_ge(t_out.sem, t_out.at(2 * h))
                for mt in range(2):
                    for tt in range(4):
                        mm = pe.transpose(bank(k, 2 + mt)[:, tt * P:(tt + 1) * P],
                                          prob[h % 2][:, tt, mt * P:(mt + 1) * P], k.ident[:, :])
                    mm.then_inc(t_full.sem, 1)
                if h >= 2:
                    pe.wait_ge(o_out.sem, o_out.at(h - 1))
                for mt in range(2):
                    pe.wait_ge(t_out.sem, t_out.at(2 * h + mt + 1))
                    mm = pe.matmul(bank(k, 4 + h % 2)[:, :], k.mv[:, layer, mt, h * P:(h + 1) * P],
                                   probT[h % 2][:, mt, :], start=(mt == 0), stop=(mt == 1))
                mm.then_inc(o_full.sem, 1)

        @block.vector
        def _(dve):
            value = lambda kk: k.catT[:, kk, :]
            dve_split(k, dve, value, 0, tiles=range(4))

            def lows(h):
                dve.wait_ge(z_full.sem, z_full.at(h + 1))
                for b in range(2):
                    dve.tensor_reduce(low[:, h, 2 * b:2 * b + 2],
                                      bank(k, b)[:, :].rearrange("p (a n) -> p a n", a=2), AX.X, ALU.min)\
                        .then_inc(low_ready.sem, 1)

            lows(0)
            for h in range(4):
                dve.wait_ge(e_ready.sem, e_ready.at(4 * (h + 1)))
                k.dve_chain.link(dve, dve.reciprocal(inv[:, h, :], tot[:, h, :]))
                dve.tensor_tensor(prob[h % 2][:, :, :], prob[h % 2][:, :, :],
                                  inv[:, h, :].unsqueeze(2).broadcast_to([P, 4, 256]), ALU.mult)\
                    .then_inc(p_ready.sem, 1)
                if h < 3:
                    lows(h + 1)
                if h >= 1:
                    dve_split(k, dve, value, 3 + h, tiles=[3 + h])
            dve_split(k, dve, value, 7, tiles=[7])

        @block.scalar
        def _(act):
            value = lambda kk: k.catT[:, kk, :]
            act_split(k, act, value, None, tiles=range(4))
            for h in range(4):
                act.wait_ge(low_ready.sem, low_ready.at(2 * (h + 1)))
                if h >= 2:
                    act.wait_ge(t_full.sem, t_full.at(2 * (h - 1)))
                for tt in range(4):
                    act.activation(prob[h % 2][:, tt, :], bank(k, tt // 2)[:, (tt % 2) * 256:(tt % 2) * 256 + 256],
                                   ACT.Exp, bias=low[:, h, tt:tt + 1], scale=-1.0,
                                   accum_out=tot[:, h, tt:tt + 1]).then_inc(e_ready.sem, 1)
                for mt in range(2):
                    act.wait_ge(t_full.sem, t_full.at(2 * h + mt + 1))
                    if h >= 2:
                        act.wait_ge(o_full.sem, o_full.at(h - 1))
                    act.copy(probT[h % 2][:, mt, :], bank(k, 2 + mt)[:, :]).then_inc(t_out.sem, 1)
                act.wait_ge(o_full.sem, o_full.at(h + 1))
                act.copy(value(4 + h), bank(k, 4 + h % 2)[:, :]).then_inc(o_out.sem, 1)
                act.wait_ge(o_out.sem, o_out.at(h + 1))
                act_split(k, act, value, None, tiles=[4 + h])
    for s, n in zip(k.ma_sig, (4, 8, 16, 4, 8, 8, 4, 4)):
        s.base += n
    k.advance(h_rounded=8, h_ready=8)


def stage_out_projection(k):
    first = k.ring.took
    with k.nc.Block() as block:
        @block.sync
        def _(sp):
            stream(k, sp, first + 8)

        @block.scalar
        def _(act):
            split_hi(k, act, first + 12)

        @block.tensor
        def _(pe):
            t = 0
            for group in range(2):
                t = pe_group(k, pe, t, [feature_tile(k, m * P) for m in range(4)])
            pe_used(k, pe)

        @block.vector
        def _(dve):
            split_lo(k, dve, first + 4)
            for g in range(2):
                split_lo(k, dve, first + 4 * g + 7)
                for t in range(4 * g, 4 * g + 4):
                    dve.wait_ge(k.tile_full.sem, k.tile_full.at(t + 1))
                    dve.tensor_tensor(k.xT[:, t, :], k.xT[:, t, :], bank(k, t)[:, :], ALU.add).then_inc(k.tile_free.sem, 1)
                split_lo(k, dve, first + 4 * g + 8)
    k.advance(tile_full=8, tile_free=8)


def stage_gla(k, a):
    C = 4
    base = 4096
    w_alpha = k.scr(base, (256,))
    g = k.scr(base + 256, (C, 256))
    tmp = k.scr(base + 1280, (C, 256))
    b = k.scr(base + 2304, (2, 512))
    eb = k.scr(base + 3328, (2, 512))
    qe = k.scr(base + 4352, (2, 512))
    kbar = k.scr(base + 5376, (2, 512))
    kbar_tok = k.scr(base + 6400, (C, 2, P))
    diff = [k.scr(base + 7424 + i * 1024, (1024,)) for i in range(2)]
    ql = [k.scr(base + 9472 + i * 1024, (2, 512)) for i in range(2)]
    kl = [k.scr(base + 11520 + i * 1024, (2, 512)) for i in range(2)]
    A = k.scr(base + 13568, (4, 512))
    Ss = [k.scr(base + 15616 + i * 512, (2, 256)) for i in range(2)]
    last = lambda t: t[:, :, :].rearrange("p i (c n) -> p (i c) n", c=C)
    w_in, y_full, ls_ready, b_full, b_ready = (k.sem(n) for n in ("w_alpha_in", "alpha_full", "decay_ready", "cum_full", "cum_ready"))
    logs = k.sem("alpha_logs")
    kb_ready, kb_turned, kb_out = k.sem("kbar_ready"), k.sem("kbar_turned"), k.sem("kbar_out")
    with k.nc.Block() as block:
        @block.sync
        def _(sp):
            sp.dma_start(w_alpha[0:16, :], a["a_w_alpha"][0]).then_inc(w_in, 16)
            sp.dma_start(w_alpha[16:17, :], a["a_b_alpha"]).then_inc(w_in, 16)

        @block.tensor
        def _(pe):
            pe.wait_ge(w_in, 32)
            for c in range(C):
                mm = pe.matmul(bank(k, c // 2)[:, (c % 2) * 256:(c % 2) * 256 + 256], k.alrT[0:17, c * P:(c + 1) * P],
                               w_alpha[0:17, :], start=True, stop=True)
            mm.then_inc(y_full, 1)
            pe.wait_ge(ls_ready, 1)
            for i in range(2):
                for c in range(C):
                    mm = pe.matmul(bank(k, 2 + i)[:, c * P:(c + 1) * P], g[:, c, i * P:(i + 1) * P], k.triu[:, :],
                                   start=True, stop=True)
            mm.then_inc(b_full, 1)
            pe.wait_ge(kb_ready, 1)
            for c in range(C):
                for i in range(2):
                    mm = pe.transpose(bank(k, 4 + c // 2)[:, ((c % 2) * 2 + i) * P:((c % 2) * 2 + i + 1) * P],
                                      kbar[:, i, c * P:(c + 1) * P], k.ident[:, :])
            mm.then_inc(kb_turned, 1)

        @block.scalar
        def _(act):
            L = lambda ins: k.act_chain.link(act, ins)
            act.wait_ge(y_full, 1)
            for h in range(2):
                src = bank(k, h)[:, :].rearrange("p (c n) -> p c n", c=2)
                L(act.activation(tmp[:, 2 * h:2 * h + 2, :], src, ACT.Abs))
                L(act.activation(tmp[:, 2 * h:2 * h + 2, :], tmp[:, 2 * h:2 * h + 2, :], ACT.Exp, scale=-1.0))
                act.activation(tmp[:, 2 * h:2 * h + 2, :], tmp[:, 2 * h:2 * h + 2, :], ACT.Ln, bias=1.0)\
                    .then_inc(logs, 1)
            act.wait_ge(b_full, 1)
            for i in range(2):
                act.mul(b[:, i, :], bank(k, 2 + i)[:, :], 1.0 / 16).then_inc(b_ready, 1)
            act.wait_ge(b_ready, 2)
            L(act.activation(eb[:, :, :], b[:, :, :], ACT.Exp))
            act.wait_ge(b_ready, 3)
            L(act.activation(kbar[:, :, :], kbar[:, :, :], ACT.Exp))
            act.sem_inc(b_ready, 1)
            act.wait_ge(kb_turned, 1)
            for h in range(2):
                act.copy(kbar_tok[:, 2 * h:2 * h + 2, :, :].rearrange("p c i n -> p (c i n)"),
                         bank(k, 4 + h)[:, :]).then_inc(kb_out, 1)

        @block.vector
        def _(dve):
            L = lambda ins: k.dve_chain.link(dve, ins)
            dve.wait_ge(logs, 2)
            for h in range(2):
                ins = dve.scalar_tensor_tensor(g[:, 2 * h:2 * h + 2, :], bank(k, h)[:, :].rearrange("p (c n) -> p c n", c=2),
                                               0.0, tmp[:, 2 * h:2 * h + 2, :], ALU.min, ALU.subtract)
                if h == 0:
                    L(ins)
            ins.then_inc(ls_ready, 1)
            dve.wait_ge(b_ready, 2)
            dve.tensor_tensor(last(kbar), last(b)[:, :, P - 1:P].broadcast_to([P, 8, P]), last(b), ALU.subtract)\
                .then_inc(b_ready, 1)
            dve.wait_ge(b_ready, 4)
            L(dve.tensor_tensor(qe[:, :, :], k.qT[:, :, :], eb[:, :, :], ALU.mult))
            dve.tensor_tensor(kbar[:, :, :], k.kT[:, :, :], kbar[:, :, :], ALU.mult).then_inc(kb_ready, 1)

    d_ready, dl_ready, e_done, qk_ready = (k.sem(n) for n in ("diff_ready", "diff_left", "level_exp", "level_qk"))
    s_full, s_done = k.sem("level_full"), k.sem("level_done")
    halves = lambda t, n: t.rearrange("p (m two n) -> p m two n", two=2, n=n)
    with k.nc.Block() as block:
        @block.vector
        def _(dve):
            L = lambda ins: k.dve_chain.link(dve, ins)
            L(dve.memset(A[:, :, :], 0.0))

            def differences(lv):
                n = 1 << lv
                m = 1024 // (2 * n)
                bv = halves(b[:, :, :].rearrange("p i n -> p (i n)"), n)
                dv = halves(diff[lv % 2], n)
                ref = bv[:, :, 0, n - 1:n].broadcast_to([P, m, n])
                if lv >= 2:
                    dve.wait_ge(qk_ready, lv - 1)
                dve.tensor_tensor(dv[:, :, 0, :], ref, bv[:, :, 0, :], ALU.subtract).then_inc(dl_ready, 1)
                dve.tensor_tensor(dv[:, :, 1, :], bv[:, :, 1, :], ref, ALU.subtract).then_inc(d_ready, 1)

            def products(lv):
                if lv == 7:
                    return
                dve.wait_ge(e_done, lv + 1)
                if lv >= 2:
                    dve.wait_ge(s_full, 4 * (lv - 1))
                e = diff[lv % 2].rearrange("p (i n) -> p i n", i=2)
                L(dve.tensor_tensor(ql[lv % 2][:, :, :], k.qT[:, :, :], e, ALU.mult))
                dve.tensor_tensor(kl[lv % 2][:, :, :], k.kT[:, :, :], e, ALU.mult).then_inc(qk_ready, 1)

            def place(lv):
                mask = (k.level[:, lv, :] if lv < 7 else k.ident[:, :]).bitcast(I32)
                for h in range(4):
                    dve.wait_ge(s_full, 4 * lv + h + 1)
                    if lv >= 1:
                        dve.wait_ge(s_done, 4 * (lv - 1) + h + 1)
                    dve.copy_predicated(A[:, h, :].rearrange("p (c n) -> p c n", c=C),
                                        mask.unsqueeze(1).broadcast_to([P, C, P]),
                                        bank(k, 4 * (lv % 2) + h)[:, :].rearrange("p (c n) -> p c n", c=C))\
                        .then_inc(s_done, 1)

            differences(0)
            for lv in range(8):
                if lv < 6:
                    differences(lv + 1)
                products(lv)
                if lv >= 1:
                    place(lv - 1)
            place(7)

        @block.scalar
        def _(act):
            for lv in range(7):
                act.wait_ge(d_ready, lv + 1)
                act.wait_ge(dl_ready, lv + 1)
                act.activation(diff[lv % 2], diff[lv % 2], ACT.Exp).then_inc(e_done, 1)

        @block.tensor
        def _(pe):
            for lv in range(8):
                q, kk = (ql[lv % 2], kl[lv % 2]) if lv < 7 else (k.qT, k.kT)
                if lv < 7:
                    pe.wait_ge(qk_ready, lv + 1)
                for h in range(4):
                    if lv >= 2:
                        pe.wait_ge(s_done, 4 * (lv - 2) + h + 1)
                    r0 = (h % 2) * 64
                    for c in range(C):
                        cs = slice(c * P, (c + 1) * P)
                        mm = pe.matmul(bank(k, 4 * (lv % 2) + h)[:, cs], kk[r0:r0 + 64, h // 2, cs], q[r0:r0 + 64, h // 2, cs],
                                       start=True, stop=True)
                    mm.then_inc(s_full, 1)

    u_full, S_ready, o_full = k.sem("gla_update_full"), k.sem("gla_state_ready"), k.sem("gla_out_full")
    o_out, sq, nf, rs = k.sem("gla_out"), k.sem("gla_squares"), k.sem("gla_sums"), k.sem("gla_rstd")
    o = A
    o_sb, osq, rstd = k.scr(base + 7424, (4, 512)), k.scr(base + 9472, (4, 512)), k.scr(base + 11520, (4, 512))
    with k.nc.Block() as block:
        @block.tensor
        def _(pe):
            for c in range(C):
                cs = slice(c * P, (c + 1) * P)
                if c < C - 1:
                    for i in range(2):
                        if c >= 1:
                            pe.wait_ge(S_ready, 2 * (c - 1) + i + 1)
                        pe.matmul(bank(k, 4 + i)[:, 0:256], kbar_tok[:, c, i, :], k.v[:, c, i * 256:(i + 1) * 256],
                                  start=True, stop=True).then_inc(u_full, 1)
                for h in range(4):
                    r0 = (h % 2) * 64
                    if c >= 1:
                        pe.wait_ge(S_ready, 2 * c)
                        pe.matmul(bank(k, h)[:, cs], Ss[(c - 1) % 2][r0:r0 + 64, h // 2, (h % 2) * P:(h % 2 + 1) * P],
                                  qe[r0:r0 + 64, h // 2, cs], start=True, stop=False)
                    mm = pe.matmul(bank(k, h)[:, cs], k.v[:, c, h * P:(h + 1) * P], A[:, h, cs], start=(c == 0), stop=True)
            mm.then_inc(o_full, 1)
            for h in range(4):
                pe.wait_ge(sq, h + 1)
                pe.matmul(bank(k, 4 + h)[:, :], k.ones[:, :], osq[:, h, :], start=True, stop=True).then_inc(nf, 1)

        @block.vector
        def _(dve):
            L = lambda ins: k.dve_chain.link(dve, ins)
            for c in range(C - 1):
                for i in range(2):
                    dve.wait_ge(u_full, 2 * c + i + 1)
                    col = eb[:, i, c * P + P - 1:c * P + P]
                    if c == 0:
                        ins = dve.tensor_copy(Ss[0][:, i, :], bank(k, 4 + i)[:, 0:256])
                    else:
                        dve.wait_ge(S_ready, 2 * c)
                        if c >= 2:
                            dve.wait_ge(u_full, 2 * c + 2)
                        ins = dve.scalar_tensor_tensor(Ss[c % 2][:, i, :], Ss[(c - 1) % 2][:, i, :], col,
                                                       bank(k, 4 + i)[:, 0:256], ALU.mult, ALU.add)
                    ins.then_inc(S_ready, 1)
            for h in range(4):
                dve.wait_ge(rs, h + 1)
                L(dve.scalar_tensor_tensor(o_sb[:, h, :], o_sb[:, h, :], k.vec(VEC_ROWS["a_g_head"]), rstd[:, h, :],
                                           ALU.mult, ALU.mult))
                L(dve.tensor_tensor(k.catT[:, h, :], o_sb[:, h, :], k.rT[:, h, :], ALU.mult))

        @block.scalar
        def _(act):
            L = lambda ins: k.act_chain.link(act, ins)
            act.wait_ge(o_full, 1)
            for h in range(4):
                act.copy(o_sb[:, h, :], bank(k, h)[:, :]).then_inc(o_out, 1)
                act.activation(osq[:, h, :], bank(k, h)[:, :], ACT.Square).then_inc(sq, 1)
            act.wait_ge(o_out, 4)
            for h in range(4):
                act.wait_ge(nf, h + 1)
                L(act.activation(rstd[:, h, :], bank(k, 4 + h)[:, :], ACT.Ln, bias=k.eps[:, 0:1], scale=1.0 / P))
            for h in range(4):
                act.activation(rstd[:, h, :], rstd[:, h, :], ACT.Exp, scale=-0.5).then_inc(rs, 1)


FF = 2816
FT = FF // P


def ffn_chunks(k, w_up, w_down):
    up = w_up.rearrange("(k p) n -> p k n", p=P)
    down = w_down.rearrange("(k p) n -> p k n", p=P)
    out = []
    for grp in range(FT // 2):
        for c in range(4):
            out.append(lambda n, grp=grp, c=c: [
                (raw_slot(k, n, 2, 512)[:, :, s * 256:(s + 1) * 256],
                 up[:, 2 * c:2 * c + 2, s * FF + grp * 256:s * FF + (grp + 1) * 256]) for s in range(2)])
    up_count = len(out)
    for kk in range(FT):
        out.append(lambda n, kk=kk: [(raw_slot(k, n, 1, 1024)[:, 0, :], down[:, kk, :])])
    return out, [2] * up_count + [1] * FT


def stage_ffn(k, w_up, gain, taps, bias, both):
    GROUPS = FT // 2
    LOOPS = (GROUPS - 3) // 2
    AHEAD = 6
    act_t = k.carve(0, (FT * 512,))
    pad = [[k.carve(FT * 512 + (2 * s + i) * 516, (516,)) for i in range(2)] for s in range(2)]
    acc = [[k.scr((2 * s + i) * 512, (512,)) for i in range(2)] for s in range(2)]
    first = k.ring.took
    UP, TOTAL = 4 * GROUPS, 4 * GROUPS + FT
    down0 = first + UP
    up = w_up.rearrange("(k p) n -> p k n", p=P)
    padded, conv_a, conv_b, silu, done, cleared, act_hi, act_lo = k.ffn_sig
    sides = 2 if both else 1
    bank_of = lambda f, s: bank(k, 2 * (f % 4) + s)

    with k.nc.Block() as block:
        @block.sync
        def _(sp):
            with sp.Fori(0, (UP - RING) // 8) as i:
                for j in range(8):
                    n = first + RING + j
                    src = up[:, 2 * (j % 4):2 * (j % 4) + 2, :]
                    pieces = [(raw_slot(k, n, 2, 512)[:, :, s * 256:(s + 1) * 256],
                               src[:, :, bass.ds(i * 512 + (s * FF + (1 + j // 4) * 256), 256)]) for s in range(2)]
                    load_chunk(k, sp, n, pieces, i)
            k.ring.out = down0
            stream(k, sp, first + TOTAL)

        @block.tensor
        def _(pe):
            pe_norm_sums(k, pe, 512)

            def group(g, reg):
                f0 = 2 * g
                tiles = [(bank_of(f0 + f, s)[:, :], feature_tile(k, s * 256 + f * P)[1]) for f in range(2) for s in range(2)]

                def before(i, kk):
                    if kk == 0 and g >= 2 and i % 2 == 0:
                        pe.wait_ge(done.sem, plus(done.at(f0 + i // 2 - 3), reg, 4))
                    if g == 0 and i == 0:
                        pe.wait_ge(k.h_ready.sem, k.h_ready.at(kk + 1))

                for c in range(4):
                    pe_chunk(k, pe, first + 4 * g + c, tiles, [2 * c, 2 * c + 1], 8, reg, before=before)

            group(0, None)
            group(1, None)
            with pe.Fori(0, LOOPS) as i:
                group(2, i)
                group(3, i)
            group(GROUPS - 1, None)
            pe_used(k, pe)

            def down(kk, reg, last=False):
                order = (4, 5, 6, 7, 0, 1, 2, 3) if kk == 0 else range(8)
                n = down0 + kk
                stage_parts = (k.h_hi[:, kk % 8, :], k.h_lo[:, kk % 8, :])
                pe.wait_ge(act_lo.sem, plus(act_lo.at(kk + 1), reg, 8))
                pe.wait_ge(k.ring.lo, plus(n + 1, reg, 8))
                wh, wl = parts(k, n, 1)
                for x, o in enumerate(order):
                    if kk == 0 and x % 4 == 0:
                        pe.wait_ge(done.sem, done.at(FT - 2 if x == 0 else FT))
                    cs = slice(o * P, (o + 1) * P)
                    p, q = pe_three(k, pe, bank(k, o)[:, :], (wh[:, 0, cs], wl[:, 0, cs]), stage_parts, kk == 0, last)
                    if x == 0 and k.ring.owed:
                        p.then_inc(k.ring.used, 1)
                    if last:
                        q.then_inc(k.tile_full.sem, 1)
                k.ring.owed = 1

            down(0, None)
            down(1, None)
            with pe.Fori(0, 2) as i:
                for kk in range(2, 10):
                    down(kk, i)
            for kk in range(18, FT):
                down(kk, None, kk == FT - 1)
            pe_used(k, pe)
        k.ring.took = first + TOTAL

        @block.gpsimd
        def _(pool):
            for s in range(sides):
                for i in range(2):
                    pool.memset(pad[s][i][:, 0:2], 0.0).then_inc(cleared.sem, 1)

        @block.scalar
        def _(act):
            act_norm(k, act)
            act.wait_ge(cleared.sem, cleared.at(2 * sides))

            def copies(f, reg):
                for s in range(sides):
                    act.wait_ge(k.tile_full.sem, plus(k.tile_full.at(2 * f + s + 1), reg, 8))
                    if f >= 2:
                        sig = (conv_a, conv_b)[s]
                        act.wait_ge(sig.sem, plus(sig.at(f - 1), reg, 4))
                    act.copy(pad[s][f % 2][:, 2:514], bank_of(f, s)[:, :]).then_inc(padded.sem, 1)

            def gate(f, reg):
                act.wait_ge(conv_a.sem, plus(conv_a.at(f + 1), reg, 4))
                act.activation(acc[0][f % 2], acc[0][f % 2], ACT.Silu).then_inc(silu.sem, 1)

            def group(g, reg, loads=2):
                for c in range(4, 7):
                    split_hi_chunk(k, act, first + 4 * g + c, reg)
                for f in (2 * g, 2 * g + 1):
                    copies(f, reg)
                for f in (2 * g, 2 * g + 1):
                    gate(f, reg)
                split_hi_chunk(k, act, first + 4 * g + 7, reg)

            group(0, None)
            group(1, None)
            with act.Fori(0, LOOPS) as i:
                group(2, i)
                group(3, i)
            group(GROUPS - 1, None)

            def product_hi(kk):
                act.wait_ge(done.sem, done.at(kk + 1))
                act.wait_ge(k.ring.used, down0 + max(kk - 7, 0))
                act.copy(k.h_hi[:, kk % 8, :], act_t[:, kk * 512:(kk + 1) * 512]).then_inc(act_hi.sem, 1)

            for kk in range(AHEAD):
                product_hi(kk)
            k.ring.hi_at = down0 + 4
            for kk in range(FT):
                split_hi(k, act, down0 + kk + 5)
                if kk + AHEAD < FT:
                    product_hi(kk + AHEAD)

        @block.vector
        def _(dve):
            dve_norm(k, dve, gain)

            def conv(f, reg):
                vec = lambda c: k.vec(c + f) if reg is None else k.vecs[:, bass.ds(reg * 4 + (c + f), 1)]
                if f >= 2:
                    dve.wait_ge(done.sem, plus(done.at(f - 1), reg, 4))
                for s in range(sides):
                    dve.wait_ge(padded.sem, plus(padded.at(sides * f + s + 1), reg, 4 * sides))
                    dst, src = acc[s][f % 2], pad[s][f % 2]
                    t0, t1, t2 = (taps(j) + s * FT for j in range(3))
                    if bias is None:
                        k.dve_chain.link(dve, dve.tensor_scalar(dst, src[:, 2:514], vec(t2), None, ALU.mult))
                    else:
                        k.dve_chain.link(dve, dve.tensor_scalar(dst, src[:, 2:514], vec(t2), vec(bias), ALU.mult, ALU.add))
                    k.dve_chain.link(dve, dve.scalar_tensor_tensor(dst, src[:, 1:513], vec(t1), dst, ALU.mult, ALU.add))
                    dve.scalar_tensor_tensor(dst, src[:, 0:512], vec(t0), dst, ALU.mult, ALU.add)\
                        .then_inc((conv_a, conv_b)[s].sem, 1)

            def gated(f, reg):
                dve.wait_ge(silu.sem, plus(silu.at(f + 1), reg, 4))
                if both:
                    dve.wait_ge(conv_b.sem, plus(conv_b.at(f + 1), reg, 4))
                else:
                    dve.wait_ge(k.tile_full.sem, plus(k.tile_full.at(2 * f + 2), reg, 8))
                other = acc[1][f % 2] if both else bank_of(f, 1)[:, :]
                dst = act_t[:, f * 512:(f + 1) * 512] if reg is None else act_t[:, bass.ds(reg * 2048 + f * 512, 512)]
                dve.tensor_tensor(dst, acc[0][f % 2], other, ALU.mult).then_inc(done.sem, 1)

            def group(g, reg):
                for c in range(4, 7):
                    split_lo_chunk(k, dve, first + 4 * g + c, reg)
                for f in (2 * g, 2 * g + 1):
                    conv(f, reg)
                for f in (2 * g, 2 * g + 1):
                    gated(f, reg)
                split_lo_chunk(k, dve, first + 4 * g + 7, reg)

            group(0, None)
            group(1, None)
            k.dve_chain.per = 4 * 2 * sides
            with dve.Fori(0, LOOPS) as i:
                k.dve_chain.reg = i
                n0 = k.dve_chain.n
                group(2, i)
                group(3, i)
                assert k.dve_chain.n - n0 == k.dve_chain.per
            k.dve_chain.reg = None
            k.dve_chain.n = n0 + k.dve_chain.per * LOOPS
            group(GROUPS - 1, None)

            def product_lo(kk):
                dve.wait_ge(act_hi.sem, act_hi.at(kk + 1))
                dve.tensor_tensor(k.h_lo[:, kk % 8, :], act_t[:, kk * 512:(kk + 1) * 512],
                                  k.h_hi[:, kk % 8, :].bitcast(F32), ALU.subtract).then_inc(act_lo.sem, 1)

            for kk in range(AHEAD):
                product_lo(kk)
            k.ring.lo_at = down0 + 4
            for kk in range(FT):
                split_lo(k, dve, down0 + kk + 5)
                if kk + AHEAD < FT:
                    product_lo(kk + AHEAD)
            for o in range(8):
                dve.wait_ge(k.tile_full.sem, k.tile_full.at(2 * FT + o + 1))
                dve.tensor_tensor(k.xT[:, o, :], k.xT[:, o, :], bank(k, o)[:, :], ALU.add).then_inc(k.tile_free.sem, 1)
    k.advance(**NORM, tile_full=2 * FT + 8, tile_free=8)
    for s, n in zip(k.ffn_sig, (FT * sides, FT, FT * (sides - 1), FT, FT, 2 * sides, FT, FT)):
        s.base += n


NCMP = 31


def kv_chunks(k, w_kv):
    wv = w_kv.rearrange("(k p) n -> p k n", p=P)
    return [lambda n, k0=k0: [
        (raw_slot(k, n, 2, 512)[:, kk, :].rearrange("p (c two d) -> p c two d", c=4, two=2)[:, :, two, :],
         wv[:, k0 + kk, 0:256].rearrange("p (c d) -> p c d", c=4)) for kk in range(2) for two in range(2)]
        for k0 in range(0, 8, 2)]


def paired_query_chunks(k, w):
    wv = w.rearrange("(k p) n -> p k n", p=P)
    return [lambda n, k0=k0: [
        (raw_slot(k, n, 2, 512)[:, kk, :].rearrange("p (j g d) -> p j g d", j=4, g=2)[:, :, g, :],
         wv[:, k0 + kk, g * 256:(g + 1) * 256].rearrange("p (j d) -> p j d", j=4)) for kk in range(2) for g in range(2)]
        for k0 in range(0, 8, 2)]


def paired_out_chunks(k, w, cols):
    return [lambda n, j0=j0: [(raw_slot(k, n, 2, 512)[g * 64:(g + 1) * 64, :, :],
                               w[g * 256 + j0 * 64:g * 256 + (j0 + 2) * 64, cols:cols + 512].rearrange("(j p) n -> p j n", p=64))
                              for g in range(2)] for j0 in (0, 2)]


def stage_nsa_in(k, a):
    N2 = NCMP + 1
    k.qT, k.mqT = k.carve(0, (4, 512)), k.carve(2048, (4, 512))
    k.ksT, k.kwT = k.carve(4096, (512,)), k.carve(4608, (512,))
    k.vsw = k.carve(5120, (4, 256))
    k.kcT, k.vc = k.carve(8192, (32,)), k.carve(8224, (P,))
    k.gates = k.carve(8352, (4, 24))
    hid = [[k.carve(8448 + (2 * s + ht) * 64, (64,)) for ht in range(2)] for s in range(2)]
    cb = k.carve(8704, (4,))
    w2k, w2v = k.carve(8712, (2, P)), k.carve(8968, (2, 64))
    kv2 = [k.carve(9280 + s * 1056, (2, 528)) for s in range(2)]
    kv_parts = [[k.scope(f"kv_{part}{s}", [P, 2, 528], F32R) for part in ("hi", "lo")] for s in range(2)]
    pe_parts = [[k.scope(f"pe_{part}{s}", [P, 18], F32R) for part in ("hi", "lo")] for s in range(2)]
    pe_cols = [k.vecs[:, VEC_ROWS[n]:VEC_ROWS[n] + 18] for n in ("pe_k", "pe_v")]
    wg, wg_hi, wg_lo = small_weights(k, "w_gate", 8, 24)
    old_sq, k.sq = k.sq, k.carve(4096, (8, 512))
    h2 = k.carve(0, (8, 512))
    small_in, kv_clear, kv_shift, small_hi, small_lo = (k.sem(n) for n in (
        "nsa_small_in", "kv_cleared", "kv_shifted", "small_hi", "small_lo"))
    gates_ready = k.sem("gates_ready")
    first = k.ring.took
    smalls = [(wg_hi, wg_lo, wg), (*pe_parts[0], pe_cols[0]), (*pe_parts[1], pe_cols[1]),
              (*kv_parts[0], kv2[0]), (*kv_parts[1], kv2[1])]
    whole = lambda t: t[tuple(slice(None) for _ in t.shape)]
    with k.nc.Block() as block:
        @block.sync
        def _(sp):
            w2 = a["w_ck2"].rearrange("(k p) n -> p k n", p=P)
            for two in range(2):
                sp.dma_start(w2k[:, :, two * 64:(two + 1) * 64], w2).then_inc(small_in, 16)
            sp.dma_start(w2v[:, :, :], a["w_cv2"].rearrange("(k p) n -> p k n", p=P)).then_inc(small_in, 16)
            sp.dma_start(wg[:, :, :], a["b_w_in"][0].rearrange("(k p) n -> p k n", p=P)[:, :, 512:536]).then_inc(small_in, 16)
            stream(k, sp, first + 24)

        @block.gpsimd
        def _(pool):
            for s in range(2):
                pool.memset(kv2[s][:, :, :], 0.0).then_inc(kv_clear, 1)

        @block.vector
        def _(dve):
            dve_norm(k, dve, VEC_ROWS["g_kv"])
            dve_normed(k, dve, lambda kk: h2[:, kk, :], lambda kk: k.xT[:, kk, :], VEC_ROWS["g_mix1"], 512)

            def small(i):
                hi, lo, src = smalls[i]
                dve.wait_ge(small_hi, i + 1)
                dve.tensor_tensor(whole(lo), whole(src), whole(hi).bitcast(F32), ALU.subtract).then_inc(small_lo, 1)

            for i in range(3):
                small(i)
            split_lo(k, dve, first + 8)
            small(3)
            small(4)
            split_lo(k, dve, first + 12)
            dve_split(k, dve, lambda kk: h2[:, kk, :], 8)
            for g in range(2, 6):
                split_lo(k, dve, first + 4 * g + 8)
            dve.wait_ge(gates_ready, 1)
            first_rows = k.gates[:, 0, :].rearrange("p (h b) -> p h b", b=3)[:, :, 0]
            k.dve_chain.link(dve, dve.tensor_scalar(first_rows, first_rows, k.valid[:, 0:1], None, ALU.mult))

        @block.scalar
        def _(act):
            act_norm(k, act)
            act.wait_ge(small_in, 64)

            def small(i):
                act.copy(whole(smalls[i][0]), whole(smalls[i][2])).then_inc(small_hi, 1)

            for i in range(3):
                small(i)
            act.wait_ge(kv_clear, 2)

            def read_out(t, count):
                for t in range(t, t + count):
                    act.wait_ge(k.tile_full.sem, k.tile_full.at(t + 1))
                    src = bank(k, t)
                    if t < 4:
                        dst = kv2[t // 2][:, t % 2, :]
                        act.copy(dst[0:64, 0:512], src[0:64, :]).then_inc(kv_shift, 1)
                        ins = act.copy(dst[64:P, 0:511], src[64:P, 1:512])
                    elif t < 6:
                        ins = act.copy(k.ksT if t == 4 else k.kwT, src[:, :])
                    elif t < 10:
                        ins = act.copy(k.vsw[:, t - 6, :], src[:, 0:256])
                    elif t < 18:
                        s, i = divmod(t - 10, 4)
                        col = cb[:, 2 * s + i % 2:2 * s + i % 2 + 1]
                        if i < 2:
                            k.act_chain.link(act, act.copy(col, src[:, 0:1]))
                            act.sem_inc(k.tile_free.sem, 1)
                            continue
                        ins = act.activation(hid[s][i - 2], src[:, 0:64], ACT.Gelu_apprx_tanh, bias=col)
                    elif t == 18:
                        act.copy(k.kcT[0:64, 0:NCMP], src[0:64, 0:NCMP]).then_inc(kv_shift, 1)
                        ins = act.copy(k.kcT[64:P, 0:NCMP], src[64:P, N2:N2 + NCMP])
                    elif t == 19:
                        ins = act.copy(k.vc[0:NCMP, :], src[0:NCMP, 0:P])
                    elif t < 24:
                        ins = act.mul(k.qT[:, t - 20, :], src[:, :], -(64 ** -0.5))
                    elif t < 28:
                        ins = act.mul(k.mqT[:, t - 24, :], src[:, :], -(128 ** -0.5))
                    else:
                        k.act_chain.link(act, act.activation(k.gates[:, :, :].rearrange("p a b -> p (a b)"), src[:, 0:96], ACT.Sigmoid))
                        act.sem_inc(gates_ready, 1)
                        act.sem_inc(k.tile_free.sem, 1)
                        continue
                    ins.then_inc(k.tile_free.sem, 1)

            split_hi(k, act, first + 7)
            read_out(0, 4)
            act.wait_ge(kv_shift, 4)
            act.wait_ge(k.tile_free.sem, k.tile_free.at(4))
            small(3)
            small(4)
            split_hi(k, act, first + 11)
            read_out(4, 6)
            split_hi(k, act, first + 12)
            act.wait_ge(k.ring.used, first + 8)
            act_split(k, act, lambda kk: h2[:, kk, :], 8)
            split_hi(k, act, first + 15)
            read_out(10, 4)
            split_hi(k, act, first + 19)
            read_out(14, 6)
            split_hi(k, act, first + 23)
            read_out(20, 4)
            split_hi(k, act, first + 27)
            read_out(24, 4)
            split_hi(k, act, first + 28)
            read_out(28, 1)

        @block.tensor
        def _(pe):
            pe_norm_sums(k, pe, 512)
            t = pe_group(k, pe, 0, [feature_tile(k, m * P) for m in range(4)], 0)
            values = lambda w: w.rearrange("p (b two n) -> p b two n", b=2, two=2)[:, :, 1, :]
            t = pe_group(k, pe, t, [feature_tile(k, c) for c in (0, 256)] + [token_tile(k, tt, values, 256) for tt in range(4)])
            for s in range(2):
                pe.wait_ge(small_lo, 4 + s)

                def hidden(ht, own):
                    def operands(j, w):
                        stat = [x[:, ht * P:(ht + 1) * P] for x in w]
                        if own:
                            return stat, [x[:, j:j + 2] for x in pe_parts[s]]
                        return stat, [x[:, :, 2 * j:2 * j + 16 * (N2 - 1) + 1:16] for x in kv_parts[s]]
                    return operands

                tiles = [(bank(k, t + i)[:, 0:2 if i < 2 else 2 * N2], hidden(i % 2, i < 2)) for i in range(4)]

                def before(i, j):
                    if j == 0 and t + i >= 8:
                        pe.wait_ge(k.tile_free.sem, k.tile_free.at(t + i - 7))

                for c in range(4):
                    n = k.ring.took
                    k.ring.took += 1
                    pe_chunk(k, pe, n, tiles, range(4 * c, 4 * c + 4), 16, before=before)
                t += 4
            pe.wait_ge(small_in, 64)
            pe.wait_ge(k.tile_free.sem, k.tile_free.at(18))
            for ht in range(2):
                mm = pe.matmul(bank(k, t)[:, 0:64], w2k[:, ht, :], hid[0][ht], start=(ht == 0), stop=(ht == 1))
            mm.then_inc(k.tile_full.sem, 1)
            t += 1
            for g in range(2):
                for ht in range(2):
                    mm = pe.matmul(bank(k, t)[0:NCMP, g * 64:(g + 1) * 64], hid[1][ht][:, g * N2:g * N2 + NCMP], w2v[:, ht, :],
                                   start=(ht == 0), stop=(ht == 1))
            mm.then_inc(k.tile_full.sem, 1)
            t += 1
            for group in range(2):
                t = pe_group(k, pe, t, [feature_tile(k, m * P) for m in range(4)], 8 if group == 0 else None)
            pe_used(k, pe)
            pe.wait_ge(k.tile_free.sem, k.tile_free.at(t - 7))
            for tt in range(4):
                ts = slice(tt * P, (tt + 1) * P)
                for kk in range(8):
                    _, mm = pe_three(k, pe, bank(k, t)[:, tt * 24:(tt + 1) * 24], (k.h_hi[:, kk, ts], k.h_lo[:, kk, ts]),
                                     (wg_hi[:, kk, :], wg_lo[:, kk, :]), kk == 0, kk == 7)
            mm.then_inc(k.tile_full.sem, 1)
    k.advance(sq_ready=8, sums_full=1, rstd_ready=1, normed=16, h_rounded=16, h_ready=16, tile_full=29, tile_free=29)
    k.sq = old_sq


def stage_nsa(k):
    prob = [[[k.scr(9184 + par * 2688 + br * 1280 + 64 * i * (i + 1), ((i + 1) * P,)) for i in range(4)]
             for br in range(2)] for par in range(2)]
    pcmp = [k.scr(9184 + par * 2688 + 2560, (4, NCMP)) for par in range(2)]
    at = [14560, 17632]
    offs = [0, 512, 896, 1152]
    pT = [[[k.scr(at[par] + br * 1280 + offs[j], (512 - j * P,)) for j in range(4)] for br in range(2)] for par in range(2)]
    pcT = [k.scr(at[par] + 2560, (512,)) for par in range(2)]
    low, tot, coef = (k.scr(20704 + i * 96, (8, 12)) for i in range(3))
    s_full, z_ready, e_done, p_ready = (k.sem(n) for n in ("nsa_scores", "nsa_lows", "nsa_exps", "nsa_probs"))
    t_full, t_out_a, t_out_v, o_full, o_out = (k.sem(n) for n in ("nsa_turned", "nsa_turned_act", "nsa_turned_dve", "nsa_full", "nsa_out"))
    bias_of, bias_cmp = k.scr(4096, (8, 512)), k.scr(8192, (8, 124))
    slopes = k.sem("alibi_ready")
    zc_ready, lc_ready = k.sem("nsa_cmp_added"), k.sem("nsa_cmp_low")
    by_vector = lambda n: (n % 9) % 2 == 1
    copies_by = lambda which, n: sum(by_vector(m) == bool(which) for m in range(n))
    copied = lambda n: (int(by_vector(n)), copies_by(int(by_vector(n)), n + 1))
    units = [(i, br) for i in range(4) for br in range(2)]

    with k.nc.Block() as block:
        @block.gpsimd
        def _(pool):
            for h in range(8):
                pool.tensor_scalar(bias_of[:, h, :], k.dist[:, :], 2.0 ** -(h + 1), None, ALU.mult).then_inc(slopes, 1)
                pool.tensor_scalar(bias_cmp[:, h, :], k.dist_cmp[:, :], 2.0 ** -(h + 1), None, ALU.mult).then_inc(slopes, 1)

        @block.tensor
        def _(pe):
            def scores(h):
                j, g = h % 4, h // 4
                r = slice(g * 64, (g + 1) * 64)
                for u, (i, br) in enumerate(units):
                    n = 8 * h + u
                    if n >= 3:
                        pe.wait_ge(z_ready, n - 2)
                    keys = (k.ksT, k.kwT)[br]
                    pe.matmul(bank(k, n % 3)[:, 0:(i + 1) * P], k.qT[r, j, i * P:(i + 1) * P], keys[r, 0:(i + 1) * P],
                              start=True, stop=True).then_inc(s_full, 1)
                if h >= 1:
                    pe.wait_ge(zc_ready, h)
                for i in range(4):
                    mm = pe.matmul(bank(k, 3)[:, i * 32:i * 32 + NCMP], k.qT[r, j, i * P:(i + 1) * P], k.kcT[r, 0:NCMP],
                                   start=True, stop=True)
                mm.then_inc(s_full, 1)

            def turn(h):
                pe.wait_ge(p_ready, 9 * (h + 1))
                for m in range(9):
                    n = 9 * h + m
                    if n >= 2:
                        which, count = copied(n - 2)
                        pe.wait_ge((t_out_a, t_out_v)[which], count)
                    b = bank(k, 4 + n % 2)
                    if m < 8:
                        br, j = divmod(m, 4)
                        for i in range(j, 4):
                            mm = pe.transpose(b[:, (i - j) * P:(i - j + 1) * P], prob[h % 2][br][i][:, j * P:(j + 1) * P], k.ident[:, :])
                    else:
                        for i in range(4):
                            mm = pe.transpose(b[0:NCMP, i * P:(i + 1) * P], pcmp[h % 2][:, i, :], k.ident[:, :])
                    mm.then_inc(t_full, 1)

            def values(h):
                if h >= 2:
                    pe.wait_ge(o_out, h - 1)
                o = bank(k, 6 + h % 2)
                for which in range(2):
                    pe.wait_ge((t_out_a, t_out_v)[which], copies_by(which, 9 * (h + 1)))
                pe.matmul(o[:, :], k.vc[0:NCMP, :], pcT[h % 2][0:NCMP, :], start=True, stop=False)
                for br in range(2):
                    for j in range(4):
                        mm = pe.matmul(o[:, j * P:512], k.vsw[:, j, br * P:(br + 1) * P], pT[h % 2][br][j],
                                       start=False, stop=(br == 1 and j == 3))
                mm.then_inc(o_full, 1)

            scores(0)
            for h in range(8):
                if h < 7:
                    scores(h + 1)
                turn(h)
                if h >= 1:
                    values(h - 1)
            values(7)

        def copy_turned(copy, eng, h, m):
            n = 9 * h + m
            eng.wait_ge(t_full, n + 1)
            if h >= 2:
                eng.wait_ge(o_full, h - 1)
            b = bank(k, 4 + n % 2)
            if m == 8:
                return copy(pcT[h % 2][0:NCMP, :], b[0:NCMP, :])
            br, j = divmod(m, 4)
            return copy(pT[h % 2][br][j], b[:, 0:512 - j * P])

        @block.vector
        def _(dve):
            L = lambda ins: k.dve_chain.link(dve, ins)

            def lows(h):
                dve.wait_ge(slopes, 2 * (h + 1))
                if h >= 2:
                    dve.wait_ge(t_full, 9 * (h - 1))
                for u, (i, br) in enumerate(units):
                    dve.wait_ge(s_full, 9 * h + u + 1)
                    n = (i + 1) * P
                    dve.tensor_tensor_reduce(prob[h % 2][br][i], bank(k, (8 * h + u) % 3)[:, 0:n],
                                             bias_of[:, h, 384 - i * P:512], 1.0, 3e38, ALU.add, ALU.min,
                                             low[:, h, 4 * br + i:4 * br + i + 1]).then_inc(z_ready, 1)
                dve.wait_ge(s_full, 9 * (h + 1))
                dve.tensor_tensor(pcmp[h % 2][:, :, :], bank(k, 3)[:, 0:P].rearrange("p (i n) -> p i n", i=4)[:, :, 0:NCMP],
                                  bias_cmp[:, h, :].rearrange("p (i n) -> p i n", i=4), ALU.add).then_inc(zc_ready, 1)
                dve.wait_ge(zc_ready, h + 1)
                dve.tensor_reduce(low[:, h, 8:12], pcmp[h % 2][:, :, :], AX.X, ALU.min).then_inc(lc_ready, 1)

            def weigh(h):
                dve.wait_ge(e_done, 12 * (h + 1))
                L(dve.reciprocal(coef[:, h, :], tot[:, h, :]))
                gates = k.gates[:, :, 3 * h:3 * h + 3].rearrange("p i b -> p b i")
                cv = coef[:, h, :].rearrange("p (b i) -> p b i", b=3)
                L(dve.tensor_tensor(cv[:, 0:2, :], cv[:, 0:2, :], gates[:, 1:3, :], ALU.mult))
                L(dve.tensor_tensor(cv[:, 2, :], cv[:, 2, :], gates[:, 0, :], ALU.mult))
                for br in range(2):
                    for i in range(4):
                        p = prob[h % 2][br][i]
                        dve.tensor_scalar(p, p, coef[:, h, 4 * br + i:4 * br + i + 1], None, ALU.mult).then_inc(p_ready, 1)
                dve.tensor_tensor(pcmp[h % 2][:, :, :], pcmp[h % 2][:, :, :],
                                  coef[:, h, 8:12].unsqueeze(2).broadcast_to([P, 4, NCMP]), ALU.mult).then_inc(p_ready, 1)

            def turned(h):
                for m in range(9):
                    if by_vector(9 * h + m):
                        copy_turned(dve.tensor_copy, dve, h, m).then_inc(t_out_v, 1)

            lows(0)
            for h in range(8):
                if h >= 1:
                    turned(h - 1)
                weigh(h)
                if h < 7:
                    lows(h + 1)
            turned(7)

        @block.scalar
        def _(act):
            def exps(h):
                for u, (i, br) in enumerate(units):
                    act.wait_ge(z_ready, 8 * h + u + 1)
                    p, c = prob[h % 2][br][i], 4 * br + i
                    act.activation(p, p, ACT.Exp, bias=low[:, h, c:c + 1], scale=-1.0,
                                   accum_out=tot[:, h, c:c + 1]).then_inc(e_done, 1)
                act.wait_ge(lc_ready, h + 1)
                for i in range(4):
                    act.activation(pcmp[h % 2][:, i, :], pcmp[h % 2][:, i, :], ACT.Exp, bias=low[:, h, 8 + i:9 + i], scale=-1.0,
                                   accum_out=tot[:, h, 8 + i:9 + i]).then_inc(e_done, 1)

            def finish(h):
                act.wait_ge(o_full, h + 1)
                r = slice(h // 4 * 64, (h // 4 + 1) * 64)
                act.copy(k.catT[r, h % 4, :], bank(k, 6 + h % 2)[r, :]).then_inc(o_out, 1)

            exps(0)
            for h in range(8):
                if h < 7:
                    exps(h + 1)
                for m in range(9):
                    if not by_vector(9 * h + m):
                        copy_turned(act.copy, act, h, m).then_inc(t_out_a, 1)
                if h >= 1:
                    finish(h - 1)
            finish(7)


def mixed_chunks(k, w, parts):
    wv = w.rearrange("(k p) n -> p k n", p=P)
    return [lambda n, k0=k0: [(raw_slot(k, n, 2, 512)[:, :, s * 256:(s + 1) * 256], wv[:, k0:k0 + 2, c:c + 256])
                              for s, c in enumerate(parts)] for k0 in range(0, 8, 2)]


def stage_mix_in(k, a):
    k.scb, k.scc, k.prod = k.carve(0, (2, 512)), k.carve(1024, (2, 512)), k.carve(2048, (2, 516))
    k.qkv = k.carve(3080, (12, 512))
    k.zT = k.carve(9224, (4, 512))
    k.sbq, k.sbk, k.sbv = k.carve(11272, (2, 512)), k.carve(12296, (2, 512)), k.carve(13320, (4, 256))
    k.gab, k.decay_all, k.decay_row = k.carve(14344, (32,)), k.carve(14376, (8,)), k.carve(14384, (8,))
    w_ab, ab_hi, ab_lo = small_weights(k, "w_ab", 8, 8)
    raw = [k.scr(i * 516, (516,)) for i in range(2)]
    acc = [k.scr(1032 + i * 512, (512,)) for i in range(2)]
    small_in, cleared, raw_in, conv_done, ab_split = (k.sem(n) for n in (
        "mix_small_in", "mix_cleared", "mix_raw_in", "mix_conv_done", "mix_ab_split"))
    silu_done = k.sem("mix_silu_done")
    old_sq, k.sq = k.sq, k.carve(9224, (8, 512))
    first = k.ring.took
    taps = VEC_ROWS["w_gdn_conv_2"]
    CONV0 = 10
    with k.nc.Block() as block:
        @block.sync
        def _(sp):
            sp.dma_start(w_ab[:, :, :], a["w_mix_in_2"][0].rearrange("(k p) n -> p k n", p=P)[:, :, 2816:2824]).then_inc(small_in, 16)
            sp.dma_start(k.decay_row[0:1, 0:4], a["gdn_a_log_2"]).then_inc(small_in, 16)
            sp.dma_start(k.decay_row[0:1, 4:8], a["gdn_dt_bias_2"]).then_inc(small_in, 16)
            stream(k, sp, first + 28)

        @block.gpsimd
        def _(pool):
            for i in range(2):
                pool.memset(raw[i][:, 0:3], 0.0).then_inc(cleared, 1)
                pool.memset(k.prod[:, i, 0:2], 0.0).then_inc(cleared, 1)

        @block.vector
        def _(dve):
            L = lambda ins: k.dve_chain.link(dve, ins)
            x = lambda kk: k.xT[:, kk, :]
            dve.wait_ge(k.rstd_ready.sem, k.rstd_ready.at(1))
            dve_normed(k, dve, x, x, VEC_ROWS["g_final"], 512)
            dve.wait_ge(k.rstd_ready.sem, k.rstd_ready.at(2))
            dve_normed(k, dve, lambda kk: k.sq[:, kk, :], x, VEC_ROWS["w_norm_mix_2"], 512)
            dve_split(k, dve, lambda kk: k.sq[:, kk, :])
            dve.wait_ge(ab_split, 1)
            dve.tensor_tensor(ab_lo[:, :, :], w_ab[:, :, :], ab_hi[:, :, :].bitcast(F32), ALU.subtract).then_inc(ab_split, 1)
            split_lo(k, dve, first + 12)
            for i in range(2):
                dve.wait_ge(k.tile_free.sem, k.tile_free.at(5 + i))
                p = k.prod[:, i, 2:514]
                L(dve.tensor_tensor(p, p, k.scc[:, i, :], ALU.mult))
            for n in range(12):
                if n % 4 == 0:
                    split_lo(k, dve, first + 15 + n)
                dve.wait_ge(raw_in, n + 1)
                if n >= 2:
                    dve.wait_ge(silu_done, n - 1)
                dst, src = acc[n % 2], raw[n % 2]
                L(dve.tensor_scalar(dst, src[:, 3:515], k.vec(taps + 36 + n), None, ALU.mult))
                for j in (2, 1):
                    L(dve.scalar_tensor_tensor(dst, src[:, j:j + 512], k.vec(taps + 12 * j + n), dst, ALU.mult, ALU.add))
                dve.scalar_tensor_tensor(dst, src[:, 0:512], k.vec(taps + n), dst, ALU.mult, ALU.add).then_inc(conv_done, 1)
                if n % 4 == 3:
                    split_lo(k, dve, first + 13 + n)
            split_lo(k, dve, first + 32)

        @block.scalar
        def _(act):
            act_squares(k, act, lambda kk: k.xT[:, kk, :], 512)
            act_rstd(k, act, 512)
            k.sums_full.base += 1
            for kk in range(8):
                act.wait_ge(k.normed.sem, k.normed.at(kk + 1))
                act.activation(k.sq[:, kk, :], k.xT[:, kk, :], ACT.Square).then_inc(k.sq_ready.sem, 1)
            act_rstd(k, act, 512)
            k.sums_full.base -= 1
            act_split(k, act, lambda kk: k.sq[:, kk, :], 8)
            act.wait_ge(small_in, 48)
            act.copy(ab_hi[:, :, :], w_ab[:, :, :]).then_inc(ab_split, 1)
            act.wait_ge(cleared, 4)

            def silu(n):
                act.wait_ge(conv_done, n + 1)
                act.activation(k.qkv[:, n, :], acc[n % 2], ACT.Silu).then_inc(silu_done, 1)

            def read_out(t, src):
                if t < 2:
                    ins = act.copy(k.scb[:, t, :], src[:, :])
                elif t < 4:
                    ins = act.copy(k.scc[:, t - 2, :], src[:, :])
                elif t < 6:
                    ins = act.copy(k.prod[:, t - 4, 2:514], src[:, :])
                elif t < 10:
                    ins = act.copy(k.sbv[:, t - 6, :], src[:, 0:256])
                elif t < 22:
                    n = t - CONV0
                    if n >= 2:
                        act.wait_ge(conv_done, n - 1)
                    k.act_chain.link(act, act.copy(raw[n % 2][:, 3:515], src[:, :]))
                    act.sem_inc(raw_in, 1)
                    act.sem_inc(k.tile_free.sem, 1)
                    if n % 4:
                        silu(n - 1)
                    if n % 4 == 3:
                        silu(n)
                    return
                elif t < 26:
                    ins = act.activation(k.zT[:, t - 22, :], src[:, :], ACT.Silu)
                elif t < 28:
                    ins = act.mul(k.sbq[:, t - 26, :], src[:, :], 64 ** -0.5)
                elif t < 30:
                    ins = act.copy(k.sbk[:, t - 28, :], src[:, :])
                else:
                    k.act_chain.link(act, act.copy(k.decay_all[:, :], src[:, 64:72]))
                    ins = act.copy(k.gab[:, :], src[:, 0:32])
                ins.then_inc(k.tile_free.sem, 1)

            t = act_groups(k, act, first, [4, 6, 4, 4, 4, 4, 4], read_out)
            act.wait_ge(k.tile_full.sem, k.tile_full.at(t + 1))
            read_out(t, bank(k, t))

        @block.tensor
        def _(pe):
            pe_norm_sums(k, pe, 512)
            k.sq_ready.base += 8
            pe_norm_sums(k, pe, 512)
            k.sq_ready.base -= 8
            t = 0
            for group in range(7):
                tiles = [feature_tile(k, m * P) for m in range(2 if group == 1 else 4)]
                if group == 1:
                    tiles += [token_tile(k, tt, lambda w: w[:, 256:512], 256) for tt in range(4)]
                t = pe_group(k, pe, t, tiles, 0 if group == 0 else None)
            pe_used(k, pe)
            pe.wait_ge(ab_split, 2)
            pe.wait_ge(k.tile_free.sem, k.tile_free.at(t - 7))
            for tt in range(4):
                ts = slice(tt * P, (tt + 1) * P)
                for kk in range(8):
                    pe_three(k, pe, bank(k, t)[:, tt * 8:(tt + 1) * 8], (k.h_hi[:, kk, ts], k.h_lo[:, kk, ts]),
                             (ab_hi[:, kk, :], ab_lo[:, kk, :]), kk == 0, kk == 7)
            pe.matmul(bank(k, t)[:, 64:72], k.ones[0:1, :], k.decay_row[0:1, :], start=True, stop=True)\
                .then_inc(k.tile_full.sem, 1)
    k.advance(sq_ready=16, sums_full=2, rstd_ready=2, normed=16, h_rounded=8, h_ready=8, tile_full=31, tile_free=31)
    k.sq = old_sq


def stage_delta(k, a):
    H, C = 4, 4
    cq, ck, cv = k.qkv[:, 0:4, :], k.qkv[:, 4:8, :], k.qkv[:, 8:12, :]
    small = lambda i: k.carve(14408 + 16 * i, (C, H))
    g, beta, G, expG, bexp, tail, tmp = (small(i) for i in range(7))
    EG = k.scr(4096, (H, 512))
    D = k.scr(6144, (H, 512))
    LT = k.scr(8192, (H, 512))
    attn = k.scr(10240, (H, 512))
    Kb, Kbar, Vb = k.scr(12288, (H, 512)), k.scr(14336, (H, 512)), k.scr(16384, (H, 512))
    X = k.scr(18432, (H, 512))
    g_wide, beta_wide = k.scr(10240, (16, P)), k.scr(12288, (16, P))
    sqs = k.scr(14336, (8, 512))
    rs = k.scr(6144, (8, 512))
    chunk = lambda t: t.rearrange("p h (c n) -> p h c n", c=C)
    by_head = lambda t: t[:, :, :].rearrange("p c h -> p h c")
    k.last_decay = k.carve(14392, (H, C))
    conv = k.prod
    sq, nf, rd = k.sem("delta_squares"), k.sem("delta_sums"), k.sem("delta_rstd")
    gates, wide, cum = k.sem("delta_gates"), k.sem("delta_wide"), k.sem("delta_cum")

    with k.nc.Block() as block:
        @block.scalar
        def _(act):
            L = lambda ins: k.act_chain.link(act, ins)
            gab = k.gab.rearrange("p (c n) -> p c n", c=C)
            L(act.activation(beta[:, :, :], gab[:, :, 4:8], ACT.Sigmoid))
            for n in range(8):
                act.activation(sqs[:, n, :], k.qkv[:, n, :], ACT.Square).then_inc(sq, 1)
            act.wait_ge(gates, 1)
            L(act.activation(tmp[:, :, :], g[:, :, :], ACT.Abs))
            L(act.activation(tmp[:, :, :], tmp[:, :, :], ACT.Exp, scale=-1.0))
            L(act.activation(k.decay_all[:, 0:4], k.decay_all[:, 0:4], ACT.Exp))
            L(act.activation(tmp[:, :, :], tmp[:, :, :], ACT.Ln, bias=1.0))
            act.sem_inc(gates, 1)
            for n in range(8):
                act.wait_ge(nf, n + 1)
                L(act.activation(rs[:, n, :], bank(k, n)[:, :], ACT.Ln, bias=k.eps[:, 0:1]))
                act.activation(rs[:, n, :], rs[:, n, :], ACT.Exp, scale=-0.5).then_inc(rd, 1)

        @block.tensor
        def _(pe):
            for n in range(8):
                pe.wait_ge(sq, n + 1)
                pe.matmul(bank(k, n)[:, :], k.ones[:, :], sqs[:, n, :], start=True, stop=True).then_inc(nf, 1)

        @block.vector
        def _(dve):
            L = lambda ins: k.dve_chain.link(dve, ins)
            gab = k.gab.rearrange("p (c n) -> p c n", c=C)
            head_row = lambda cols: k.decay_all[:, cols:cols + 4].unsqueeze(1).broadcast_to([P, C, H])
            dve.tensor_tensor(g[:, :, :], gab[:, :, 0:4], head_row(4), ALU.add).then_inc(gates, 1)
            taps = VEC_ROWS["w_sconv_2"]
            for i in range(2):
                y = k.scc[:, i, :]
                L(dve.tensor_scalar(y, conv[:, i, 2:514], k.vec(taps + 4 + i), None, ALU.mult))
                L(dve.scalar_tensor_tensor(y, conv[:, i, 1:513], k.vec(taps + 2 + i), y, ALU.mult, ALU.add))
                L(dve.scalar_tensor_tensor(y, conv[:, i, 0:512], k.vec(taps + i), y, ALU.mult, ALU.add))
                L(dve.tensor_tensor(k.catT[:, i, :], y, k.scb[:, i, :], ALU.mult))
            dve.wait_ge(gates, 2)
            L(dve.scalar_tensor_tensor(g[:, :, :], g[:, :, :], 0.0, tmp[:, :, :], ALU.max, ALU.add))
            L(dve.scalar_tensor_tensor(g[:, :, :], g[:, :, :], -1.0, head_row(0), ALU.mult, ALU.mult))
            flat = lambda t: t[:, :, :].rearrange("p c h -> p (c h)").unsqueeze(2).broadcast_to([P, 16, P])
            ones = k.ones[:, :].unsqueeze(1).broadcast_to([P, 16, P])
            L(dve.tensor_tensor(g_wide[:, :, :], ones, flat(g), ALU.mult))
            L(dve.tensor_tensor(beta_wide[:, :, :], ones, flat(beta), ALU.mult))
            for n in range(8):
                dve.wait_ge(rd, n + 1)
                dst = k.qkv[:, n, :]
                dve.scalar_tensor_tensor(dst, dst, 128 ** -0.5 if n < 4 else 1.0, rs[:, n, :], ALU.mult, ALU.mult).then_inc(wide, 1)
            dve.wait_ge(wide, 8)

    gb, bb, st, ex, dc = (k.sem(n) for n in ("delta_G_wide", "delta_beta_wide", "delta_steps", "delta_exps", "delta_decay"))
    with k.nc.Block() as block:
        @block.tensor
        def _(pe):
            for h in range(H):
                for c in range(C):
                    mm = pe.matmul(bank(k, h)[:, c * P:(c + 1) * P], g_wide[:, c * H + h, :], k.triu[:, :], start=True, stop=True)
                mm.then_inc(gb, 1)
            pe.matmul(bank(k, 4)[:, 0:16], k.triu[:, :], g[:, :, :].rearrange("p c h -> p (c h)"), start=True, stop=True)\
                .then_inc(cum, 1)
            pe.wait_ge(st, 1)
            for h in range(H):
                for c in range(C):
                    mm = pe.matmul(bank(k, 4 + h)[:, c * P:(c + 1) * P], beta_wide[:, c * H + h, :], k.ident[:, :], start=True, stop=True)
                mm.then_inc(bb, 1)

        @block.vector
        def _(dve):
            L = lambda ins: k.dve_chain.link(dve, ins)
            dve.wait_ge(cum, 1)
            dve.tensor_copy(G[:, :, :].rearrange("p c h -> p (c h)"), bank(k, 4)[:, 0:16]).then_inc(st, 1)
            dve.wait_ge(st, 1)
            for h in range(H):
                dve.wait_ge(ex, h + 1)
                for c in range(C):
                    ins = dve.tensor_scalar(D[:, h, c * P:(c + 1) * P], bank(k, h)[:, c * P:(c + 1) * P], G[:, c, h:h + 1], 0.0,
                                            ALU.subtract, ALU.min)
                    ins.then_inc(dc, 1)
                dve.tensor_tensor(tail[:, :, h], bank(k, h)[:, P - 1:512:P], G[:, :, h], ALU.subtract).then_inc(dc, 1)
            dve.wait_ge(ex, 7)
            L(dve.tensor_tensor(bexp[:, :, :], beta[:, :, :], expG[:, :, :], ALU.mult))
            mask = lambda m: m[:, :].unsqueeze(1).broadcast_to([P, C, P])
            for h in range(H):
                L(dve.tensor_tensor(chunk(D)[:, h], chunk(D)[:, h], mask(k.triu), ALU.mult))
                dve.wait_ge(bb, h + 1)
                L(dve.tensor_tensor(LT[:, h, :], D[:, h, :], bank(k, 4 + h)[:, :], ALU.mult))
                L(dve.tensor_tensor(chunk(LT)[:, h], chunk(LT)[:, h], mask(k.triu_strict), ALU.mult))

        @block.scalar
        def _(act):
            for h in range(H):
                act.wait_ge(gb, h + 1)
                act.activation(EG[:, h, :], bank(k, h)[:, :], ACT.Exp).then_inc(ex, 1)
            act.wait_ge(st, 1)
            act.activation(expG[:, :, :], G[:, :, :], ACT.Exp).then_inc(ex, 1)
            act.wait_ge(dc, 20)
            act.activation(tail[:, :, :], tail[:, :, :], ACT.Exp).then_inc(ex, 1)
            act.activation(D[:, :, :], D[:, :, :], ACT.Exp).then_inc(ex, 1)

    turned, used, prod_f, prod_r, qe_ready = (k.sem(n) for n in ("delta_turned", "delta_turned_used", "delta_prod", "delta_prod_used", "delta_qe"))
    with k.nc.Block() as block:
        @block.tensor
        def _(pe):
            for n in range(8):
                src = (ck, cv)[n % 2][:, n // 2, :]
                if n >= 4:
                    pe.wait_ge(used, n - 3)
                for c in range(C):
                    mm = pe.transpose(bank(k, n % 4)[:, c * P:(c + 1) * P], src[:, c * P:(c + 1) * P], k.ident[:, :])
                mm.then_inc(turned, 1)
            for n in range(8):
                h = n // 2
                if n >= 4:
                    pe.wait_ge(prod_r, n - 3)
                for c in range(C):
                    cs = slice(c * P, (c + 1) * P)
                    mm = pe.matmul(bank(k, 4 + n % 4)[:, cs], ck[:, h, cs], (ck, cq)[n % 2][:, h, cs], start=True, stop=True)
                mm.then_inc(prod_f, 1)

        @block.vector
        def _(dve):
            for n in range(8):
                h = n // 2
                dve.wait_ge(turned, n + 1)
                src = bank(k, n % 4)[:, :].rearrange("p (c n) -> p c n", c=C)
                wide_of = lambda t: by_head(t)[:, h, :].unsqueeze(2).broadcast_to([P, C, P])
                if n % 2 == 0:
                    k.dve_chain.link(dve, dve.tensor_tensor(chunk(Kbar)[:, h], src, wide_of(tail), ALU.mult))
                    dve.tensor_tensor(chunk(Kb)[:, h], src, wide_of(bexp), ALU.mult).then_inc(used, 1)
                else:
                    dve.tensor_tensor(chunk(Vb)[:, h], src, wide_of(beta), ALU.mult).then_inc(used, 1)
            for n in range(8):
                h = n // 2
                dve.wait_ge(prod_f, n + 1)
                dst, w = (LT, LT) if n % 2 == 0 else (attn, D)
                dve.tensor_tensor(dst[:, h, :], bank(k, 4 + n % 4)[:, :], w[:, h, :], ALU.mult).then_inc(prod_r, 1)

        @block.gpsimd
        def _(pool):
            k.pool_chain.link(pool, pool.tensor_copy(k.last_decay[:, :, :], EG[:, :, P - 1:512:P]))
            for h in range(H):
                pool.tensor_tensor(EG[:, h, :], EG[:, h, :], cq[:, h, :], ALU.mult).then_inc(qe_ready, 1)
            pool.wait_ge(qe_ready, H)

    R = cv
    Y = k.carve(3080, (H, 512))
    Lm = k.scr(6144, (4, 512))
    lm, yf, yr, xf, xr, rf, rr = (k.sem(n) for n in ("inv_masked", "inv_y", "inv_y_out", "inv_x", "inv_x_out", "inv_r", "inv_r_out"))
    eye = k.sem("inv_eye")
    with k.nc.Block() as block:
        @block.gpsimd
        def _(pool):
            mask = lambda lv: k.level[:, lv, :].unsqueeze(1).broadcast_to([P, C, P])
            for lv in range(7):
                for h in range(H):
                    n = lv * H + h
                    if n >= 4:
                        pool.wait_ge(yf, n - 3)
                    pool.tensor_tensor(chunk(Lm)[:, n % 4], chunk(LT)[:, h], mask(lv), ALU.mult).then_inc(lm, 1)

        @block.tensor
        def _(pe):
            blocks = [slice(c * P, (c + 1) * P) for c in range(C)]
            pe.wait_ge(eye, 8)
            for lv in range(7):
                def first(h):
                    n = lv * H + h
                    pe.wait_ge(lm, n + 1)
                    if lv:
                        pe.wait_ge(xr, (lv - 1) * H + h + 1)
                    if n >= 2:
                        pe.wait_ge(yr, n - 1)
                    for cs in blocks:
                        mm = pe.matmul(bank(k, n % 2)[:, cs], Lm[:, n % 4, cs], X[:, h, cs], start=True, stop=True)
                    mm.then_inc(yf, 1)

                def second(h):
                    n = lv * H + h
                    pe.wait_ge(yr, n + 1)
                    if lv:
                        pe.wait_ge(rr, (lv - 1) * H + h + 1)
                    if n >= 2:
                        pe.wait_ge(rr, n - 1)
                    if lv < 6:
                        if n >= 2:
                            pe.wait_ge(xr, n - 1)
                        for cs in blocks:
                            mm = pe.matmul(bank(k, 2 + n % 2)[:, cs], R[:, h, cs], Y[:, h, cs], start=True, stop=True)
                        mm.then_inc(xf, 1)
                    for cs in blocks:
                        mm = pe.matmul(bank(k, 4 + n % 2)[:, cs], Y[:, h, cs], R[:, h, cs], start=True, stop=True)
                    mm.then_inc(rf, 1)

                first(0)
                for h in range(H):
                    if h < 3:
                        first(h + 1)
                    second(h)

        @block.scalar
        def _(act):
            for n in range(7 * H):
                act.wait_ge(yf, n + 1)
                if n >= H:
                    act.wait_ge(rf, n - H + 1)
                act.copy(Y[:, n % H, :], bank(k, n % 2)[:, :]).then_inc(yr, 1)

        @block.vector
        def _(dve):
            eyes = k.ident[:, :].unsqueeze(1).broadcast_to([P, C, P])
            for h in range(H):
                dve.tensor_copy(chunk(X)[:, h], eyes).then_inc(eye, 1)
                dve.tensor_copy(chunk(R)[:, h], eyes).then_inc(eye, 1)
            dve.wait_ge(eye, 8)
            for n in range(7 * H):
                h = n % H
                if n < 6 * H:
                    dve.wait_ge(xf, n + 1)
                    if n >= H:
                        dve.wait_ge(xr, n - H + 1)
                    dve.tensor_tensor(X[:, h, :], X[:, h, :], bank(k, 2 + n % 2)[:, :], ALU.subtract).then_inc(xr, 1)
                dve.wait_ge(rf, n + 1)
                if n >= H:
                    dve.wait_ge(rr, n - H + 1)
                dve.tensor_tensor(R[:, h, :], R[:, h, :], bank(k, 4 + n % 2)[:, :], ALU.subtract).then_inc(rr, 1)

    S = [k.carve(5128 + i * 512, (H, P)) for i in range(2)]
    vn = [k.carve(6152 + i * 512, (H, P)) for i in range(2)]
    uw, uo = k.sem("delta_uw"), k.sem("delta_uw_out")
    with k.nc.Block() as block:
        @block.tensor
        def _(pe):
            for n in range(8):
                h = n // 2
                for c in range(C):
                    cs = slice(c * P, (c + 1) * P)
                    l, r = (R, Vb) if n % 2 == 0 else (Kb, R)
                    mm = pe.matmul(bank(k, n)[:, cs], l[:, h, cs], r[:, h, cs], start=True, stop=True)
                mm.then_inc(uw, 1)

        @block.scalar
        def _(act):
            for n in range(1, 8, 2):
                act.wait_ge(uw, n + 1)
                act.copy(Kb[:, n // 2, :], bank(k, n)[:, :]).then_inc(uo, 1)

        @block.vector
        def _(dve):
            for n in range(0, 8, 2):
                dve.wait_ge(uw, n + 1)
                dve.tensor_copy(Vb[:, n // 2, :], bank(k, n)[:, :]).then_inc(uo, 1)

    ws, vr, of, df, sr = (k.sem(n) for n in ("delta_ws", "delta_v_new", "delta_out", "delta_update", "delta_state"))
    o_sq, o_nf, o_rd, o_cp = (k.sem(n) for n in ("delta_out_sq", "delta_out_sums", "delta_out_rstd", "delta_out_copied"))
    o_sb, osq, rstd = k.scr(6144, (H, 512)), k.scr(8192, (H, 512)), k.scr(18432, (H, 512))
    with k.nc.Block() as block:
        @block.tensor
        def _(pe):
            for c in range(C):
                cs = slice(c * P, (c + 1) * P)
                s = S[(c - 1) % 2]
                if c:
                    pe.wait_ge(sr, c)
                    for h in range(H):
                        mm = pe.matmul(bank(k, 4)[:, h * P:(h + 1) * P], Kb[:, h, cs], s[:, h, :], start=True, stop=True)
                    mm.then_inc(ws, 1)
                    for h in range(H):
                        pe.matmul(bank(k, h)[:, cs], s[:, h, :], EG[:, h, cs], start=True, stop=False)
                pe.wait_ge(vr, c + 1)
                if c < C - 1:
                    for h in range(H):
                        mm = pe.matmul(bank(k, 5)[:, h * P:(h + 1) * P], Kbar[:, h, cs], vn[c % 2][:, h, :], start=True, stop=True)
                    mm.then_inc(df, 1)
                for h in range(H):
                    mm = pe.matmul(bank(k, h)[:, cs], vn[c % 2][:, h, :], attn[:, h, cs], start=(c == 0), stop=True)
            mm.then_inc(of, 1)
            for h in range(H):
                pe.wait_ge(o_sq, h + 1)
                pe.matmul(bank(k, 4 + h)[:, :], k.ones[:, :], osq[:, h, :], start=True, stop=True).then_inc(o_nf, 1)

        @block.vector
        def _(dve):
            L = lambda ins: k.dve_chain.link(dve, ins)
            for c in range(C):
                u = chunk(Vb)[:, :, c, :]
                if c == 0:
                    dve.tensor_copy(vn[0][:, :, :], u).then_inc(vr, 1)
                else:
                    dve.wait_ge(ws, c)
                    dve.tensor_tensor(vn[c % 2][:, :, :], u, bank(k, 4)[:, :].rearrange("p (h n) -> p h n", h=H), ALU.subtract)\
                        .then_inc(vr, 1)
                if c < C - 1:
                    dve.wait_ge(df, c + 1)
                    d = bank(k, 5)[:, :].rearrange("p (h n) -> p h n", h=H)
                    if c == 0:
                        dve.tensor_copy(S[0][:, :, :], d).then_inc(sr, 1)
                    else:
                        L(dve.tensor_tensor(S[c % 2][:, :, :], S[(c - 1) % 2][:, :, :],
                                            k.last_decay[:, :, c].unsqueeze(2).broadcast_to([P, H, P]), ALU.mult))
                        dve.tensor_tensor(S[c % 2][:, :, :], S[c % 2][:, :, :], d, ALU.add).then_inc(sr, 1)
            for h in range(H):
                dve.wait_ge(o_rd, h + 1)
                L(dve.scalar_tensor_tensor(o_sb[:, h, :], o_sb[:, h, :], k.vec(VEC_ROWS["w_gdn_norm_2"]), rstd[:, h, :],
                                           ALU.mult, ALU.mult))
                L(dve.tensor_tensor(k.catT[:, 2 + h, :], o_sb[:, h, :], k.zT[:, h, :], ALU.mult))

        @block.scalar
        def _(act):
            act.wait_ge(of, 1)
            for h in range(H):
                act.copy(o_sb[:, h, :], bank(k, h)[:, :]).then_inc(o_cp, 1)
                act.activation(osq[:, h, :], bank(k, h)[:, :], ACT.Square).then_inc(o_sq, 1)
            act.wait_ge(o_cp, 4)
            for h in range(H):
                act.wait_ge(o_nf, h + 1)
                k.act_chain.link(act, act.activation(rstd[:, h, :], bank(k, 4 + h)[:, :], ACT.Ln, bias=k.eps[:, 0:1], scale=1.0 / P))
            for h in range(H):
                act.activation(rstd[:, h, :], rstd[:, h, :], ACT.Exp, scale=-0.5).then_inc(o_rd, 1)


def stage_stick(k):
    z = [[k.scr(4096 + par * 2560 + off, (512 - j * P,)) for j, off in enumerate((0, 512, 896, 1152))] for par in range(2)]
    sp_ = [[k.scr(5376 + par * 2560 + off, (512 - j * P,)) for j, off in enumerate((0, 512, 896, 1152))] for par in range(2)]
    zf, zc, zl, spr, tf, wr, ar, am, of, oc = (k.sem(n) for n in (
        "stick_z", "stick_z_copied", "stick_logs", "stick_softplus", "stick_tail", "stick_exponent", "stick_exp", "stick_masked",
        "stick_full", "stick_out"))
    with k.nc.Block() as block:
        @block.tensor
        def _(pe):
            def scores(h):
                r = slice(h % 2 * 64, h % 2 * 64 + 64)
                for m, j in enumerate((3, 2, 1, 0)):
                    n = 4 * h + m
                    if n >= 2:
                        pe.wait_ge(spr, n - 1)
                    pe.matmul(bank(k, n % 2)[:, 0:512 - j * P], k.sbk[r, h // 2, j * P:(j + 1) * P], k.sbq[r, h // 2, j * P:512],
                              start=True, stop=True).then_inc(zf, 1)

            def tails(h):
                for m, j in enumerate((3, 2, 1, 0)):
                    n = 4 * h + m
                    pe.wait_ge(spr, n + 1)
                    if n >= 2:
                        pe.wait_ge(wr, n - 1)
                    b = bank(k, 2 + n % 2)
                    mm = pe.matmul(b[:, 0:512 - j * P], k.tril[:, :], sp_[h % 2][j], start=True, stop=(j == 3))
                    for jj in range(j + 1, 4):
                        mm = pe.matmul(b[:, (jj - j) * P:512 - j * P], k.ones[:, :], sp_[h % 2][jj], start=False, stop=(jj == 3))
                    mm.then_inc(tf, 1)

            def values(h):
                if h >= 2:
                    pe.wait_ge(oc, h - 1)
                pe.wait_ge(am, 4 * (h + 1))
                for j in range(4):
                    mm = pe.matmul(bank(k, 4 + h % 2)[:, j * P:512], k.sbv[:, j, (h // 2) * P:(h // 2 + 1) * P], z[h % 2][j],
                                   start=(j == 0), stop=(j == 3))
                mm.then_inc(of, 1)

            scores(0)
            for h in range(4):
                if h < 3:
                    scores(h + 1)
                tails(h)
                values(h)

        @block.scalar
        def _(act):
            L = lambda ins: k.act_chain.link(act, ins)

            def logs(h):
                if h >= 2:
                    act.wait_ge(of, h - 1)
                for m, j in enumerate((3, 2, 1, 0)):
                    n = 4 * h + m
                    act.wait_ge(zf, n + 1)
                    src, s = bank(k, n % 2)[:, 0:512 - j * P], sp_[h % 2][j]
                    act.copy(z[h % 2][j], src).then_inc(zc, 1)
                    L(act.activation(s, src, ACT.Abs))
                    L(act.activation(s, s, ACT.Exp, scale=-1.0))
                    act.activation(s, s, ACT.Ln, bias=1.0).then_inc(zl, 1)

            value = lambda kk: k.catT[:, kk, :]
            logs(0)
            act_split(k, act, value, None, tiles=range(6))
            for h in range(4):
                if h < 3:
                    logs(h + 1)
                for m, j in enumerate((3, 2, 1, 0)):
                    act.wait_ge(wr, 4 * h + m + 1)
                    act.activation(z[h % 2][j], z[h % 2][j], ACT.Exp).then_inc(ar, 1)
                act.wait_ge(of, h + 1)
                r = slice(h % 2 * 64, h % 2 * 64 + 64)
                act.copy(k.catT[r, 6 + h // 2, :], bank(k, 4 + h % 2)[r, :]).then_inc(oc, 1)
                if h % 2:
                    act.wait_ge(oc, h + 1)
                    act_split(k, act, value, None, tiles=[6 + h // 2])

        @block.vector
        def _(dve):
            L = lambda ins: k.dve_chain.link(dve, ins)

            def softplus(h):
                for m, j in enumerate((3, 2, 1, 0)):
                    n = 4 * h + m
                    dve.wait_ge(zl, n + 1)
                    s = sp_[h % 2][j]
                    L(dve.scalar_tensor_tensor(s, bank(k, n % 2)[:, 0:512 - j * P], 0.0, s, ALU.max, ALU.add))
                    dve.tensor_tensor(s[:, 0:P], s[:, 0:P], k.triu_strict[:, :], ALU.mult).then_inc(spr, 1)

            def exponents(h):
                for m, j in enumerate((3, 2, 1, 0)):
                    n = 4 * h + m
                    dve.wait_ge(tf, n + 1)
                    dve.wait_ge(zc, n + 1)
                    w = z[h % 2][j]
                    L(dve.tensor_tensor(w, w, bank(k, 2 + n % 2)[:, 0:512 - j * P], ALU.subtract))
                    dve.tensor_scalar(w[:, 0:P], w[:, 0:P], 0.0, None, ALU.min).then_inc(wr, 1)

            def mask(h):
                for m, j in enumerate((3, 2, 1, 0)):
                    dve.wait_ge(ar, 4 * h + m + 1)
                    w = z[h % 2][j][:, 0:P]
                    dve.tensor_tensor(w, w, k.triu_strict[:, :], ALU.mult).then_inc(am, 1)

            value = lambda kk: k.catT[:, kk, :]
            softplus(0)
            dve_split(k, dve, value, 0, tiles=range(6))
            for h in range(4):
                if h < 3:
                    softplus(h + 1)
                exponents(h)
                mask(h)
                if h == 2:
                    dve_split(k, dve, value, 6, tiles=[6])
            dve_split(k, dve, value, 7, tiles=[7])
    k.advance(h_rounded=8, h_ready=8)


def stage_final(k, out):
    rows = k.carve(4096, (4, 1024))
    turned, copied, stored = k.sem("final_turned"), k.sem("final_copied"), k.sem("final_stored")
    with k.nc.Block() as block:
        @block.scalar
        def _(act):
            act_squares(k, act, lambda kk: k.xT[:, kk, :], 512)
            act_rstd(k, act, 512)
            for n in range(8):
                act.wait_ge(turned, n + 1)
                act.copy(rows[:, n // 2, (n % 2) * 512:(n % 2 + 1) * 512], bank(k, n)[:, :]).then_inc(copied, 1)

        @block.vector
        def _(dve):
            dve.wait_ge(k.rstd_ready.sem, k.rstd_ready.at(1))
            dve_normed(k, dve, lambda kk: k.sq[:, kk, :], lambda kk: k.xT[:, kk, :], VEC_ROWS["w_norm_final_2"], 512)

        @block.tensor
        def _(pe):
            pe_norm_sums(k, pe, 512)
            for n in range(8):
                pe.wait_ge(k.normed.sem, k.normed.at(4 * (n % 2 + 1)))
                for m in range(4):
                    kk = (n % 2) * 4 + m
                    mm = pe.transpose(bank(k, n)[:, m * P:(m + 1) * P], k.sq[:, kk, (n // 2) * P:(n // 2 + 1) * P], k.ident[:, :])
                mm.then_inc(turned, 1)

        @block.sync
        def _(sp):
            for n in range(8):
                sp.wait_ge(copied, n + 1)
                half = slice((n % 2) * 512, (n % 2 + 1) * 512)
                sp.dma_start(out[0, (n // 2) * P:(n // 2 + 1) * P, half], rows[:, n // 2, half]).then_inc(stored, 16)
            sp.wait_ge(stored, 128)


KEEP = 15400
DENSE_SCRATCH = 2100
MIXER_SCRATCH = 21600


def program(k, a, out):
    conv = lambda name: (lambda j: VEC_ROWS[name] + j * FT)

    def plain(*args):
        c = chunks_of(k, *args)
        return c, [1] * len(c)

    def counted(c, n):
        return c, [n] * len(c)

    def paired_out(w):
        return [x for cols in (0, 512) for x in (counted(paired_out_chunks(k, w, cols), 2),
                                                 counted(chunks_of(k, w, cols)[2:], 1))]

    w_mem, w_in, w_mix = a["w_mem_kv"], a["a_w_in"][0], a["w_mix_in_2"][0]
    return [
        (True, [plain(w_mem[l], cols) for l in range(2) for cols in (0, 512)] +
               [plain(w_in, cols) for cols in (0, 512, 1024, 1552)],
         [lambda: stage_setup(k, a), lambda: stage_memory(k, a), lambda: stage_gla_in(k, a)]),
        (False, [], [lambda: stage_gla(k, a), lambda: stage_mem_attention(k, 0)]),
        (True, [plain(a["a_w_out"][0], cols) for cols in (0, 512)] + [ffn_chunks(k, a["w_up"][0], a["w_down"][0])] +
               [counted(kv_chunks(k, a["w_kv"]), 4), plain(a["w_kv"], 256), plain(a["w_ck1"], 0, 256, 4),
                plain(a["w_cv1"], 0, 256, 4), counted(paired_query_chunks(k, a["b_w_in"][0]), 4),
                plain(a["b_w_in"][0], 536)],
         [lambda: stage_out_projection(k),
          lambda: stage_ffn(k, a["w_up"][0], VEC_ROWS["g_ffn0"], conv("conv_w0"), VEC_ROWS["conv_b0"], False),
          lambda: stage_nsa_in(k, a)]),
        (False, [], [lambda: stage_nsa(k), lambda: stage_mem_attention(k, 1)]),
        (True, paired_out(a["b_w_out"][0]) + [ffn_chunks(k, a["w_up"][1], a["w_down"][1])] +
               [plain(w_mix, 0), counted(mixed_chunks(k, w_mix, (512, 3336)), 2)] +
               [plain(w_mix, cols) for cols in (768, 1280, 1792, 2304, 2824)],
         [lambda: stage_out_projection(k),
          lambda: stage_ffn(k, a["w_up"][1], VEC_ROWS["g_ffn1"], conv("conv_w1"), VEC_ROWS["conv_b1"], False),
          lambda: stage_mix_in(k, a)]),
        (False, [], [lambda: stage_delta(k, a), lambda: stage_stick(k)]),
        (True, [plain(a["w_mix_out_2"][0], cols) for cols in (0, 512)] +
               [ffn_chunks(k, a["w_ffn_up_2"][0], a["w_ffn_down_2"][0])],
         [lambda: stage_out_projection(k),
          lambda: stage_ffn(k, a["w_ffn_up_2"][0], VEC_ROWS["w_norm_ffn_2"], lambda j: VEC_ROWS[f"ffn_conv2_{j}"], None, True),
          lambda: stage_final(k, out)]),
    ]


def build(nc, a, out, until=99, debug=None):
    k = K()
    k.nc = nc
    ctx = ExitStack()
    with ctx:
        def sb(name, shape, dt=F32):
            return ctx.enter_context(nc.sbuf_tensor(name, shape, dt))

        k.sem = lambda name: ctx.enter_context(nc.semaphore(name))
        k.xT = sb("xT", [P, 8, 512])
        k.h_hi, k.h_lo = sb("h_hi", [P, 8, 512], F32R), sb("h_lo", [P, 8, 512], F32R)
        k.vecs = sb("vecs", [P, VEC_TILES * P])
        k.ident, k.ones, k.triu, k.triu_strict, k.tril = (sb(n, [P, P]) for n in ("ident", "ones", "triu", "triu_strict", "tril"))
        k.level = sb("level", [P, 7, P])
        k.eps, k.valid = sb("eps", [P, 1]), sb("valid", [P, 1])
        k.rstd = sb("rstd", [P, 512])
        k.dist, k.dist_cmp = sb("dist", [P, 512]), sb("dist_cmp", [P, 4 * 31])
        k.keep = sb("keep", [P, KEEP])
        k.psum = [ctx.enter_context(nc.psum_tensor(f"bank{i}", [P, 512], F32)) for i in range(8)]
        k.vec = lambda c: k.vecs[:, c:c + 1]

        def carved(tensor, size, at, shape):
            n = 1
            for s in shape:
                n *= s
            assert at + n <= size, (at, shape)
            ap = tensor[:, at:at + n]
            if len(shape) == 2:
                return ap.rearrange("p (a b) -> p a b", a=shape[0])
            if len(shape) == 3:
                return ap.rearrange("p (a b c) -> p a b c", a=shape[0], b=shape[1])
            return ap

        k.carve = lambda at, shape: carved(k.keep, KEEP, at, shape)
        k.sq = k.carve(0, (8, 512))
        k.mkT = k.carve(KEEP - 4096, (2, 4, 256))
        k.mv = k.carve(KEEP - 2048, (2, 2, 512))
        k.memT = k.carve(9216, (8, 256))
        k.ma = 4096
        signals = {name: Signal(k.sem(name)) for name in
                   ("tile_full", "tile_free", "sq_ready", "sums_full", "rstd_ready", "normed", "h_rounded", "h_ready")}
        k.tile_full, k.tile_free = signals["tile_full"], signals["tile_free"]
        k.sq_ready, k.sums_full, k.rstd_ready = signals["sq_ready"], signals["sums_full"], signals["rstd_ready"]
        k.normed, k.h_rounded, k.h_ready = signals["normed"], signals["h_rounded"], signals["h_ready"]
        k.ma_sig = [Signal(k.sem("mem_" + n)) for n in ("scores", "lows", "exps", "probs", "turned", "turned_out", "full", "out")]
        k.ffn_sig = [Signal(k.sem("ffn_" + n)) for n in
                     ("padded", "conv_a", "conv_b", "silu", "done", "cleared", "product_hi", "product_lo")]

        def advance(**counts):
            for name, n in counts.items():
                signals[name].base += n

        k.advance = advance
        k.dve_chain, k.act_chain, k.pool_chain = (Chain(k.sem(n)) for n in ("vector_order", "scalar_order", "pool_order"))
        phases = program(k, a, out)
        k.plan, loads, ends = [], [], []
        for _, groups, _ in phases:
            for chunks, counts in groups:
                k.plan.extend(chunks)
                loads.extend(counts)
            ends.append(len(k.plan))
        k.ring = Ring([k.sem(f"weights_in{i}") for i in range(RING)], k.sem("weights_hi"), k.sem("weights_lo"),
                      k.sem("weights_used"), loads)
        ran = 0
        for number, (dense, _, stages) in enumerate(phases):
            k.phase_end = ends[number]
            with ExitStack() as phase:
                k.scope = lambda name, shape, dt: phase.enter_context(nc.sbuf_tensor(f"{name}_{number}", shape, dt))
                if dense:
                    k.raw = [k.scope(f"raw{i}", [P, SLOT], F32) for i in range(RING)]
                    k.w_hi = [k.scope(f"w_hi{i}", [P, SLOT], F32R) for i in range(RING)]
                    k.w_lo = [k.scope(f"w_lo{i}", [P, SLOT], F32R) for i in range(RING)]
                size = DENSE_SCRATCH if dense else MIXER_SCRATCH
                scratch = k.scope("scratch", [P, size], F32)
                k.scr = lambda at, shape: carved(scratch, size, at, shape)
                if not dense:
                    k.catT = k.scr(0, (8, 512))
                for stage in stages:
                    if ran < until:
                        stage()
                    ran += 1
                if debug and ran >= until:
                    debug(k, ctx)
                    debug = None
                    until = 0


_INS = ['x', 'mem', 'g_mix', 'g_ffn', 'g_mem', 'w_mem_kv', 'w_up', 'conv_w', 'conv_b', 'w_down', 'a_w_in', 'a_w_alpha',
        'a_b_alpha', 'a_g_head', 'a_w_out', 'g_kv', 'w_kv', 'pe_k', 'pe_v', 'w_ck1', 'w_ck2', 'w_cv1', 'w_cv2', 'b_w_in',
        'b_w_out', 'g_final', 'w_norm_mix_2', 'w_mix_in_2', 'w_sconv_2', 'w_gdn_conv_2', 'gdn_a_log_2', 'gdn_dt_bias_2',
        'w_gdn_norm_2', 'w_mix_out_2', 'w_norm_ffn_2', 'w_ffn_up_2', 'w_ffn_conv_2', 'w_ffn_down_2', 'w_norm_final_2']
_OUT = ((1, 512, 1024), 'float32')


def kernel(**inputs):
    import numpy as _np
    import concourse.bacc as _bacc
    from concourse import mybir as _mybir
    from concourse.bass_utils import run_bass_kernel_spmd as _run

    nc = _bacc.Bacc("TRN2", target_bir_lowering=False, num_devices=1)
    arrays, args = {}, {}
    for name in _INS:
        v = _np.ascontiguousarray(inputs[name])
        arrays[f"in_{name}"] = v
        args[name] = nc.dram_tensor(f"in_{name}", v.shape, _mybir.dt.from_np(v.dtype), kind="ExternalInput").ap()
    out = nc.dram_tensor("out", _OUT[0], _mybir.dt.from_np(_np.dtype(_OUT[1])), kind="ExternalOutput").ap()
    build(nc, args, out)
    r = _run(nc, [arrays], core_ids=[0])
    return r.results[0]["out"]
```

```python
from contextlib import ExitStack

import concourse.bass as bass
from concourse import mybir

F32 = mybir.dt.float32
F32R = mybir.dt.float32r
I32 = mybir.dt.int32
ALU = mybir.AluOpType
ACT = mybir.ActivationFunctionType
AX = mybir.AxisListType

P = 128
RING = 4
SLOT = 1024
BIG = 1e30


class Signal:

    def __init__(self, sem):
        self.sem = sem
        self.base = 0

    def at(self, n):
        return self.base + n


class Chain:

    def __init__(self, sem):
        self.sem = sem
        self.n = 0
        self.reg = None
        self.per = 0

    def link(self, eng, ins):
        self.n += 1
        ins.then_inc(self.sem, 1)
        eng.wait_ge(self.sem, self.n if self.reg is None else self.n + self.reg * self.per)


class Ring:

    def __init__(self, landed, hi, lo, used, loads):
        self.landed = landed
        self.hi = hi
        self.lo = lo
        self.used = used
        self.loads = loads
        self.out = 0
        self.hi_at = 0
        self.lo_at = 0
        self.took = 0
        self.owed = 0

    def full(self, n):
        return 16 * sum(self.loads[m] for m in range(n % RING, n + 1, RING))


class K:
    pass


def bank(k, i):
    return k.psum[i % 8]


def plus(count, reg, per):
    return count if reg is None else reg * per + count


def load_chunk(k, sp, n, pieces, reg=None, per=8):
    r = k.ring
    if n >= RING:
        sp.wait_ge(r.lo, plus(n - RING + 1, reg, per))
    for dst, src in pieces:
        sp.dma_start(dst, src).then_inc(r.landed[n % RING], 16)


def raw_slot(k, n, kt, cols):
    return k.raw[n % RING][:, :].rearrange("p (k n) -> p k n", k=kt)


def parts(k, n, kt):
    return [w[n % RING][:, :].rearrange("p (k n) -> p k n", k=kt) for w in (k.w_hi, k.w_lo)]


def chunks_of(k, w, cols, width=512, kt=2):
    wv = w.rearrange("(k p) n -> p k n", p=P)
    return [lambda n, k0=k0: [(raw_slot(k, n, kt, width)[:, :, :], wv[:, k0:k0 + kt, cols:cols + width])]
            for k0 in range(0, w.shape[0] // P, kt)]


def stream(k, sp, upto):
    end = min(upto + RING, k.phase_end)
    while k.ring.out < end:
        n = k.ring.out
        load_chunk(k, sp, n, k.plan[n](n))
        k.ring.out += 1


def split_hi_chunk(k, act, n, reg=None, loads=2, per=8):
    r = k.ring
    act.wait_ge(r.landed[n % RING], plus(r.full(n), reg, 16 * loads * per // RING))
    if n >= RING:
        act.wait_ge(r.used, plus(n - RING + 1, reg, per))
    act.copy(k.w_hi[n % RING][:, :], k.raw[n % RING][:, :]).then_inc(r.hi, 1)


def split_lo_chunk(k, dve, n, reg=None, per=8):
    r = k.ring
    dve.wait_ge(r.hi, plus(n + 1, reg, per))
    dve.tensor_tensor(k.w_lo[n % RING][:, :], k.raw[n % RING][:, :], k.w_hi[n % RING][:, :].bitcast(F32), ALU.subtract)\
        .then_inc(r.lo, 1)


def split_hi(k, act, upto):
    while k.ring.hi_at < min(upto, k.phase_end):
        split_hi_chunk(k, act, k.ring.hi_at)
        k.ring.hi_at += 1


def split_lo(k, dve, upto):
    while k.ring.lo_at < min(upto, k.phase_end):
        split_lo_chunk(k, dve, k.ring.lo_at)
        k.ring.lo_at += 1


def pe_warm(k, pe, count, b=7):
    for _ in range(count):
        pe.matmul(bank(k, b)[:, :], k.ident[:, :], k.level[:, 0:4, :].rearrange("p a n -> p (a n)"), start=True, stop=True)


def pe_used(k, pe):
    if k.ring.owed:
        pe.drain().then_inc(k.ring.used, k.ring.owed)
        k.ring.owed = 0


def pe_three(k, pe, out, stat, mov, first, last):
    (sh, sl), (mh, ml) = stat, mov
    a = pe.matmul(out, sh, mh, start=first, stop=False)
    pe.matmul(out, sh, ml, start=False, stop=False)
    c = pe.matmul(out, sl, mh, start=False, stop=last)
    return a, c


def pe_chunk(k, pe, n, tiles, rows, total, reg=None, per=8, before=None):
    pe.wait_ge(k.ring.lo, plus(n + 1, reg, per))
    w = parts(k, n, len(rows))
    steps = [(r, i) for r in range(len(rows)) for i in range(len(tiles))]
    if rows[-1] == total - 1:
        steps = [(r, i) for i in range(len(tiles)) for r in range(len(rows))]
    for r, i in steps:
        kk, (out, operands) = rows[r], tiles[i]
        if before is not None:
            before(i, kk)
        stat, mov = operands(kk, [x[:, r, :] for x in w])
        a, c = pe_three(k, pe, out, stat, mov, kk == 0, kk == total - 1)
        if r == 0 and i == 0 and k.ring.owed:
            a.then_inc(k.ring.used, k.ring.owed)
        if kk == total - 1:
            c.then_inc(k.tile_full.sem, 1)
    k.ring.owed = 1


def pe_group(k, pe, t, tiles, h_from=None):
    def before(i, kk):
        if kk == 0 and t + i >= 8:
            pe.wait_ge(k.tile_free.sem, k.tile_free.at(t + i - 7))
        if h_from is not None and i == 0:
            pe.wait_ge(k.h_ready.sem, k.h_ready.at(h_from + kk + 1))

    outs = [(out(bank(k, t + i)), operands) for i, (out, operands) in enumerate(tiles)]
    for c in range(4):
        n = k.ring.took
        k.ring.took += 1
        pe_chunk(k, pe, n, outs, [2 * c, 2 * c + 1], 8, before=before)
    return t + len(tiles)


def feature_tile(k, c0, tokens=slice(0, 512)):
    n = tokens.stop - tokens.start
    return (lambda b: b[:, 0:n],
            lambda kk, w: ([x[:, c0:c0 + P] for x in w], [k.h_hi[:, kk, tokens], k.h_lo[:, kk, tokens]]))


def token_tile(k, tt, view, width, at=0):
    ts = slice(at + tt * P, at + (tt + 1) * P)
    return (lambda b: b[:, 0:width],
            lambda kk, w: ([k.h_hi[:, kk, ts], k.h_lo[:, kk, ts]], [view(x) for x in w]))


def act_squares(k, act, src, n, dim=1024):
    for kk in range(8):
        act.activation(k.sq[:, kk, 0:n], src(kk), ACT.Square, scale=dim ** -0.5).then_inc(k.sq_ready.sem, 1)


def act_load_ln(k, act):
    k.act_chain.link(act, act.activation(k.spare[:, 0:1], k.eps[:, 0:1], ACT.Ln))


def act_new_squares(k, act, tiles):
    for kk in tiles:
        act.wait_ge(k.tile_free.sem, k.tile_free.at(kk + 1))
        act.activation(k.sq[:, kk, :], k.xT[:, kk, :], ACT.Square, scale=1024 ** -0.5).then_inc(k.sq_ready.sem, 1)


def pool_new_sums(k, pool):
    for kk in range(1, 6):
        pool.wait_ge(k.sq_ready.sem, k.sq_ready.at(kk + 1))
        ins = pool.tensor_tensor(k.sq[:, 0, :], k.sq[:, 0, :], k.sq[:, kk, :], ALU.add)
        if kk < 5:
            k.pool_chain.link(pool, ins)
    ins.then_inc(k.sq_added.sem, 1)


def pe_new_sums(k, pe):
    pe.wait_ge(k.sq_added.sem, k.sq_added.at(1))
    pe.matmul(bank(k, 0)[:, :], k.ones[:, :], k.sq[:, 0, :], start=True, stop=False)
    for kk in (6, 7):
        pe.wait_ge(k.sq_ready.sem, k.sq_ready.at(kk + 1))
        mm = pe.matmul(bank(k, 0)[:, :], k.ones[:, :], k.sq[:, kk, :], start=False, stop=(kk == 7))
    mm.then_inc(k.sums_full.sem, 1)


def pe_norm_sums(k, pe, n=512, tiles=range(8), b=0):
    for kk in tiles:
        pe.wait_ge(k.sq_ready.sem, k.sq_ready.at(kk + 1))
        mm = pe.matmul(bank(k, b)[:, 0:n], k.ones[:, :], k.sq[:, kk, 0:n], start=(kk == 0), stop=(kk == 7))
        if kk == 7:
            mm.then_inc(k.sums_full.sem, 1)


def act_rstd(k, act, n=512, b=0):
    act.wait_ge(k.sums_full.sem, k.sums_full.at(1))
    k.act_chain.link(act, act.activation(k.rstd[:, 0:n], bank(k, b)[:, 0:n], ACT.Ln, bias=k.eps[:, 0:1]))
    act.activation(k.rstd[:, 0:n], k.rstd[:, 0:n], ACT.Exp, scale=-0.5).then_inc(k.rstd_ready.sem, 1)


def dve_normed(k, dve, dst, src, gain, n, split_at=None, tokens=slice(0, 512)):
    for kk in range(8):
        dve.scalar_tensor_tensor(dst(kk), src(kk), k.vec(gain + kk), k.rstd[:, 0:n], ALU.mult, ALU.mult)\
            .then_inc(k.normed.sem, 1)
        if split_at is not None and kk:
            dve_split(k, dve, dst, split_at + kk - 1, tokens, [kk - 1])
    if split_at is not None:
        dve_split(k, dve, dst, split_at + 7, tokens, [7])


def act_split(k, act, value, at, tokens=slice(0, 512), tiles=range(8)):
    for i, kk in enumerate(tiles):
        if at is not None:
            act.wait_ge(k.normed.sem, k.normed.at(at + i + 1))
        act.copy(k.h_hi[:, kk, tokens], value(kk)).then_inc(k.h_rounded.sem, 1)


def dve_split(k, dve, value, at=0, tokens=slice(0, 512), tiles=range(8)):
    for i, kk in enumerate(tiles):
        dve.wait_ge(k.h_rounded.sem, k.h_rounded.at(at + i + 1))
        dve.tensor_tensor(k.h_lo[:, kk, tokens], value(kk), k.h_hi[:, kk, tokens].bitcast(F32), ALU.subtract)\
            .then_inc(k.h_ready.sem, 1)


def act_norm(k, act):
    act_rstd(k, act)
    act_split(k, act, lambda kk: k.sq[:, kk, :], 0)


def dve_norm(k, dve, gain):
    dve.wait_ge(k.rstd_ready.sem, k.rstd_ready.at(1))
    dve_normed(k, dve, lambda kk: k.sq[:, kk, :], lambda kk: k.xT[:, kk, :], gain, 512, 0)


NORM = dict(sums_full=1, rstd_ready=1, normed=8, h_rounded=8, h_ready=8)


def act_groups(k, act, first, sizes, read_out):
    t = 0
    for g, size in enumerate(sizes):
        split_hi(k, act, first + 4 * g + 7)
        for _ in range(size):
            act.wait_ge(k.tile_full.sem, k.tile_full.at(t + 1))
            read_out(t, bank(k, t))
            t += 1
        split_hi(k, act, first + 4 * g + 8)
    return t


def dve_groups(k, dve, first, groups, each=None):
    for g in range(groups):
        split_lo(k, dve, first + 4 * g + 8)
        if each is not None:
            each(g)


VEC_ROWS = {}


def vector_tiles(a):
    rows = []

    def put(name, tile, at, src):
        rows.append((tile, at, src))
        VEC_ROWS[name] = tile * P + at
        return at + src.shape[0]

    r = lambda v: v.rearrange("(n p) -> n p", p=P)
    at = 0
    for l in range(2):
        at = put(f"g_mix{l}", 0, at, r(a["g_mix"][l]))
        at = put(f"g_ffn{l}", 0, at, r(a["g_ffn"][l]))
        at = put(f"g_mem{l}", 0, at, r(a["g_mem"][l]))
    for name in ("g_kv", "g_final"):
        at = put(name, 0, at, r(a[name]))
    at = put("w_norm_mix_2", 0, at, r(a["w_norm_mix_2"][0]))
    at = put("w_norm_ffn_2", 0, at, r(a["w_norm_ffn_2"][0]))
    at = put("w_norm_final_2", 0, at, r(a["w_norm_final_2"]))
    at = put("a_g_head", 0, at, r(a["a_g_head"][0]))
    at = put("w_gdn_norm_2", 0, at, r(a["w_gdn_norm_2"][0]))
    conv = a["conv_w"].rearrange("l j (n p) -> l (j n) p", p=P)
    at = put("conv_w0", 1, 0, conv[0])
    at = put("conv_b0", 1, at, r(a["conv_b"][0]))
    at = put("conv_b1", 1, at, r(a["conv_b"][1]))
    at = put("conv_w1", 2, 0, conv[1])
    at = put("w_sconv_2", 2, at, a["w_sconv_2"][0].rearrange("j (n p) -> (j n) p", p=P))
    at = put("w_gdn_conv_2", 2, at, a["w_gdn_conv_2"][0].rearrange("j (n p) -> (j n) p", p=P))
    fc = a["w_ffn_conv_2"][0].rearrange("j (n p) -> j n p", p=P)
    at = put("ffn_conv2_0", 3, 0, fc[0])
    at = put("ffn_conv2_1", 3, at, fc[1])
    at = put("ffn_conv2_2", 4, 0, fc[2])
    at = put("pe_k", 4, at, a["pe_k"].rearrange("(j q) d -> j (q d)", q=2))
    at = put("pe_v", 4, at, a["pe_v"].rearrange("(j q) d -> j (q d)", q=2))
    return rows


VEC_TILES = 5


def stage_setup(k, a):
    rows = vector_tiles(a)
    x_rows = k.carve(0, (4, 1024))
    mem_rows = k.carve(4096, (2, 1024))
    v_rows = k.carve(6144, (VEC_TILES, P))
    iota_f = k.carve(7168, (512,)).bitcast(I32)
    iota_c = k.carve(7680, (4 * 31,)).bitcast(I32)
    ip = k.carve(7808, (P,)).bitcast(I32)
    ic = k.carve(7936, (P,)).bitcast(I32)
    xo = k.carve(8064, (P,)).bitcast(I32)
    sh = k.carve(8192, (7 * P,)).bitcast(I32)
    x_in, mem_in, v_in = k.sem("x_in"), k.sem("mem_in"), k.sem("vectors_in")
    rows_clear, consts, iotas = k.sem("rows_clear"), k.sem("constants"), k.sem("iotas")
    turned, out = k.sem("turned"), k.sem("turned_out")
    jobs = [("x", tt, m) for m in range(8) for tt in range(4)] + [("mem", tt, m) for m in range(8) for tt in range(2)]

    with k.nc.Block() as block:
        @block.sync
        def _(sp):
            for tt in range(4):
                sp.dma_start(x_rows[:, tt, :], a["x"][0, tt * P:(tt + 1) * P, :]).then_inc(x_in, 16)
            for tt in range(2):
                sp.dma_start(mem_rows[:, tt, :], a["mem"][0, tt * P:(tt + 1) * P, :]).then_inc(mem_in, 16)
            stream(k, sp, 0)

        @block.scalar
        def _(act):
            act.wait_ge(rows_clear, 1)
            for tile, at, src in rows:
                act.dma_start(v_rows[at:at + src.shape[0], tile, :], src).then_inc(v_in, 16)

        @block.gpsimd
        def _(pool):
            k.pool_chain.link(pool, pool.memset(k.ones[:, :], 1.0))
            k.pool_chain.link(pool, pool.affine_select(k.triu[:, :], k.ones[:, :], [[1, P]], ALU.is_ge, 0.0,
                                                       base=0, channel_multiplier=-1))
            k.pool_chain.link(pool, pool.affine_select(k.ident[:, :], k.triu[:, :], [[1, P]], ALU.is_equal, 0.0,
                                                       base=0, channel_multiplier=-1))
            pool.affine_select(k.triu_strict[:, :], k.triu[:, :], [[1, P]], ALU.not_equal, 0.0,
                               base=0, channel_multiplier=-1).then_inc(consts, 1)
            k.pool_chain.link(pool, pool.affine_select(k.tril[:, :], k.ones[:, :], [[-1, P]], ALU.is_ge, 0.0,
                                                       base=0, channel_multiplier=1))
            pool.iota(iota_f, [[-1, 512]], base=384, channel_multiplier=1).then_inc(iotas, 1)
            pool.iota(iota_c, [[P, 4], [-16, 31]], base=-31, channel_multiplier=1).then_inc(iotas, 1)
            pool.iota(ip, [[0, P]], base=0, channel_multiplier=1).then_inc(iotas, 1)
            pool.iota(ic, [[1, P]], base=0, channel_multiplier=0).then_inc(iotas, 1)

        @block.vector
        def _(dve):
            L = lambda ins: k.dve_chain.link(dve, ins)
            dve.memset(v_rows[:, :, :], 0.0).then_inc(rows_clear, 1)
            L(dve.memset(k.eps[:, :], 1e-6))
            dve.wait_ge(iotas, 4)
            dve.wait_ge(consts, 1)
            L(dve.tensor_copy(k.dist[:, :], iota_f))
            L(dve.tensor_copy(k.dist_cmp[:, :], iota_c))
            L(dve.tensor_scalar(k.valid[:, :], k.dist_cmp[:, 0:1], 0.0, None, ALU.is_ge))
            L(dve.tensor_tensor(xo, ip, ic, ALU.bitwise_xor))
            for lg in range(7):
                piece = sh[:, lg * P:(lg + 1) * P]
                L(dve.tensor_scalar(piece, xo, lg, None, ALU.logical_shift_right))
                L(dve.scalar_tensor_tensor(k.level[:, lg, :], piece, 1.0, k.triu[:, :], ALU.is_equal, ALU.mult))
            for n, (what, tt, m) in enumerate(jobs):
                dve.wait_ge(turned, n + 1)
                dst = k.xT[:, m, tt * P:(tt + 1) * P] if what == "x" else k.memT[:, m, tt * P:(tt + 1) * P]
                dve.tensor_copy(dst, bank(k, n)[:, 0:P]).then_inc(out, 1)
            for t in range(VEC_TILES):
                dve.wait_ge(turned, len(jobs) + t + 1)
                dve.tensor_copy(k.vecs[:, t * P:(t + 1) * P], bank(k, len(jobs) + t)[:, 0:P]).then_inc(out, 1)

        @block.tensor
        def _(pe):
            pe.wait_ge(consts, 1)
            pe.wait_ge(x_in, 64)
            for n, (what, tt, m) in enumerate(jobs):
                if n == 32:
                    pe.wait_ge(mem_in, 32)
                if n >= 8:
                    pe.wait_ge(out, n - 7)
                src = (x_rows if what == "x" else mem_rows)[:, tt, m * P:(m + 1) * P]
                pe.transpose(bank(k, n)[:, 0:P], src, k.ident[:, :]).then_inc(turned, 1)
            pe.wait_ge(v_in, 16 * len(rows))
            for t in range(VEC_TILES):
                n = len(jobs) + t
                pe.wait_ge(out, n - 7)
                pe.transpose(bank(k, n)[:, 0:P], v_rows[:, t, :], k.ident[:, :]).then_inc(turned, 1)

    masked = k.sem("masked")
    with k.nc.Block() as block:
        @block.gpsimd
        def _(pool):
            pool.affine_select(k.dist[:, :], k.dist[:, :], [[-1, 512]], ALU.is_ge, BIG, base=384,
                               channel_multiplier=1).then_inc(masked, 1)
            pool.affine_select(k.dist_cmp[:, :], k.dist_cmp[:, :], [[P, 4], [-16, 31]], ALU.is_ge, BIG, base=-31,
                               channel_multiplier=1).then_inc(masked, 1)
            pool.wait_ge(masked, 2)


def stage_memory(k, a):
    M = 256
    first = k.ring.took
    cols = [slice(0, M), slice(M, 2 * M)]
    value = [lambda kk: k.sq[:, kk, M:2 * M], lambda kk: k.sq[:, kk, 0:M]]
    sizes = [4, 2, 4, 2]
    with k.nc.Block() as block:
        @block.sync
        def _(sp):
            stream(k, sp, first + 16)

        @block.scalar
        def _(act):
            act_squares(k, act, lambda kk: k.memT[:, kk, :], M)
            split_hi(k, act, first + 4)
            act_rstd(k, act, M)
            for l in range(2):
                act_split(k, act, value[l], 8 * l, cols[l])

            def read_out(t, src):
                l, m = divmod(t, 6)
                dst = k.mkT[:, l, m, :] if m < 4 else k.mv[:, l, m - 4, :]
                act.copy(dst, src[:, 0:M if m < 4 else 512]).then_inc(k.tile_free.sem, 1)

            act_groups(k, act, first, sizes, read_out)

        @block.vector
        def _(dve):
            split_lo(k, dve, first + 4)
            dve.wait_ge(k.rstd_ready.sem, k.rstd_ready.at(1))
            for l in range(2):
                dve_normed(k, dve, value[l], lambda kk: k.memT[:, kk, :], VEC_ROWS[f"g_mem{l}"], M, 8 * l, cols[l])
            dve_groups(k, dve, first, 4)

        @block.tensor
        def _(pe):
            pe_norm_sums(k, pe, M)
            pe_warm(k, pe, 5)
            t = 0
            for l in range(2):
                t = pe_group(k, pe, t, [feature_tile(k, m * P, cols[l]) for m in range(4)], 8 * l)
                t = pe_group(k, pe, t, [token_tile(k, tt, lambda w: w[:, :], 512, l * M) for tt in range(2)])
            pe_used(k, pe)
    k.advance(sq_ready=8, sums_full=1, rstd_ready=1, normed=16, h_rounded=16, h_ready=16, tile_full=12, tile_free=12)


def small_weights(k, name, kt, n, pad=0):
    raw = k.scope(f"{name}_raw", [P, kt, n], F32)
    return raw, k.scope(f"{name}_hi", [P, kt, max(n, pad)], F32R), k.scope(f"{name}_lo", [P, kt, max(n, pad)], F32R)


def pe_few(k, pe, t, weights):
    if t >= 8:
        pe.wait_ge(k.tile_free.sem, k.tile_free.at(t - 7))
    for kk in range(8):
        _, mm = pe_three(k, pe, bank(k, t)[:, :], [w[:, kk, :] for w in weights],
                         (k.h_hi[:, kk, :], k.h_lo[:, kk, :]), kk == 0, kk == 7)
    mm.then_inc(k.tile_full.sem, 1)


def stage_gla_in(k, a):
    k.qT, k.kT = k.carve(0, (2, 512)), k.carve(1024, (2, 512))
    k.v = k.carve(2048, (4, 512))
    k.rT = k.carve(4096, (4, 512))
    k.mqT = k.carve(6144, (4, 512))
    k.alrT = k.carve(8192, (512,))
    w_alr, alr_hi, alr_lo = small_weights(k, "w_alr", 8, 16, P)
    alr_in, ones_row, alr_split = k.sem("alr_in"), k.sem("ones_row"), k.sem("alr_split")
    first = k.ring.took
    with k.nc.Block() as block:
        @block.sync
        def _(sp):
            sp.dma_start(w_alr[:, :, :], a["a_w_in"][0].rearrange("(k p) n -> p k n", p=P)[:, :, 1536:1552]).then_inc(alr_in, 16)
            stream(k, sp, first + 16)

        @block.gpsimd
        def _(pool):
            pool.memset(k.alrT[0:32, :], 1.0).then_inc(ones_row, 1)
            for part in (alr_hi, alr_lo):
                pool.memset(part[:, :, :].bitcast(F32), 0.0).then_inc(ones_row, 1)

        @block.scalar
        def _(act):
            act_squares(k, act, lambda kk: k.xT[:, kk, :], 512)
            act_norm(k, act)
            act.wait_ge(alr_in, 16)
            act.wait_ge(ones_row, 3)
            act.copy(alr_hi[:, :, 0:16], w_alr[:, :, :]).then_inc(alr_split, 1)

            def read_out(t, src):
                if t < 2:
                    ins = act.mul(k.qT[:, t, :], src[:, :], 64 ** -0.5)
                elif t < 4:
                    ins = act.copy(k.kT[:, t - 2, :], src[:, :])
                elif t < 8:
                    ins = act.copy(k.v[:, t - 4, :], src[:, :])
                elif t < 12:
                    ins = act.activation(k.rT[:, t - 8, :], src[:, :], ACT.Silu)
                elif t < 16:
                    ins = act.mul(k.mqT[:, t - 12, :], src[:, :], -(128 ** -0.5))
                else:
                    ins = act.copy(k.alrT[0:16, :], src[0:16, :])
                ins.then_inc(k.tile_free.sem, 1)

            t = act_groups(k, act, first, [4] * 4, read_out)
            act.wait_ge(k.tile_full.sem, k.tile_full.at(t + 1))
            read_out(t, bank(k, t))

        @block.vector
        def _(dve):
            dve_norm(k, dve, VEC_ROWS["g_mix0"])
            dve.wait_ge(alr_split, 1)
            dve.tensor_tensor(alr_lo[:, :, 0:16], w_alr[:, :, :], alr_hi[:, :, 0:16].bitcast(F32), ALU.subtract)\
                .then_inc(alr_split, 1)
            dve_groups(k, dve, first, 4)

        @block.tensor
        def _(pe):
            pe_norm_sums(k, pe, 512)
            pe_warm(k, pe, 5)
            t = 0
            for group in range(4):
                if group == 1:
                    tiles = [token_tile(k, tt, lambda w: w[:, :], 512) for tt in range(4)]
                else:
                    tiles = [feature_tile(k, m * P) for m in range(4)]
                t = pe_group(k, pe, t, tiles, 0 if group == 0 else None)
            pe_used(k, pe)
            pe.wait_ge(alr_split, 2)
            pe_few(k, pe, t, (alr_hi, alr_lo))
    k.advance(**NORM, sq_ready=8, tile_full=17, tile_free=17)


def stage_mem_attention(k, layer):
    prob = [k.carve(i * 1024, (4, 256)) for i in range(2)]
    probT = [k.carve(4096 + i * 1024, (2, 512)) for i in range(2)]
    low, tot, inv = (k.carve(8704 + i * 16, (4, 4)) for i in range(3))
    first = k.ring.took
    z_full, low_ready, e_ready, p_ready, t_full, t_out, o_full, o_out = k.ma_sig
    with k.nc.Block() as block:
        @block.sync
        def _(sp):
            stream(k, sp, first)

        @block.tensor
        def _(pe):
            def scores(h):
                if h >= 2:
                    pe.wait_ge(e_ready.sem, e_ready.at(4 * (h - 1)))
                for tt in range(4):
                    mm = pe.matmul(bank(k, 6 * (h % 2) + tt // 2)[:, (tt % 2) * 256:(tt % 2) * 256 + 256],
                                   k.mqT[:, h, tt * P:(tt + 1) * P], k.mkT[:, layer, h, :], start=True, stop=True)
                mm.then_inc(z_full.sem, 1)

            scores(0)
            scores(1)
            for h in range(4):
                if 1 <= h < 3:
                    scores(h + 1)
                if h >= 2:
                    pe.wait_ge(o_out.sem, o_out.at(h - 1))
                pe_warm(k, pe, 3, 4 + h % 2)
                pe.wait_ge(p_ready.sem, p_ready.at(h + 1))
                if h >= 1:
                    pe.wait_ge(t_out.sem, t_out.at(2 * h))
                for mt in range(2):
                    for tt in range(4):
                        mm = pe.transpose(bank(k, 2 + mt)[:, tt * P:(tt + 1) * P],
                                          prob[h % 2][:, tt, mt * P:(mt + 1) * P], k.ident[:, :])
                    mm.then_inc(t_full.sem, 1)
                for mt in range(2):
                    pe.wait_ge(t_out.sem, t_out.at(2 * h + mt + 1))
                    mm = pe.matmul(bank(k, 4 + h % 2)[:, :], k.mv[:, layer, mt, h * P:(h + 1) * P],
                                   probT[h % 2][:, mt, :], start=(mt == 0), stop=(mt == 1))
                mm.then_inc(o_full.sem, 1)

        @block.vector
        def _(dve):
            value = lambda kk: k.catT[:, kk, :]
            dve_split(k, dve, value, 0, tiles=range(4))

            def lows(h):
                dve.wait_ge(z_full.sem, z_full.at(h + 1))
                for b in range(2):
                    dve.tensor_reduce(low[:, h, 2 * b:2 * b + 2],
                                      bank(k, 6 * (h % 2) + b)[:, :].rearrange("p (a n) -> p a n", a=2), AX.X, ALU.min)\
                        .then_inc(low_ready.sem, 1)

            lows(0)
            lows(1)
            for h in range(4):
                dve.wait_ge(e_ready.sem, e_ready.at(4 * (h + 1)))
                k.dve_chain.link(dve, dve.reciprocal(inv[:, h, :], tot[:, h, :]))
                dve.tensor_tensor(prob[h % 2][:, :, :], prob[h % 2][:, :, :],
                                  inv[:, h, :].unsqueeze(2).broadcast_to([P, 4, 256]), ALU.mult)\
                    .then_inc(p_ready.sem, 1)
                if h < 2:
                    lows(h + 2)
                if h >= 1:
                    dve_split(k, dve, value, 3 + h, tiles=[3 + h])
                split_lo(k, dve, first + h + 1)
            dve_split(k, dve, value, 7, tiles=[7])

        @block.scalar
        def _(act):
            value = lambda kk: k.catT[:, kk, :]
            act_split(k, act, value, None, tiles=range(4))

            def exps(h):
                act.wait_ge(low_ready.sem, low_ready.at(2 * (h + 1)))
                if h >= 2:
                    act.wait_ge(t_full.sem, t_full.at(2 * (h - 1)))
                for tt in range(4):
                    act.activation(prob[h % 2][:, tt, :], bank(k, 6 * (h % 2) + tt // 2)[:, (tt % 2) * 256:(tt % 2) * 256 + 256],
                                   ACT.Exp, bias=low[:, h, tt:tt + 1], scale=-1.0,
                                   accum_out=tot[:, h, tt:tt + 1]).then_inc(e_ready.sem, 1)

            exps(0)
            for h in range(4):
                if h < 3:
                    exps(h + 1)
                for mt in range(2):
                    act.wait_ge(t_full.sem, t_full.at(2 * h + mt + 1))
                    if h >= 2:
                        act.wait_ge(o_full.sem, o_full.at(h - 1))
                    act.copy(probT[h % 2][:, mt, :], bank(k, 2 + mt)[:, :]).then_inc(t_out.sem, 1)
                split_hi(k, act, first + h + 1)
                act.wait_ge(o_full.sem, o_full.at(h + 1))
                act.copy(value(4 + h), bank(k, 4 + h % 2)[:, :]).then_inc(o_out.sem, 1)
                act.wait_ge(o_out.sem, o_out.at(h + 1))
                act_split(k, act, value, None, tiles=[4 + h])
    for s, n in zip(k.ma_sig, (4, 8, 16, 4, 8, 8, 4, 4)):
        s.base += n
    k.advance(h_rounded=8, h_ready=8)


def stage_out_projection(k):
    first = k.ring.took
    with k.nc.Block() as block:
        @block.sync
        def _(sp):
            stream(k, sp, first + 8)

        @block.scalar
        def _(act):
            split_hi(k, act, first + 8)
            act_load_ln(k, act)
            act_new_squares(k, act, range(4))
            split_hi(k, act, first + 10)
            act_new_squares(k, act, range(4, 8))

        @block.gpsimd
        def _(pool):
            pool_new_sums(k, pool)

        @block.tensor
        def _(pe):
            t = pe_group(k, pe, 0, [feature_tile(k, m * P) for m in range(4)])
            pe_group(k, pe, t, [feature_tile(k, m * P) for m in range(4)])
            pe_new_sums(k, pe)
            pe_used(k, pe)

        @block.vector
        def _(dve):
            split_lo(k, dve, first + 4)
            for g in range(2):
                split_lo(k, dve, first + (7, 10)[g])
                for t in range(4 * g, 4 * g + 4):
                    dve.wait_ge(k.tile_full.sem, k.tile_full.at(t + 1))
                    dve.tensor_tensor(k.xT[:, t, :], k.xT[:, t, :], bank(k, t)[:, :], ALU.add).then_inc(k.tile_free.sem, 1)
                split_lo(k, dve, first + (8, 10)[g])
    k.advance(tile_full=8, tile_free=8, sq_ready=8, sq_added=1)


def stage_gla(k, a):
    C = 4
    base = 4096
    w_alpha = k.scr(base, (256,))
    g = k.scr(base + 256, (C, 256))
    tmp = k.scr(base + 1280, (C, 256))
    b = k.scr(base + 2304, (2, 512))
    eb = k.scr(base + 3328, (2, 512))
    qe = k.scr(base + 4352, (2, 512))
    kbar = k.scr(base + 5376, (2, 512))
    kbar_tok = k.scr(base + 6400, (C, 2, P))
    diff = [k.scr(base + 7424 + i * 1024, (1024,)) for i in range(2)]
    ql = [k.scr(base + 9472 + i * 1024, (2, 512)) for i in range(2)]
    kl = [k.scr(base + 11520 + i * 1024, (2, 512)) for i in range(2)]
    A = k.scr(base + 13568, (4, 512))
    Ss = [k.scr(base + 15616 + i * 512, (2, 256)) for i in range(2)]
    last = lambda t: t[:, :, :].rearrange("p i (c n) -> p (i c) n", c=C)
    w_in, y_full, ls_ready, b_full, b_ready = (k.sem(n) for n in ("w_alpha_in", "alpha_full", "decay_ready", "cum_full", "cum_ready"))
    logs = k.sem("alpha_logs")
    kb_ready, kb_turned, kb_out = k.sem("kbar_ready"), k.sem("kbar_turned"), k.sem("kbar_out")
    with k.nc.Block() as block:
        @block.sync
        def _(sp):
            sp.dma_start(w_alpha[0:16, :], a["a_w_alpha"][0]).then_inc(w_in, 16)
            sp.dma_start(w_alpha[16:17, :], a["a_b_alpha"]).then_inc(w_in, 16)

        @block.tensor
        def _(pe):
            pe.wait_ge(w_in, 32)
            for c in range(C):
                mm = pe.matmul(bank(k, c // 2)[:, (c % 2) * 256:(c % 2) * 256 + 256], k.alrT[0:17, c * P:(c + 1) * P],
                               w_alpha[0:17, :], start=True, stop=True)
            mm.then_inc(y_full, 1)
            pe_warm(k, pe, 8)
            pe.wait_ge(ls_ready, 1)
            for i in range(2):
                for c in range(C):
                    mm = pe.matmul(bank(k, 2 + i)[:, c * P:(c + 1) * P], g[:, c, i * P:(i + 1) * P], k.triu[:, :],
                                   start=True, stop=True)
            mm.then_inc(b_full, 1)
            pe_warm(k, pe, 7)
            pe.wait_ge(kb_ready, 1)
            for c in range(C):
                for i in range(2):
                    mm = pe.transpose(bank(k, 4 + c // 2)[:, ((c % 2) * 2 + i) * P:((c % 2) * 2 + i + 1) * P],
                                      kbar[:, i, c * P:(c + 1) * P], k.ident[:, :])
            mm.then_inc(kb_turned, 1)

        @block.scalar
        def _(act):
            L = lambda ins: k.act_chain.link(act, ins)
            act.wait_ge(y_full, 1)
            for h in range(2):
                src = bank(k, h)[:, :].rearrange("p (c n) -> p c n", c=2)
                L(act.activation(tmp[:, 2 * h:2 * h + 2, :], src, ACT.Abs))
            L(act.activation(tmp[:, :, :], tmp[:, :, :], ACT.Exp, scale=-1.0))
            act.activation(tmp[:, :, :], tmp[:, :, :], ACT.Ln, bias=1.0).then_inc(logs, 1)
            act.wait_ge(b_full, 1)
            for i in range(2):
                act.mul(b[:, i, :], bank(k, 2 + i)[:, :], 1.0 / 16).then_inc(b_ready, 1)
            act.wait_ge(b_ready, 2)
            L(act.activation(eb[:, :, :], b[:, :, :], ACT.Exp))
            act.wait_ge(b_ready, 3)
            L(act.activation(kbar[:, :, :], kbar[:, :, :], ACT.Exp))
            act.sem_inc(b_ready, 1)
            act.wait_ge(kb_turned, 1)
            for h in range(2):
                act.copy(kbar_tok[:, 2 * h:2 * h + 2, :, :].rearrange("p c i n -> p (c i n)"),
                         bank(k, 4 + h)[:, :]).then_inc(kb_out, 1)

        @block.vector
        def _(dve):
            L = lambda ins: k.dve_chain.link(dve, ins)
            dve.wait_ge(logs, 1)
            for h in range(2):
                ins = dve.scalar_tensor_tensor(g[:, 2 * h:2 * h + 2, :], bank(k, h)[:, :].rearrange("p (c n) -> p c n", c=2),
                                               0.0, tmp[:, 2 * h:2 * h + 2, :], ALU.min, ALU.subtract)
                if h == 0:
                    L(ins)
            ins.then_inc(ls_ready, 1)
            dve.wait_ge(b_ready, 2)
            dve.tensor_tensor(last(kbar), last(b)[:, :, P - 1:P].broadcast_to([P, 8, P]), last(b), ALU.subtract)\
                .then_inc(b_ready, 1)
            dve.wait_ge(b_ready, 4)
            L(dve.tensor_tensor(qe[:, :, :], k.qT[:, :, :], eb[:, :, :], ALU.mult))
            dve.tensor_tensor(kbar[:, :, :], k.kT[:, :, :], kbar[:, :, :], ALU.mult).then_inc(kb_ready, 1)

    d_ready, dl_ready, e_done, qk_ready = (k.sem(n) for n in ("diff_ready", "diff_left", "level_exp", "level_qk"))
    s_full, s_done = k.sem("level_full"), k.sem("level_done")
    halves = lambda t, n: t.rearrange("p (m two n) -> p m two n", two=2, n=n)
    right = lambda t, lv: halves(t[:, :, :].rearrange("p i n -> p (i n)"), 1 << lv)[:, :, 1, :]
    with k.nc.Block() as block:
        @block.vector
        def _(dve):
            L = lambda ins: k.dve_chain.link(dve, ins)
            L(dve.memset(A[:, :, :], 0.0))

            def differences(lv):
                n = 1 << lv
                m = 1024 // (2 * n)
                bv = halves(b[:, :, :].rearrange("p i n -> p (i n)"), n)
                dv = halves(diff[lv % 2], n)
                ref = bv[:, :, 0, n - 1:n].broadcast_to([P, m, n])
                if lv >= 2:
                    dve.wait_ge(qk_ready, lv - 1)
                dve.tensor_tensor(dv[:, :, 0, :], ref, bv[:, :, 0, :], ALU.subtract).then_inc(dl_ready, 1)
                dve.tensor_tensor(dv[:, :, 1, :], bv[:, :, 1, :], ref, ALU.subtract).then_inc(d_ready, 1)

            def products(lv):
                if lv == 7:
                    return
                dve.wait_ge(e_done, lv + 1)
                if lv >= 2:
                    dve.wait_ge(s_full, 4 * (lv - 1))
                e = diff[lv % 2].rearrange("p (i n) -> p i n", i=2)
                L(dve.tensor_tensor(right(ql[lv % 2], lv), right(k.qT, lv), right(e, lv), ALU.mult))
                dve.tensor_tensor(kl[lv % 2][:, :, :], k.kT[:, :, :], e, ALU.mult).then_inc(qk_ready, 1)

            def place(lv):
                mask = (k.level[:, lv, :] if lv < 7 else k.ident[:, :]).bitcast(I32)
                n = 1 << lv
                by_block = lambda t: t.rearrange("p (c m two n) -> p c m two n", c=C, two=2, n=n)[:, :, :, 1, :]
                for h in range(4):
                    dve.wait_ge(s_full, 4 * lv + h + 1)
                    if lv >= 1:
                        dve.wait_ge(s_done, 4 * (lv - 1) + h + 1)
                    if lv < 7:
                        dve.copy_predicated(by_block(A[:, h, :]),
                                            mask.rearrange("p (m two n) -> p m two n", two=2, n=n)[:, :, 1, :]
                                            .unsqueeze(1).broadcast_to([P, C, 64 // n, n]),
                                            bank(k, 4 * (lv % 2) + h)[:, 0:256].rearrange("p (c m n) -> p c m n", c=C, n=n))\
                            .then_inc(s_done, 1)
                        continue
                    dve.copy_predicated(A[:, h, :].rearrange("p (c n) -> p c n", c=C),
                                        mask.unsqueeze(1).broadcast_to([P, C, P]),
                                        bank(k, 4 * (lv % 2) + h)[:, :].rearrange("p (c n) -> p c n", c=C))\
                        .then_inc(s_done, 1)

            differences(0)
            for lv in range(8):
                if lv < 6:
                    differences(lv + 1)
                products(lv)
                if lv >= 1:
                    place(lv - 1)
            place(7)

        @block.scalar
        def _(act):
            for lv in range(7):
                act.wait_ge(d_ready, lv + 1)
                act.wait_ge(dl_ready, lv + 1)
                act.activation(diff[lv % 2], diff[lv % 2], ACT.Exp).then_inc(e_done, 1)

        @block.tensor
        def _(pe):
            pe_warm(k, pe, 6)
            for lv in range(8):
                q, kk = (ql[lv % 2], kl[lv % 2]) if lv < 7 else (k.qT, k.kT)
                if lv < 7:
                    pe.wait_ge(qk_ready, lv + 1)
                for h in range(4):
                    if lv >= 2:
                        pe.wait_ge(s_done, 4 * (lv - 2) + h + 1)
                    r0 = (h % 2) * 64
                    for c in range(C):
                        cs = slice(c * P, (c + 1) * P)
                        qc, out = q[r0:r0 + 64, h // 2, cs], bank(k, 4 * (lv % 2) + h)[:, cs]
                        if lv < 7:
                            n = 1 << lv
                            qc = qc.rearrange("p (m two n) -> p m two n", two=2, n=n)[:, :, 1, :]
                            out = bank(k, 4 * (lv % 2) + h)[:, c * 64:(c + 1) * 64]
                            out = out.rearrange("p (m n) -> p m n", n=n)
                        mm = pe.matmul(out, kk[r0:r0 + 64, h // 2, cs], qc, start=True, stop=True)
                    mm.then_inc(s_full, 1)

    u_full, S_ready, o_full = k.sem("gla_update_full"), k.sem("gla_state_ready"), k.sem("gla_out_full")
    sq, nf, rs = k.sem("gla_squares"), k.sem("gla_sums"), k.sem("gla_rstd")
    o = A
    o_sb, osq, rstd = k.scr(base + 7424, (4, 512)), k.scr(base + 9472, (4, 512)), k.scr(base + 11520, (4, 512))
    with k.nc.Block() as block:
        @block.tensor
        def _(pe):
            for c in range(C):
                cs = slice(c * P, (c + 1) * P)
                if c < C - 1:
                    for i in range(2):
                        if c >= 1:
                            pe.wait_ge(S_ready, 2 * (c - 1) + i + 1)
                        pe.matmul(bank(k, 4 + i)[:, 0:256], kbar_tok[:, c, i, :], k.v[:, c, i * 256:(i + 1) * 256],
                                  start=True, stop=True).then_inc(u_full, 1)
                for h in range(4):
                    r0 = (h % 2) * 64
                    if c >= 1:
                        pe.wait_ge(S_ready, 2 * c)
                        pe.matmul(bank(k, h)[:, cs], Ss[(c - 1) % 2][r0:r0 + 64, h // 2, (h % 2) * P:(h % 2 + 1) * P],
                                  qe[r0:r0 + 64, h // 2, cs], start=True, stop=False)
                    mm = pe.matmul(bank(k, h)[:, cs], k.v[:, c, h * P:(h + 1) * P], A[:, h, cs], start=(c == 0), stop=True)
            mm.then_inc(o_full, 1)
            for h in range(4):
                pe.wait_ge(sq, h + 1)
                pe.matmul(bank(k, 4 + h)[:, :], k.ones[:, :], osq[:, h, :], start=True, stop=True).then_inc(nf, 1)
            pe.wait_ge(rs, 1)
            pe_warm(k, pe, 5, 4)

        @block.vector
        def _(dve):
            L = lambda ins: k.dve_chain.link(dve, ins)
            for c in range(C - 1):
                for i in range(2):
                    dve.wait_ge(u_full, 2 * c + i + 1)
                    col = eb[:, i, c * P + P - 1:c * P + P]
                    if c == 0:
                        ins = dve.tensor_copy(Ss[0][:, i, :], bank(k, 4 + i)[:, 0:256])
                    else:
                        dve.wait_ge(S_ready, 2 * c)
                        if c >= 2:
                            dve.wait_ge(u_full, 2 * c + 2)
                        ins = dve.scalar_tensor_tensor(Ss[c % 2][:, i, :], Ss[(c - 1) % 2][:, i, :], col,
                                                       bank(k, 4 + i)[:, 0:256], ALU.mult, ALU.add)
                    ins.then_inc(S_ready, 1)
            for h in range(4):
                dve.wait_ge(rs, h + 1)
                L(dve.scalar_tensor_tensor(o_sb[:, h, :], bank(k, h)[:, :], k.vec(VEC_ROWS["a_g_head"]), rstd[:, h, :],
                                           ALU.mult, ALU.mult))
                L(dve.tensor_tensor(k.catT[:, h, :], o_sb[:, h, :], k.rT[:, h, :], ALU.mult))

        @block.scalar
        def _(act):
            act.wait_ge(o_full, 1)
            for h in range(4):
                act.activation(osq[:, h, :], bank(k, h)[:, :], ACT.Square, scale=P ** -0.5).then_inc(sq, 1)
            L = lambda ins: k.act_chain.link(act, ins)
            for h in range(4):
                act.wait_ge(nf, h + 1)
                L(act.activation(rstd[:, h, :], bank(k, 4 + h)[:, :], ACT.Ln, bias=k.eps[:, 0:1]))
            for h in range(4):
                act.activation(rstd[:, h, :], rstd[:, h, :], ACT.Exp, scale=-0.5).then_inc(rs, 1)


FF = 2816
FT = FF // P


def ffn_chunks(k, w_up, w_down):
    up = w_up.rearrange("(k p) n -> p k n", p=P)
    down = w_down.rearrange("(k p) n -> p k n", p=P)
    out = []
    for grp in range(FT // 2):
        for c in range(4):
            out.append(lambda n, grp=grp, c=c: [
                (raw_slot(k, n, 2, 512)[:, :, s * 256:(s + 1) * 256],
                 up[:, 2 * c:2 * c + 2, s * FF + grp * 256:s * FF + (grp + 1) * 256]) for s in range(2)])
    up_count = len(out)
    for kk in range(FT):
        out.append(lambda n, kk=kk: [(raw_slot(k, n, 1, 1024)[:, 0, :], down[:, kk, :])])
    return out, [2] * up_count + [1] * FT


def stage_ffn(k, w_up, gain, taps, bias, both):
    GROUPS = FT // 2
    LOOPS = (GROUPS - 3) // 2
    AHEAD = 6
    act_t = k.carve(0, (FT * 512,))
    pad = [[k.carve(FT * 512 + (2 * s + i) * 516, (516,)) for i in range(2)] for s in range(2)]
    acc = [[k.scr((2 * s + i) * 512, (512,)) for i in range(2)] for s in range(2)]
    first = k.ring.took
    UP, TOTAL = 4 * GROUPS, 4 * GROUPS + FT
    down0 = first + UP
    up = w_up.rearrange("(k p) n -> p k n", p=P)
    padded, conv_a, conv_b, silu, done, cleared, act_hi, act_lo = k.ffn_sig
    sides = 2 if both else 1
    bank_of = lambda f, s: bank(k, 2 * (f % 4) + s)

    with k.nc.Block() as block:
        @block.sync
        def _(sp):
            with sp.Fori(0, (UP - RING) // 8) as i:
                for j in range(8):
                    n = first + RING + j
                    src = up[:, 2 * (j % 4):2 * (j % 4) + 2, :]
                    pieces = [(raw_slot(k, n, 2, 512)[:, :, s * 256:(s + 1) * 256],
                               src[:, :, bass.ds(i * 512 + (s * FF + (1 + j // 4) * 256), 256)]) for s in range(2)]
                    load_chunk(k, sp, n, pieces, i)
            k.ring.out = down0
            stream(k, sp, first + TOTAL)

        @block.tensor
        def _(pe):
            def group(g, reg):
                f0 = 2 * g
                tiles = [(bank_of(f0 + f, s)[:, :], feature_tile(k, s * 256 + f * P)[1]) for f in range(2) for s in range(2)]

                def before(i, kk):
                    if kk == 0 and g >= 2 and i % 2 == 0:
                        pe.wait_ge(done.sem, plus(done.at(f0 + i // 2 - 3), reg, 4))
                    if g == 0 and i == 0:
                        pe.wait_ge(k.h_ready.sem, k.h_ready.at(kk + 1))

                for c in range(4):
                    pe_chunk(k, pe, first + 4 * g + c, tiles, [2 * c, 2 * c + 1], 8, reg, before=before)

            pe_warm(k, pe, 5)
            group(0, None)
            group(1, None)
            with pe.Fori(0, LOOPS) as i:
                group(2, i)
                group(3, i)
            group(GROUPS - 1, None)
            pe_used(k, pe)

            def down_ready(kk, reg=None):
                pe.wait_ge(act_lo.sem, plus(act_lo.at(kk + 1), reg, 8))
                pe.wait_ge(k.ring.lo, plus(down0 + kk + 1, reg, 8))

            def down(kk, o):
                wh, wl = parts(k, down0 + kk, 1)
                cs = slice(o * P, (o + 1) * P)
                return pe_three(k, pe, bank(k, o)[:, :], (wh[:, 0, cs], wl[:, 0, cs]),
                                (k.h_hi[:, kk % 8, :], k.h_lo[:, kk % 8, :]), kk == 0, kk == FT - 1)

            down_ready(0)
            pe.wait_ge(done.sem, done.at(FT - 2))
            for o in range(4, 8):
                down(0, o)
            down_ready(1)
            for o in range(4, 8):
                down(1, o)
            pe.wait_ge(done.sem, done.at(FT))
            for kk in range(2):
                for o in range(4):
                    down(kk, o)
            k.ring.owed = 2

            def down_all(kk, reg):
                down_ready(kk, reg)
                for o in range(8):
                    p, _ = down(kk, o)
                    if o == 0:
                        p.then_inc(k.ring.used, k.ring.owed)
                k.ring.owed = 1

            down_all(2, None)
            with pe.Fori(0, 2) as i:
                for kk in range(3, 11):
                    down_all(kk, i)
            down_all(19, None)
            down_ready(FT - 2)
            down_ready(FT - 1)
            for o in range(8):
                p, _ = down(FT - 2, o)
                if o == 0:
                    p.then_inc(k.ring.used, 1)
                down(FT - 1, o)[1].then_inc(k.tile_full.sem, 1)
            pe_new_sums(k, pe)
            k.ring.owed = 2
            pe_used(k, pe)
        k.ring.took = first + TOTAL

        @block.gpsimd
        def _(pool):
            for s in range(sides):
                for i in range(2):
                    pool.memset(pad[s][i][:, 0:2], 0.0).then_inc(cleared.sem, 1)
            pool_new_sums(k, pool)

        @block.scalar
        def _(act):
            act_norm(k, act)
            split_hi(k, act, first + 4)
            act.wait_ge(cleared.sem, cleared.at(2 * sides))

            def copies(f, reg):
                for s in range(sides):
                    act.wait_ge(k.tile_full.sem, plus(k.tile_full.at(2 * f + s + 1), reg, 8))
                    if f >= 2:
                        sig = (conv_a, conv_b)[s]
                        act.wait_ge(sig.sem, plus(sig.at(f - 1), reg, 4))
                    act.copy(pad[s][f % 2][:, 2:514], bank_of(f, s)[:, :]).then_inc(padded.sem, 1)

            def gate(f, reg):
                act.wait_ge(conv_a.sem, plus(conv_a.at(f + 1), reg, 4))
                act.activation(acc[0][f % 2], acc[0][f % 2], ACT.Silu).then_inc(silu.sem, 1)

            def group(g, reg, loads=2):
                for c in range(4, 7):
                    split_hi_chunk(k, act, first + 4 * g + c, reg)
                for f in (2 * g, 2 * g + 1):
                    copies(f, reg)
                for f in (2 * g, 2 * g + 1):
                    gate(f, reg)
                split_hi_chunk(k, act, first + 4 * g + 7, reg)

            group(0, None)
            group(1, None)
            with act.Fori(0, LOOPS) as i:
                group(2, i)
                group(3, i)

            def product_hi(kk):
                act.wait_ge(done.sem, done.at(kk + 1))
                act.wait_ge(k.ring.used, down0 + max(kk - 7, 0))
                act.copy(k.h_hi[:, kk % 8, :], act_t[:, kk * 512:(kk + 1) * 512]).then_inc(act_hi.sem, 1)

            for c in range(3):
                split_hi_chunk(k, act, down0 + c)
            copies(FT - 2, None)
            copies(FT - 1, None)
            product_hi(0)
            product_hi(1)
            gate(FT - 2, None)
            gate(FT - 1, None)
            split_hi_chunk(k, act, down0 + 3)
            for kk in range(2, AHEAD):
                product_hi(kk)
            k.ring.hi_at = down0 + 4
            for kk in range(FT - 2):
                split_hi(k, act, down0 + kk + 5)
                if kk + AHEAD < FT:
                    product_hi(kk + AHEAD)
            act_load_ln(k, act)
            act_new_squares(k, act, range(8))

        @block.vector
        def _(dve):
            dve_norm(k, dve, gain)
            split_lo(k, dve, first + 4)

            def conv(f, reg):
                vec = lambda c: k.vec(c + f) if reg is None else k.vecs[:, bass.ds(reg * 4 + (c + f), 1)]
                if f >= 2:
                    dve.wait_ge(done.sem, plus(done.at(f - 1), reg, 4))
                for s in range(sides):
                    dve.wait_ge(padded.sem, plus(padded.at(sides * f + s + 1), reg, 4 * sides))
                    dst, src = acc[s][f % 2], pad[s][f % 2]
                    t0, t1, t2 = (taps(j) + s * FT for j in range(3))
                    if bias is None:
                        k.dve_chain.link(dve, dve.tensor_scalar(dst, src[:, 2:514], vec(t2), None, ALU.mult))
                    else:
                        k.dve_chain.link(dve, dve.tensor_scalar(dst, src[:, 2:514], vec(t2), vec(bias), ALU.mult, ALU.add))
                    k.dve_chain.link(dve, dve.scalar_tensor_tensor(dst, src[:, 1:513], vec(t1), dst, ALU.mult, ALU.add))
                    dve.scalar_tensor_tensor(dst, src[:, 0:512], vec(t0), dst, ALU.mult, ALU.add)\
                        .then_inc((conv_a, conv_b)[s].sem, 1)

            def gated(f, reg):
                dve.wait_ge(silu.sem, plus(silu.at(f + 1), reg, 4))
                if both:
                    dve.wait_ge(conv_b.sem, plus(conv_b.at(f + 1), reg, 4))
                else:
                    dve.wait_ge(k.tile_full.sem, plus(k.tile_full.at(2 * f + 2), reg, 8))
                other = acc[1][f % 2] if both else bank_of(f, 1)[:, :]
                dst = act_t[:, f * 512:(f + 1) * 512] if reg is None else act_t[:, bass.ds(reg * 2048 + f * 512, 512)]
                dve.tensor_tensor(dst, acc[0][f % 2], other, ALU.mult).then_inc(done.sem, 1)

            def group(g, reg):
                for c in range(4, 7):
                    split_lo_chunk(k, dve, first + 4 * g + c, reg)
                for f in (2 * g, 2 * g + 1):
                    conv(f, reg)
                for f in (2 * g, 2 * g + 1):
                    gated(f, reg)
                split_lo_chunk(k, dve, first + 4 * g + 7, reg)

            group(0, None)
            group(1, None)
            k.dve_chain.per = 4 * 2 * sides
            with dve.Fori(0, LOOPS) as i:
                k.dve_chain.reg = i
                n0 = k.dve_chain.n
                group(2, i)
                group(3, i)
                assert k.dve_chain.n - n0 == k.dve_chain.per
            k.dve_chain.reg = None
            k.dve_chain.n = n0 + k.dve_chain.per * LOOPS

            def product_lo(kk):
                dve.wait_ge(act_hi.sem, act_hi.at(kk + 1))
                dve.tensor_tensor(k.h_lo[:, kk % 8, :], act_t[:, kk * 512:(kk + 1) * 512],
                                  k.h_hi[:, kk % 8, :].bitcast(F32), ALU.subtract).then_inc(act_lo.sem, 1)

            for c in range(3):
                split_lo_chunk(k, dve, down0 + c)
            conv(FT - 2, None)
            product_lo(0)
            product_lo(1)
            conv(FT - 1, None)
            gated(FT - 2, None)
            gated(FT - 1, None)
            split_lo_chunk(k, dve, down0 + 3)
            for kk in range(2, AHEAD):
                product_lo(kk)
            k.ring.lo_at = down0 + 4
            for kk in range(FT - 2):
                split_lo(k, dve, down0 + kk + 5)
                if kk + AHEAD < FT:
                    product_lo(kk + AHEAD)
            for o in range(8):
                dve.wait_ge(k.tile_full.sem, k.tile_full.at(2 * FT + o + 1))
                dve.tensor_tensor(k.xT[:, o, :], k.xT[:, o, :], bank(k, o)[:, :], ALU.add).then_inc(k.tile_free.sem, 1)
    k.advance(**NORM, sq_ready=8, sq_added=1, tile_full=2 * FT + 8, tile_free=8)
    for s, n in zip(k.ffn_sig, (FT * sides, FT, FT * (sides - 1), FT, FT, 2 * sides, FT, FT)):
        s.base += n


NCMP = 31


def kv_chunks(k, w_kv):
    wv = w_kv.rearrange("(k p) n -> p k n", p=P)
    return [lambda n, k0=k0: [
        (raw_slot(k, n, 2, 512)[:, kk, :].rearrange("p (c two d) -> p c two d", c=4, two=2)[:, :, two, :],
         wv[:, k0 + kk, 0:256].rearrange("p (c d) -> p c d", c=4)) for kk in range(2) for two in range(2)]
        for k0 in range(0, 8, 2)]


def paired_query_chunks(k, w):
    wv = w.rearrange("(k p) n -> p k n", p=P)
    return [lambda n, k0=k0: [
        (raw_slot(k, n, 2, 512)[:, kk, :].rearrange("p (j g d) -> p j g d", j=4, g=2)[:, :, g, :],
         wv[:, k0 + kk, g * 256:(g + 1) * 256].rearrange("p (j d) -> p j d", j=4)) for kk in range(2) for g in range(2)]
        for k0 in range(0, 8, 2)]


def paired_out_chunks(k, w, cols):
    return [lambda n, j0=j0: [(raw_slot(k, n, 2, 512)[g * 64:(g + 1) * 64, :, :],
                               w[g * 256 + j0 * 64:g * 256 + (j0 + 2) * 64, cols:cols + 512].rearrange("(j p) n -> p j n", p=64))
                              for g in range(2)] for j0 in (0, 2)]


def stage_nsa_in(k, a):
    N2, WIDE, POS = NCMP + 3, 560, NCMP + 1
    k.qT, k.mqT = k.carve(0, (4, 512)), k.carve(2048, (4, 512))
    k.ksT, k.kwT = k.carve(4096, (512,)), k.carve(4608, (512,))
    k.vsw = k.carve(5120, (4, 256))
    k.kcT, k.vc = k.carve(8192, (32,)), k.carve(8224, (P,))
    k.gates = k.carve(8352, (4, 24))
    hid = [[k.carve(8448 + (2 * s + ht) * 2 * N2, (2 * N2,)) for ht in range(2)] for s in range(2)]
    cb = k.carve(8724, (4,))
    w2k, w2v = k.carve(8728, (2, P)), k.carve(8984, (2, 64))
    kv2 = [k.carve(9280 + s * 2 * WIDE, (2, WIDE)) for s in range(2)]
    kv_parts = [[k.scope(f"kv_{part}{s}", [P, 2 * WIDE], F32R) for part in ("hi", "lo")] for s in range(2)]
    pe_cols = [k.vecs[:, VEC_ROWS[n]:VEC_ROWS[n] + 16] for n in ("pe_k", "pe_v")]
    wg, gates_t = k.scr(0, (8, 24)), k.scr(192, (512,))
    wg_parts = [x[:, 0:8 * P].rearrange("p (k n) -> p k n", k=8) for x in kv_parts[0]]
    old_sq, k.sq = k.sq, k.carve(4096, (8, 512))
    h2 = k.carve(0, (8, 512))
    small_in, kv_clear, kv_shift, small_hi, small_lo = (k.sem(n) for n in (
        "nsa_small_in", "kv_cleared", "kv_shifted", "small_hi", "small_lo"))
    gates_ready = k.sem("gates_ready")
    first = k.ring.took
    flat = lambda t: t[:, :, :].rearrange("p a b -> p (a b)")
    smalls = [(x[0][:, :], x[1][:, :], flat(kv2[s])) for s, x in enumerate(kv_parts)]
    smalls.append((*[x[:, :, 0:24] for x in wg_parts], wg))
    with k.nc.Block() as block:
        @block.sync
        def _(sp):
            w2 = a["w_ck2"].rearrange("(k p) n -> p k n", p=P)
            for two in range(2):
                sp.dma_start(w2k[:, :, two * 64:(two + 1) * 64], w2).then_inc(small_in, 16)
            sp.dma_start(w2v[:, :, :], a["w_cv2"].rearrange("(k p) n -> p k n", p=P)).then_inc(small_in, 16)
            sp.dma_start(wg[:, :, :], a["b_w_in"][0].rearrange("(k p) n -> p k n", p=P)[:, :, 512:536]).then_inc(small_in, 16)
            stream(k, sp, first + 24)

        @block.gpsimd
        def _(pool):
            for s in range(2):
                pool.memset(kv2[s][:, :, :], 0.0).then_inc(kv_clear, 1)

        @block.vector
        def _(dve):
            dve_norm(k, dve, VEC_ROWS["g_kv"])
            split_lo(k, dve, first + 4)
            dve_normed(k, dve, lambda kk: h2[:, kk, :], lambda kk: k.xT[:, kk, :], VEC_ROWS["g_mix1"], 512)

            def small(i):
                hi, lo, src = smalls[i]
                dve.wait_ge(small_hi, i + 1)
                dve.tensor_tensor(lo, src, hi.bitcast(F32), ALU.subtract).then_inc(small_lo, 1)

            split_lo(k, dve, first + 8)
            small(0)
            small(1)
            split_lo(k, dve, first + 12)
            dve_split(k, dve, lambda kk: h2[:, kk, :], 8)
            split_lo(k, dve, first + 16)
            small(2)
            for g in range(3, 6):
                split_lo(k, dve, first + 4 * g + 8)
            dve.wait_ge(gates_ready, 1)
            first_rows = k.gates[:, 0, :].rearrange("p (h b) -> p h b", b=3)[:, :, 0]
            k.dve_chain.link(dve, dve.tensor_scalar(first_rows, first_rows, k.valid[:, 0:1], None, ALU.mult))

        @block.scalar
        def _(act):
            act_norm(k, act)
            split_hi(k, act, first + 4)
            act.wait_ge(small_in, 64)

            def small(i):
                act.copy(smalls[i][0], smalls[i][2]).then_inc(small_hi, 1)

            act.wait_ge(kv_clear, 2)
            for s in range(2):
                act.copy(kv2[s][:, 0, 512:544:2], pe_cols[s]).then_inc(kv_shift, 1)

            def read_out(t, count):
                for t in range(t, t + count):
                    act.wait_ge(k.tile_full.sem, k.tile_full.at(t + 1))
                    src = bank(k, t)
                    if t < 4:
                        dst = kv2[t // 2][:, t % 2, :]
                        act.copy(dst[0:64, 0:512], src[0:64, :]).then_inc(kv_shift, 1)
                        ins = act.copy(dst[64:P, 0:511], src[64:P, 1:512])
                    elif t < 6:
                        ins = act.copy(k.ksT if t == 4 else k.kwT, src[:, :])
                    elif t < 10:
                        ins = act.copy(k.vsw[:, t - 6, :], src[:, 0:256])
                    elif t < 14:
                        s, ht = divmod(t - 10, 2)
                        col = cb[:, 2 * s + ht:2 * s + ht + 1]
                        k.act_chain.link(act, act.copy(col, src[:, POS:POS + 1]))
                        ins = act.activation(hid[s][ht], src[:, 0:2 * N2], ACT.Gelu_apprx_tanh, bias=col)
                    elif t == 14:
                        act.copy(k.kcT[0:64, 0:NCMP], src[0:64, 0:NCMP]).then_inc(kv_shift, 1)
                        ins = act.copy(k.kcT[64:P, 0:NCMP], src[64:P, N2:N2 + NCMP])
                    elif t == 15:
                        ins = act.copy(k.vc[0:NCMP, :], src[0:NCMP, 0:P])
                    elif t < 20:
                        ins = act.mul(k.qT[:, t - 16, :], src[:, :], -(64 ** -0.5))
                    elif t == 20:
                        ins = act.copy(gates_t[0:24, :], src[0:24, :])
                    elif t < 25:
                        ins = act.mul(k.mqT[:, t - 21, :], src[:, :], -(128 ** -0.5))
                    else:
                        k.act_chain.link(act, act.activation(k.gates[:, :, :].rearrange("p a b -> p (a b)"), src[:, 0:96], ACT.Sigmoid))
                        act.sem_inc(gates_ready, 1)
                        act.sem_inc(k.tile_free.sem, 1)
                        continue
                    ins.then_inc(k.tile_free.sem, 1)

            split_hi(k, act, first + 7)
            read_out(0, 4)
            act.wait_ge(kv_shift, 6)
            act.wait_ge(k.tile_free.sem, k.tile_free.at(4))
            small(0)
            small(1)
            split_hi(k, act, first + 11)
            read_out(4, 6)
            split_hi(k, act, first + 12)
            act.wait_ge(k.ring.used, first + 8)
            act_split(k, act, lambda kk: h2[:, kk, :], 8)
            split_hi(k, act, first + 15)
            read_out(10, 2)
            split_hi(k, act, first + 16)
            act.wait_ge(k.ring.used, first + 12)
            small(2)
            split_hi(k, act, first + 19)
            read_out(12, 4)
            split_hi(k, act, first + 23)
            read_out(16, 5)
            split_hi(k, act, first + 27)
            read_out(21, 4)
            split_hi(k, act, first + 28)
            read_out(25, 1)

        @block.tensor
        def _(pe):
            pe_warm(k, pe, 5)
            t = pe_group(k, pe, 0, [feature_tile(k, m * P) for m in range(4)], 0)
            values = lambda w: w.rearrange("p (b two n) -> p b two n", b=2, two=2)[:, :, 1, :]
            t = pe_group(k, pe, t, [feature_tile(k, c) for c in (0, 256)] + [token_tile(k, tt, values, 256) for tt in range(4)])
            for s in range(2):
                pe.wait_ge(small_lo, 1 + s)

                pairs = [x[:, :].rearrange("p (g n) -> p g n", g=2) for x in kv_parts[s]]

                def hidden(ht):
                    return lambda j, w: ([x[:, ht * P:(ht + 1) * P] for x in w],
                                         [x[:, :, 2 * j:2 * j + 16 * (N2 - 1) + 1:16] for x in pairs])

                tiles = [(bank(k, t + i)[:, 0:2 * N2], hidden(i)) for i in range(2)]

                def before(i, j):
                    if j == 0 and t + i >= 8:
                        pe.wait_ge(k.tile_free.sem, k.tile_free.at(t + i - 7))

                for c in range(4):
                    n = k.ring.took
                    k.ring.took += 1
                    pe_chunk(k, pe, n, tiles, range(4 * c, 4 * c + 4), 16, before=before)
                t += 2
            pe.wait_ge(small_in, 64)
            pe.wait_ge(k.tile_free.sem, k.tile_free.at(14))
            for ht in range(2):
                mm = pe.matmul(bank(k, t)[:, 0:2 * N2], w2k[:, ht, :], hid[0][ht], start=(ht == 0), stop=(ht == 1))
            mm.then_inc(k.tile_full.sem, 1)
            t += 1
            for g in range(2):
                for ht in range(2):
                    mm = pe.matmul(bank(k, t)[0:NCMP, g * 64:(g + 1) * 64], hid[1][ht][:, g * N2:g * N2 + NCMP], w2v[:, ht, :],
                                   start=(ht == 0), stop=(ht == 1))
            mm.then_inc(k.tile_full.sem, 1)
            t += 1
            t = pe_group(k, pe, t, [feature_tile(k, m * P) for m in range(4)], 8)
            pe.wait_ge(small_lo, 3)
            pe_few(k, pe, t, wg_parts)
            t = pe_group(k, pe, t + 1, [feature_tile(k, m * P) for m in range(4)])
            pe_used(k, pe)
            pe.wait_ge(k.tile_free.sem, k.tile_free.at(21))
            for tt in range(4):
                mm = pe.transpose(bank(k, t)[:, tt * 24:(tt + 1) * 24], gates_t[0:24, tt * P:(tt + 1) * P], k.ident[0:24, 0:24])
            mm.then_inc(k.tile_full.sem, 1)
    k.advance(sums_full=1, rstd_ready=1, normed=16, h_rounded=16, h_ready=16, tile_full=26, tile_free=26)
    k.sq = old_sq


def stage_nsa(k):
    prob = [[[k.scr(9184 + par * 2688 + br * 1280 + 64 * i * (i + 1), ((i + 1) * P,)) for i in range(4)]
             for br in range(2)] for par in range(2)]
    pcmp = [k.scr(9184 + par * 2688 + 2560, (4, NCMP)) for par in range(2)]
    at = [14560, 17632]
    offs = [0, 512, 896, 1152]
    pT = [[[k.scr(at[par] + br * 1280 + offs[j], (512 - j * P,)) for j in range(4)] for br in range(2)] for par in range(2)]
    pcT = [k.scr(at[par] + 2560, (512,)) for par in range(2)]
    low, tot, coef = (k.scr(20704 + i * 96, (8, 12)) for i in range(3))
    s_full, z_ready, e_done, p_ready = (k.sem(n) for n in ("nsa_scores", "nsa_lows", "nsa_exps", "nsa_probs"))
    t_full, t_out_a, t_out_v, o_full, o_out = (k.sem(n) for n in ("nsa_turned", "nsa_turned_act", "nsa_turned_dve", "nsa_full", "nsa_out"))
    bias_of, bias_cmp = k.scr(4096, (8, 512)), k.scr(8192, (8, 124))
    slopes = k.sem("alibi_ready")
    zc_ready, lc_ready = k.sem("nsa_cmp_added"), k.sem("nsa_cmp_low")
    by_vector = lambda n: (n % 9) % 2 == 1
    copies_by = lambda which, n: sum(by_vector(m) == bool(which) for m in range(n))
    copied = lambda n: (int(by_vector(n)), copies_by(int(by_vector(n)), n + 1))
    units = [(i, br) for i in range(4) for br in range(2)]

    with k.nc.Block() as block:
        @block.gpsimd
        def _(pool):
            for h in range(2, 8):
                pool.tensor_scalar(bias_of[:, h, :], k.dist[:, :], 2.0 ** -(h + 1), None, ALU.mult).then_inc(slopes, 1)
                pool.tensor_scalar(bias_cmp[:, h, :], k.dist_cmp[:, :], 2.0 ** -(h + 1), None, ALU.mult).then_inc(slopes, 1)

        @block.tensor
        def _(pe):
            def scores(h, u):
                j, g = h % 4, h // 4
                r = slice(g * 64, (g + 1) * 64)
                if u < 8:
                    i, br = units[u]
                    n = 8 * h + u
                    if n >= 3:
                        pe.wait_ge(z_ready, n - 2)
                    keys = (k.ksT, k.kwT)[br]
                    pe.matmul(bank(k, n % 3)[:, 0:(i + 1) * P], k.qT[r, j, i * P:(i + 1) * P], keys[r, 0:(i + 1) * P],
                              start=True, stop=True).then_inc(s_full, 1)
                    return
                if h >= 1:
                    pe.wait_ge(zc_ready, h)
                for i in range(4):
                    mm = pe.matmul(bank(k, 3)[:, i * 32:i * 32 + NCMP], k.qT[r, j, i * P:(i + 1) * P], k.kcT[r, 0:NCMP],
                                   start=True, stop=True)
                mm.then_inc(s_full, 1)

            def turn(h, m):
                if m in (0, 4, 8):
                    pe.wait_ge(p_ready, 9 * h + min(m + 4, 9))
                n = 9 * h + m
                if n >= 2:
                    which, count = copied(n - 2)
                    pe.wait_ge((t_out_a, t_out_v)[which], count)
                b = bank(k, 4 + n % 2)
                if m < 8:
                    br, j = divmod(m, 4)
                    for i in range(j, 4):
                        mm = pe.transpose(b[:, (i - j) * P:(i - j + 1) * P], prob[h % 2][br][i][:, j * P:(j + 1) * P], k.ident[:, :])
                else:
                    for i in range(4):
                        mm = pe.transpose(b[0:NCMP, i * P:(i + 1) * P], pcmp[h % 2][:, i, :], k.ident[:, :])
                mm.then_inc(t_full, 1)

            def values(h):
                if h >= 2:
                    pe.wait_ge(o_out, h - 1)
                o = bank(k, 6 + h % 2)
                for which in range(2):
                    pe.wait_ge((t_out_a, t_out_v)[which], copies_by(which, 9 * (h + 1)))
                pe.matmul(o[:, :], k.vc[0:NCMP, :], pcT[h % 2][0:NCMP, :], start=True, stop=False)
                for br in range(2):
                    for j in range(4):
                        mm = pe.matmul(o[:, j * P:512], k.vsw[:, j, br * P:(br + 1) * P], pT[h % 2][br][j],
                                       start=False, stop=(br == 1 and j == 3))
                mm.then_inc(o_full, 1)

            for u in range(9):
                scores(0, u)
            for h in range(8):
                if h >= 1:
                    values(h - 1)
                for m in range(9):
                    turn(h, m)
                    if h < 7:
                        scores(h + 1, m)
            values(7)

        def copy_turned(copy, eng, h, m):
            n = 9 * h + m
            eng.wait_ge(t_full, n + 1)
            if h >= 2:
                eng.wait_ge(o_full, h - 1)
            b = bank(k, 4 + n % 2)
            if m == 8:
                return copy(pcT[h % 2][0:NCMP, :], b[0:NCMP, :])
            br, j = divmod(m, 4)
            return copy(pT[h % 2][br][j], b[:, 0:512 - j * P])

        @block.vector
        def _(dve):
            L = lambda ins: k.dve_chain.link(dve, ins)

            for h in range(2):
                L(dve.tensor_scalar(bias_of[:, h, :], k.dist[:, :], 2.0 ** -(h + 1), None, ALU.mult))
                L(dve.tensor_scalar(bias_cmp[:, h, :], k.dist_cmp[:, :], 2.0 ** -(h + 1), None, ALU.mult))

            def lows(h, u):
                if h >= 2 and u == 0:
                    dve.wait_ge(slopes, 2 * (h - 1))
                    dve.wait_ge(t_full, 9 * (h - 1))
                if u < 8:
                    i, br = units[u]
                    dve.wait_ge(s_full, 9 * h + u + 1)
                    n = (i + 1) * P
                    dve.tensor_tensor_reduce(prob[h % 2][br][i], bank(k, (8 * h + u) % 3)[:, 0:n],
                                             bias_of[:, h, 384 - i * P:512], 1.0, 3e38, ALU.add, ALU.min,
                                             low[:, h, 4 * br + i:4 * br + i + 1]).then_inc(z_ready, 1)
                    return
                dve.wait_ge(s_full, 9 * (h + 1))
                dve.tensor_tensor(pcmp[h % 2][:, :, :], bank(k, 3)[:, 0:P].rearrange("p (i n) -> p i n", i=4)[:, :, 0:NCMP],
                                  bias_cmp[:, h, :].rearrange("p (i n) -> p i n", i=4), ALU.add).then_inc(zc_ready, 1)
                dve.wait_ge(zc_ready, h + 1)
                dve.tensor_reduce(low[:, h, 8:12], pcmp[h % 2][:, :, :], AX.X, ALU.min).then_inc(lc_ready, 1)

            def weigh(h):
                dve.wait_ge(e_done, 12 * (h + 1))
                L(dve.reciprocal(coef[:, h, :], tot[:, h, :]))
                gates = k.gates[:, :, 3 * h:3 * h + 3].rearrange("p i b -> p b i")
                cv = coef[:, h, :].rearrange("p (b i) -> p b i", b=3)
                L(dve.tensor_tensor(cv[:, 0:2, :], cv[:, 0:2, :], gates[:, 1:3, :], ALU.mult))
                L(dve.tensor_tensor(cv[:, 2, :], cv[:, 2, :], gates[:, 0, :], ALU.mult))
                for br in range(2):
                    for i in range(4):
                        p = prob[h % 2][br][i]
                        dve.tensor_scalar(p, p, coef[:, h, 4 * br + i:4 * br + i + 1], None, ALU.mult).then_inc(p_ready, 1)
                dve.tensor_tensor(pcmp[h % 2][:, :, :], pcmp[h % 2][:, :, :],
                                  coef[:, h, 8:12].unsqueeze(2).broadcast_to([P, 4, NCMP]), ALU.mult).then_inc(p_ready, 1)

            for u in range(9):
                lows(0, u)
            for h in range(8):
                weigh(h)
                for m in range(9):
                    if by_vector(9 * h + m):
                        copy_turned(dve.tensor_copy, dve, h, m).then_inc(t_out_v, 1)
                    if h < 7:
                        lows(h + 1, m)

        @block.scalar
        def _(act):
            def exps(h, u):
                if u < 8:
                    i, br = units[u]
                    act.wait_ge(z_ready, 8 * h + u + 1)
                    p, c = prob[h % 2][br][i], 4 * br + i
                    act.activation(p, p, ACT.Exp, bias=low[:, h, c:c + 1], scale=-1.0,
                                   accum_out=tot[:, h, c:c + 1]).then_inc(e_done, 1)
                    return
                act.wait_ge(lc_ready, h + 1)
                for i in range(4):
                    act.activation(pcmp[h % 2][:, i, :], pcmp[h % 2][:, i, :], ACT.Exp, bias=low[:, h, 8 + i:9 + i], scale=-1.0,
                                   accum_out=tot[:, h, 8 + i:9 + i]).then_inc(e_done, 1)

            def finish(h):
                act.wait_ge(o_full, h + 1)
                r = slice(h // 4 * 64, (h // 4 + 1) * 64)
                act.copy(k.catT[r, h % 4, :], bank(k, 6 + h % 2)[r, :]).then_inc(o_out, 1)

            for u in range(9):
                exps(0, u)
            for h in range(8):
                for m in range(9):
                    if not by_vector(9 * h + m):
                        copy_turned(act.copy, act, h, m).then_inc(t_out_a, 1)
                    if h >= 1 and m == 0:
                        finish(h - 1)
                    if h < 7:
                        exps(h + 1, m)
            finish(7)


def mixed_chunks(k, w, parts):
    wv = w.rearrange("(k p) n -> p k n", p=P)
    return [lambda n, k0=k0: [(raw_slot(k, n, 2, 512)[:, :, s * 256:(s + 1) * 256], wv[:, k0:k0 + 2, c:c + 256])
                              for s, c in enumerate(parts)] for k0 in range(0, 8, 2)]


def stage_mix_in(k, a):
    k.scb, k.scc, k.prod = k.carve(0, (2, 512)), k.carve(1024, (2, 512)), k.carve(2048, (2, 516))
    k.qkv = k.carve(3080, (12, 512))
    k.zT = k.carve(9224, (4, 512))
    k.sbq, k.sbk, k.sbv = k.carve(11272, (2, 512)), k.carve(12296, (2, 512)), k.carve(13320, (4, 256))
    k.gab, k.decay_all, k.decay_row = k.carve(14344, (32,)), k.carve(14376, (8,)), k.carve(14384, (8,))
    w_ab, ab_hi, ab_lo = small_weights(k, "w_ab", 8, 8, P)
    ab_t = k.scr(2056, (512,))
    raw = [k.scr(i * 516, (516,)) for i in range(2)]
    acc = [k.scr(1032 + i * 512, (512,)) for i in range(2)]
    small_in, cleared, raw_in, conv_done, ab_split = (k.sem(n) for n in (
        "mix_small_in", "mix_cleared", "mix_raw_in", "mix_conv_done", "mix_ab_split"))
    silu_done = k.sem("mix_silu_done")
    old_sq, k.sq = k.sq, k.carve(9224, (8, 512))
    first = k.ring.took
    taps = VEC_ROWS["w_gdn_conv_2"]
    CONV0 = 10
    with k.nc.Block() as block:
        @block.sync
        def _(sp):
            sp.dma_start(w_ab[:, :, :], a["w_mix_in_2"][0].rearrange("(k p) n -> p k n", p=P)[:, :, 2816:2824]).then_inc(small_in, 16)
            sp.dma_start(k.decay_row[0:1, 0:4], a["gdn_a_log_2"]).then_inc(small_in, 16)
            sp.dma_start(k.decay_row[0:1, 4:8], a["gdn_dt_bias_2"]).then_inc(small_in, 16)
            stream(k, sp, first + 28)

        @block.gpsimd
        def _(pool):
            for part in (ab_hi, ab_lo):
                pool.memset(part[:, :, :].bitcast(F32), 0.0).then_inc(cleared, 1)
            for i in range(2):
                pool.memset(raw[i][:, 0:3], 0.0).then_inc(cleared, 1)
                pool.memset(k.prod[:, i, 0:2], 0.0).then_inc(cleared, 1)

        @block.vector
        def _(dve):
            L = lambda ins: k.dve_chain.link(dve, ins)
            x = lambda kk: k.xT[:, kk, :]
            dve.wait_ge(k.rstd_ready.sem, k.rstd_ready.at(1))
            dve_normed(k, dve, x, x, VEC_ROWS["g_final"], 512)
            dve.wait_ge(k.rstd_ready.sem, k.rstd_ready.at(2))
            dve_normed(k, dve, lambda kk: k.sq[:, kk, :], x, VEC_ROWS["w_norm_mix_2"], 512, 0)
            dve.wait_ge(ab_split, 1)
            dve.tensor_tensor(ab_lo[:, :, 0:8], w_ab[:, :, :], ab_hi[:, :, 0:8].bitcast(F32), ALU.subtract).then_inc(ab_split, 1)
            split_lo(k, dve, first + 12)
            for i in range(2):
                dve.wait_ge(k.tile_free.sem, k.tile_free.at(5 + i))
                p = k.prod[:, i, 2:514]
                L(dve.tensor_tensor(p, p, k.scc[:, i, :], ALU.mult))
            for n in range(12):
                if n % 4 == 0:
                    split_lo(k, dve, first + 15 + n)
                dve.wait_ge(raw_in, n + 1)
                if n >= 2:
                    dve.wait_ge(silu_done, n - 1)
                dst, src = acc[n % 2], raw[n % 2]
                L(dve.tensor_scalar(dst, src[:, 3:515], k.vec(taps + 36 + n), None, ALU.mult))
                for j in (2, 1):
                    L(dve.scalar_tensor_tensor(dst, src[:, j:j + 512], k.vec(taps + 12 * j + n), dst, ALU.mult, ALU.add))
                dve.scalar_tensor_tensor(dst, src[:, 0:512], k.vec(taps + n), dst, ALU.mult, ALU.add).then_inc(conv_done, 1)
                if n % 4 == 3:
                    split_lo(k, dve, first + 13 + n)
            split_lo(k, dve, first + 32)

        @block.scalar
        def _(act):
            act_rstd(k, act)
            for kk in range(8):
                act.wait_ge(k.normed.sem, k.normed.at(kk + 1))
                act.activation(k.sq[:, kk, :], k.xT[:, kk, :], ACT.Square, scale=1024 ** -0.5).then_inc(k.sq_ready.sem, 1)
            k.sums_full.base += 1
            act_rstd(k, act)
            k.sums_full.base -= 1
            act_split(k, act, lambda kk: k.sq[:, kk, :], 8)
            act.wait_ge(small_in, 48)
            act.wait_ge(cleared, 6)
            act.copy(ab_hi[:, :, 0:8], w_ab[:, :, :]).then_inc(ab_split, 1)

            def silu(n):
                act.wait_ge(conv_done, n + 1)
                act.activation(k.qkv[:, n, :], acc[n % 2], ACT.Silu).then_inc(silu_done, 1)

            def read_out(t, src):
                if t < 2:
                    ins = act.copy(k.scb[:, t, :], src[:, :])
                elif t < 4:
                    ins = act.copy(k.scc[:, t - 2, :], src[:, :])
                elif t < 6:
                    ins = act.copy(k.prod[:, t - 4, 2:514], src[:, :])
                elif t < 10:
                    ins = act.copy(k.sbv[:, t - 6, :], src[:, 0:256])
                elif t < 22:
                    n = t - CONV0
                    if n >= 2:
                        act.wait_ge(conv_done, n - 1)
                    k.act_chain.link(act, act.copy(raw[n % 2][:, 3:515], src[:, :]))
                    act.sem_inc(raw_in, 1)
                    act.sem_inc(k.tile_free.sem, 1)
                    if n % 4:
                        silu(n - 1)
                    if n % 4 == 3:
                        silu(n)
                    return
                elif t < 26:
                    ins = act.activation(k.zT[:, t - 22, :], src[:, :], ACT.Silu)
                elif t == 26:
                    ins = act.copy(ab_t[0:8, :], src[0:8, :])
                elif t < 29:
                    ins = act.mul(k.sbq[:, t - 27, :], src[:, :], 64 ** -0.5)
                elif t < 31:
                    ins = act.copy(k.sbk[:, t - 29, :], src[:, :])
                else:
                    k.act_chain.link(act, act.copy(k.decay_all[:, :], src[:, 64:72]))
                    ins = act.copy(k.gab[:, :], src[:, 0:32])
                ins.then_inc(k.tile_free.sem, 1)

            t = act_groups(k, act, first, [4, 6, 4, 4, 4, 5, 4], read_out)
            act.wait_ge(k.tile_full.sem, k.tile_full.at(t + 1))
            read_out(t, bank(k, t))

        @block.tensor
        def _(pe):
            pe_warm(k, pe, 4)
            pe_norm_sums(k, pe)
            pe_warm(k, pe, 5)
            t = 0
            for group in range(7):
                tiles = [feature_tile(k, m * P) for m in range(2 if group == 1 else 4)]
                if group == 1:
                    tiles += [token_tile(k, tt, lambda w: w[:, 256:512], 256) for tt in range(4)]
                t = pe_group(k, pe, t, tiles, 0 if group == 0 else None)
                if group == 5:
                    pe.wait_ge(ab_split, 2)
                    pe_few(k, pe, t, (ab_hi, ab_lo))
                    t += 1
            pe_used(k, pe)
            pe.wait_ge(k.tile_free.sem, k.tile_free.at(27))
            for tt in range(4):
                pe.transpose(bank(k, t)[:, tt * 8:(tt + 1) * 8], ab_t[0:8, tt * P:(tt + 1) * P], k.ident[0:8, 0:8])
            pe.matmul(bank(k, t)[:, 64:72], k.ones[0:1, :], k.decay_row[0:1, :], start=True, stop=True)\
                .then_inc(k.tile_full.sem, 1)
    k.advance(sq_ready=8, sums_full=2, rstd_ready=2, normed=16, h_rounded=8, h_ready=8, tile_full=32, tile_free=32)
    k.sq = old_sq


def stage_delta(k, a):
    H, C = 4, 4
    cq, ck, cv = k.qkv[:, 0:4, :], k.qkv[:, 4:8, :], k.qkv[:, 8:12, :]
    small = lambda i: k.carve(14408 + 16 * i, (C, H))
    g, beta, G, expG, bexp, tail, tmp = (small(i) for i in range(7))
    EG = k.scr(4096, (H, 512))
    D = k.scr(6144, (H, 512))
    LT = k.scr(8192, (H, 512))
    attn = k.scr(10240, (H, 512))
    Kb, Kbar, Vb = k.scr(12288, (H, 512)), k.scr(14336, (H, 512)), k.scr(16384, (H, 512))
    X = k.scr(18432, (H, 512))
    g_wide, beta_wide = k.scr(10240, (16, P)), k.scr(12288, (16, P))
    sqs = k.scr(14336, (8, 512))
    rs = k.scr(6144, (8, 512))
    chunk = lambda t: t.rearrange("p h (c n) -> p h c n", c=C)
    by_head = lambda t: t[:, :, :].rearrange("p c h -> p h c")
    k.last_decay = k.carve(14392, (H, C))
    conv = k.prod
    sq, nf, rd = k.sem("delta_squares"), k.sem("delta_sums"), k.sem("delta_rstd")
    gates, wide, cum = k.sem("delta_gates"), k.sem("delta_wide"), k.sem("delta_cum")

    with k.nc.Block() as block:
        @block.scalar
        def _(act):
            L = lambda ins: k.act_chain.link(act, ins)
            gab = k.gab.rearrange("p (c n) -> p c n", c=C)
            L(act.activation(beta[:, :, :], gab[:, :, 4:8], ACT.Sigmoid))
            for n in range(8):
                act.activation(sqs[:, n, :], k.qkv[:, n, :], ACT.Square).then_inc(sq, 1)
            act.wait_ge(gates, 1)
            L(act.activation(tmp[:, :, :], g[:, :, :], ACT.Abs))
            L(act.activation(tmp[:, :, :], tmp[:, :, :], ACT.Exp, scale=-1.0))
            L(act.activation(k.decay_all[:, 0:4], k.decay_all[:, 0:4], ACT.Exp))
            L(act.activation(tmp[:, :, :], tmp[:, :, :], ACT.Ln, bias=1.0))
            act.sem_inc(gates, 1)
            for n in range(8):
                act.wait_ge(nf, n + 1)
                L(act.activation(rs[:, n, :], bank(k, n)[:, :], ACT.Ln, bias=k.eps[:, 0:1]))
            for n in range(8):
                act.activation(rs[:, n, :], rs[:, n, :], ACT.Exp, scale=-0.5).then_inc(rd, 1)

        @block.tensor
        def _(pe):
            for n in range(8):
                pe.wait_ge(sq, n + 1)
                pe.matmul(bank(k, n)[:, :], k.ones[:, :], sqs[:, n, :], start=True, stop=True).then_inc(nf, 1)
            pe.wait_ge(rd, 1)
            pe_warm(k, pe, 5, 0)

        @block.vector
        def _(dve):
            L = lambda ins: k.dve_chain.link(dve, ins)
            gab = k.gab.rearrange("p (c n) -> p c n", c=C)
            head_row = lambda cols: k.decay_all[:, cols:cols + 4].unsqueeze(1).broadcast_to([P, C, H])
            dve.tensor_tensor(g[:, :, :], gab[:, :, 0:4], head_row(4), ALU.add).then_inc(gates, 1)
            taps = VEC_ROWS["w_sconv_2"]
            for i in range(2):
                y = k.scc[:, i, :]
                L(dve.tensor_scalar(y, conv[:, i, 2:514], k.vec(taps + 4 + i), None, ALU.mult))
                L(dve.scalar_tensor_tensor(y, conv[:, i, 1:513], k.vec(taps + 2 + i), y, ALU.mult, ALU.add))
                L(dve.scalar_tensor_tensor(y, conv[:, i, 0:512], k.vec(taps + i), y, ALU.mult, ALU.add))
                L(dve.tensor_tensor(k.catT[:, i, :], y, k.scb[:, i, :], ALU.mult))
            dve.wait_ge(gates, 2)
            L(dve.scalar_tensor_tensor(g[:, :, :], g[:, :, :], 0.0, tmp[:, :, :], ALU.max, ALU.add))
            L(dve.scalar_tensor_tensor(g[:, :, :], g[:, :, :], -1.0, head_row(0), ALU.mult, ALU.mult))
            flat = lambda t: t[:, :, :].rearrange("p c h -> p (c h)").unsqueeze(2).broadcast_to([P, 16, P])
            ones = k.ones[:, :].unsqueeze(1).broadcast_to([P, 16, P])
            L(dve.tensor_tensor(g_wide[:, :, :], ones, flat(g), ALU.mult))
            L(dve.tensor_tensor(beta_wide[:, :, :], ones, flat(beta), ALU.mult))
            for n in range(8):
                dve.wait_ge(rd, n + 1)
                dst = k.qkv[:, n, :]
                dve.scalar_tensor_tensor(dst, dst, 128 ** -0.5 if n < 4 else 1.0, rs[:, n, :], ALU.mult, ALU.mult).then_inc(wide, 1)
            dve.wait_ge(wide, 8)

    gb, bb, st, ex, dc = (k.sem(n) for n in ("delta_G_wide", "delta_beta_wide", "delta_steps", "delta_exps", "delta_decay"))
    with k.nc.Block() as block:
        @block.tensor
        def _(pe):
            for h in range(H):
                for c in range(C):
                    mm = pe.matmul(bank(k, h)[:, c * P:(c + 1) * P], g_wide[:, c * H + h, :], k.triu[:, :], start=True, stop=True)
                mm.then_inc(gb, 1)
            pe.matmul(bank(k, 4)[:, 0:16], k.triu[:, :], g[:, :, :].rearrange("p c h -> p (c h)"), start=True, stop=True)\
                .then_inc(cum, 1)
            pe.wait_ge(st, 1)
            for h in range(H):
                for c in range(C):
                    mm = pe.matmul(bank(k, 4 + h)[:, c * P:(c + 1) * P], beta_wide[:, c * H + h, :], k.ident[:, :], start=True, stop=True)
                mm.then_inc(bb, 1)
            pe.wait_ge(dc, 5)
            pe_warm(k, pe, 4, 0)

        @block.vector
        def _(dve):
            L = lambda ins: k.dve_chain.link(dve, ins)
            dve.wait_ge(cum, 1)
            dve.tensor_copy(G[:, :, :].rearrange("p c h -> p (c h)"), bank(k, 4)[:, 0:16]).then_inc(st, 1)
            dve.wait_ge(st, 1)
            for h in range(H):
                dve.wait_ge(ex, h + 1)
                for c in range(C):
                    ins = dve.tensor_scalar(D[:, h, c * P:(c + 1) * P], bank(k, h)[:, c * P:(c + 1) * P], G[:, c, h:h + 1], 0.0,
                                            ALU.subtract, ALU.min)
                    ins.then_inc(dc, 1)
                dve.tensor_tensor(tail[:, :, h], bank(k, h)[:, P - 1:512:P], G[:, :, h], ALU.subtract).then_inc(dc, 1)
            dve.wait_ge(ex, 7)
            L(dve.tensor_tensor(bexp[:, :, :], beta[:, :, :], expG[:, :, :], ALU.mult))
            for h in range(H):
                dve.wait_ge(bb, h + 1)
                L(dve.tensor_tensor(LT[:, h, :], D[:, h, :], bank(k, 4 + h)[:, :], ALU.mult))

        @block.scalar
        def _(act):
            for h in range(H):
                act.wait_ge(gb, h + 1)
                act.activation(EG[:, h, :], bank(k, h)[:, :], ACT.Exp).then_inc(ex, 1)
            act.wait_ge(st, 1)
            act.activation(expG[:, :, :], G[:, :, :], ACT.Exp).then_inc(ex, 1)
            act.wait_ge(dc, 20)
            act.activation(tail[:, :, :], tail[:, :, :], ACT.Exp).then_inc(ex, 1)
            act.activation(D[:, :, :], D[:, :, :], ACT.Exp).then_inc(ex, 1)

    turned, used, prod_f, prod_r, qe_ready = (k.sem(n) for n in ("delta_turned", "delta_turned_used", "delta_prod", "delta_prod_used", "delta_qe"))
    with k.nc.Block() as block:
        @block.tensor
        def _(pe):
            for n in range(8):
                src = (ck, cv)[n % 2][:, n // 2, :]
                if n >= 4:
                    pe.wait_ge(used, n - 3)
                for c in range(C):
                    mm = pe.transpose(bank(k, n % 4)[:, c * P:(c + 1) * P], src[:, c * P:(c + 1) * P], k.ident[:, :])
                mm.then_inc(turned, 1)
            for n in range(8):
                h = n // 2
                if n >= 4:
                    pe.wait_ge(prod_r, n - 3)
                for c in range(C):
                    cs = slice(c * P, (c + 1) * P)
                    mm = pe.matmul(bank(k, 4 + n % 4)[:, cs], ck[:, h, cs], (ck, cq)[n % 2][:, h, cs], start=True, stop=True)
                mm.then_inc(prod_f, 1)

        @block.vector
        def _(dve):
            for h in range(H):
                k.dve_chain.link(dve, dve.tensor_tensor(chunk(D)[:, h], chunk(D)[:, h],
                                                        k.triu[:, :].unsqueeze(1).broadcast_to([P, C, P]), ALU.mult))
            for n in range(8):
                h = n // 2
                dve.wait_ge(turned, n + 1)
                src = bank(k, n % 4)[:, :].rearrange("p (c n) -> p c n", c=C)
                wide_of = lambda t: by_head(t)[:, h, :].unsqueeze(2).broadcast_to([P, C, P])
                if n % 2 == 0:
                    k.dve_chain.link(dve, dve.tensor_tensor(chunk(Kbar)[:, h], src, wide_of(tail), ALU.mult))
                    dve.tensor_tensor(chunk(Kb)[:, h], src, wide_of(bexp), ALU.mult).then_inc(used, 1)
                else:
                    dve.tensor_tensor(chunk(Vb)[:, h], src, wide_of(beta), ALU.mult).then_inc(used, 1)
            for n in range(8):
                h = n // 2
                dve.wait_ge(prod_f, n + 1)
                dst, w = (LT, LT) if n % 2 == 0 else (attn, D)
                dve.tensor_tensor(dst[:, h, :], bank(k, 4 + n % 4)[:, :], w[:, h, :], ALU.mult).then_inc(prod_r, 1)

        @block.gpsimd
        def _(pool):
            k.pool_chain.link(pool, pool.tensor_copy(k.last_decay[:, :, :], EG[:, :, P - 1:512:P]))
            for h in range(H):
                pool.tensor_tensor(EG[:, h, :], EG[:, h, :], cq[:, h, :], ALU.mult).then_inc(qe_ready, 1)
            pool.wait_ge(qe_ready, H)

    R = cv
    Y = k.carve(3080, (H, 512))
    Lm = k.scr(6144, (4, 512))
    lm, yf, yr, xf, xr, rf, rr = (k.sem(n) for n in ("inv_masked", "inv_y", "inv_y_out", "inv_x", "inv_x_out", "inv_r", "inv_r_out"))
    with k.nc.Block() as block:
        @block.gpsimd
        def _(pool):
            mask = lambda lv: k.level[:, lv, :].unsqueeze(1).broadcast_to([P, C, P])
            for lv in range(7):
                for h in range(H):
                    n = lv * H + h
                    if n >= 4:
                        pool.wait_ge(yf, n - 3)
                    if lv == 1:
                        pool.wait_ge(rr, h + 1)
                    pool.tensor_tensor(chunk(Lm)[:, n % 4], chunk(LT)[:, h], mask(lv), ALU.mult).then_inc(lm, 1)

        @block.tensor
        def _(pe):
            blocks = [slice(c * P, (c + 1) * P) for c in range(C)]
            for h in range(H):
                pe.wait_ge(lm, h + 1)
                if h >= 2:
                    pe.wait_ge(yr, h - 1)
                for cs in blocks:
                    mm = pe.transpose(bank(k, h % 2)[:, cs], Lm[:, h, cs], k.ident[:, :])
                mm.then_inc(yf, 1)
            for lv in range(1, 7):
                def first(h):
                    n = lv * H + h
                    pe.wait_ge(lm, n + 1)
                    pe.wait_ge(xr, (lv - 1) * H + h + 1)
                    pe.wait_ge(yr, n - 1)
                    for cs in blocks:
                        mm = pe.matmul(bank(k, n % 2)[:, cs], Lm[:, n % 4, cs], X[:, h, cs], start=True, stop=True)
                    mm.then_inc(yf, 1)

                def second(h):
                    n = lv * H + h
                    pe.wait_ge(yr, n + 1)
                    pe.wait_ge(rr, (lv - 1) * H + h + 1)
                    pe.wait_ge(rr, n - 1)
                    if lv < 6:
                        pe.wait_ge(xr, n - 1)
                        for cs in blocks:
                            mm = pe.matmul(bank(k, 2 + n % 2)[:, cs], R[:, h, cs], Y[:, h, cs], start=True, stop=True)
                        mm.then_inc(xf, 1)
                    for cs in blocks:
                        mm = pe.matmul(bank(k, 4 + n % 2)[:, cs], Y[:, h, cs], R[:, h, cs], start=True, stop=True)
                    mm.then_inc(rf, 1)

                first(0)
                for h in range(H):
                    if h < 3:
                        first(h + 1)
                    second(h)

        @block.scalar
        def _(act):
            for n in range(7 * H):
                act.wait_ge(yf, n + 1)
                if n >= 2 * H:
                    act.wait_ge(rf, n - 2 * H + 1)
                elif n >= H:
                    act.wait_ge(xr, n - H + 1)
                act.copy(Y[:, n % H, :], bank(k, n % 2)[:, :]).then_inc(yr, 1)

        @block.vector
        def _(dve):
            eyes = k.ident[:, :].unsqueeze(1).broadcast_to([P, C, P])
            for h in range(H):
                dve.wait_ge(lm, h + 1)
                dve.tensor_tensor(chunk(R)[:, h], eyes, chunk(Lm)[:, h], ALU.subtract).then_inc(rr, 1)
                dve.wait_ge(yr, h + 1)
                dve.tensor_tensor(chunk(X)[:, h], eyes, chunk(Y)[:, h], ALU.subtract).then_inc(xr, 1)
            for n in range(H, 7 * H):
                h = n % H
                if n < 6 * H:
                    dve.wait_ge(xf, n - H + 1)
                    dve.wait_ge(xr, n - H + 1)
                    dve.tensor_tensor(X[:, h, :], X[:, h, :], bank(k, 2 + n % 2)[:, :], ALU.subtract).then_inc(xr, 1)
                dve.wait_ge(rf, n - H + 1)
                dve.wait_ge(rr, n - H + 1)
                dve.tensor_tensor(R[:, h, :], R[:, h, :], bank(k, 4 + n % 2)[:, :], ALU.subtract).then_inc(rr, 1)

    S = [k.carve(5128 + i * 512, (H, P)) for i in range(2)]
    vn = [k.carve(6152 + i * 512, (H, P)) for i in range(2)]
    uw, uo = k.sem("delta_uw"), k.sem("delta_uw_out")
    with k.nc.Block() as block:
        @block.tensor
        def _(pe):
            for n in range(8):
                h = n // 2
                for c in range(C):
                    cs = slice(c * P, (c + 1) * P)
                    l, r = (R, Vb) if n % 2 == 0 else (Kb, R)
                    mm = pe.matmul(bank(k, n)[:, cs], l[:, h, cs], r[:, h, cs], start=True, stop=True)
                mm.then_inc(uw, 1)

        @block.scalar
        def _(act):
            for n in range(1, 8, 2):
                act.wait_ge(uw, n + 1)
                act.copy(Kb[:, n // 2, :], bank(k, n)[:, :]).then_inc(uo, 1)

        @block.vector
        def _(dve):
            for n in range(0, 8, 2):
                dve.wait_ge(uw, n + 1)
                dve.tensor_copy(Vb[:, n // 2, :], bank(k, n)[:, :]).then_inc(uo, 1)

    ws, vr, of, df, sr = (k.sem(n) for n in ("delta_ws", "delta_v_new", "delta_out", "delta_update", "delta_state"))
    o_sq, o_nf, o_rd = (k.sem(n) for n in ("delta_out_sq", "delta_out_sums", "delta_out_rstd"))
    o_sb, osq, rstd = k.scr(6144, (H, 512)), k.scr(8192, (H, 512)), k.scr(18432, (H, 512))
    with k.nc.Block() as block:
        @block.tensor
        def _(pe):
            for c in range(C):
                cs = slice(c * P, (c + 1) * P)
                s = S[(c - 1) % 2]
                if c:
                    pe.wait_ge(sr, c)
                    for h in range(H):
                        mm = pe.matmul(bank(k, 4)[:, h * P:(h + 1) * P], Kb[:, h, cs], s[:, h, :], start=True, stop=True)
                    mm.then_inc(ws, 1)
                    for h in range(H):
                        pe.matmul(bank(k, h)[:, cs], s[:, h, :], EG[:, h, cs], start=True, stop=False)
                pe.wait_ge(vr, c + 1)
                if c < C - 1:
                    for h in range(H):
                        mm = pe.matmul(bank(k, 5)[:, h * P:(h + 1) * P], Kbar[:, h, cs], vn[c % 2][:, h, :], start=True, stop=True)
                    mm.then_inc(df, 1)
                for h in range(H):
                    mm = pe.matmul(bank(k, h)[:, cs], vn[c % 2][:, h, :], attn[:, h, cs], start=(c == 0), stop=True)
            mm.then_inc(of, 1)
            for h in range(H):
                pe.wait_ge(o_sq, h + 1)
                pe.matmul(bank(k, 4 + h)[:, :], k.ones[:, :], osq[:, h, :], start=True, stop=True).then_inc(o_nf, 1)
            pe.wait_ge(o_rd, 1)
            pe_warm(k, pe, 5, 4)

        @block.vector
        def _(dve):
            L = lambda ins: k.dve_chain.link(dve, ins)
            for c in range(C):
                u = chunk(Vb)[:, :, c, :]
                if c == 0:
                    dve.tensor_copy(vn[0][:, :, :], u).then_inc(vr, 1)
                else:
                    dve.wait_ge(ws, c)
                    dve.tensor_tensor(vn[c % 2][:, :, :], u, bank(k, 4)[:, :].rearrange("p (h n) -> p h n", h=H), ALU.subtract)\
                        .then_inc(vr, 1)
                if c < C - 1:
                    dve.wait_ge(df, c + 1)
                    d = bank(k, 5)[:, :].rearrange("p (h n) -> p h n", h=H)
                    if c == 0:
                        dve.tensor_copy(S[0][:, :, :], d).then_inc(sr, 1)
                    else:
                        L(dve.tensor_tensor(S[c % 2][:, :, :], S[(c - 1) % 2][:, :, :],
                                            k.last_decay[:, :, c].unsqueeze(2).broadcast_to([P, H, P]), ALU.mult))
                        dve.tensor_tensor(S[c % 2][:, :, :], S[c % 2][:, :, :], d, ALU.add).then_inc(sr, 1)
            for h in range(H):
                dve.wait_ge(o_rd, h + 1)
                L(dve.scalar_tensor_tensor(o_sb[:, h, :], bank(k, h)[:, :], k.vec(VEC_ROWS["w_gdn_norm_2"]), rstd[:, h, :],
                                           ALU.mult, ALU.mult))
                L(dve.tensor_tensor(k.catT[:, 2 + h, :], o_sb[:, h, :], k.zT[:, h, :], ALU.mult))

        @block.scalar
        def _(act):
            act.wait_ge(of, 1)
            for h in range(H):
                act.activation(osq[:, h, :], bank(k, h)[:, :], ACT.Square, scale=P ** -0.5).then_inc(o_sq, 1)
            for h in range(H):
                act.wait_ge(o_nf, h + 1)
                k.act_chain.link(act, act.activation(rstd[:, h, :], bank(k, 4 + h)[:, :], ACT.Ln, bias=k.eps[:, 0:1]))
            for h in range(H):
                act.activation(rstd[:, h, :], rstd[:, h, :], ACT.Exp, scale=-0.5).then_inc(o_rd, 1)


def stage_stick(k):
    z = [[k.carve(3080 + par * 2560 + off, (512 - j * P,)) for j, off in enumerate((0, 512, 896, 1152))] for par in range(3)]
    sp_ = [[k.carve(4360 + par * 2560 + off, (512 - j * P,)) for j, off in enumerate((0, 512, 896, 1152))] for par in range(3)]
    zf, zc, za, zl, spr, tf, wr, ar, am, of, oc = (k.sem(n) for n in (
        "stick_z", "stick_z_copied", "stick_z_abs", "stick_logs", "stick_softplus", "stick_tail", "stick_exponent", "stick_exp", "stick_masked",
        "stick_full", "stick_out"))
    first = k.ring.took
    with k.nc.Block() as block:
        @block.sync
        def _(sp):
            stream(k, sp, first)

        @block.gpsimd
        def _(pool):
            for kk in range(6):
                k.pool_chain.link(pool, pool.tensor_copy(k.h_hi[:, kk, :], k.catT[:, kk, :]))
                k.pool_chain.link(pool, pool.tensor_tensor(k.h_lo[:, kk, :], k.catT[:, kk, :], k.h_hi[:, kk, :].bitcast(F32),
                                                           ALU.subtract))

        @block.tensor
        def _(pe):
            def scores(h):
                r = slice(h % 2 * 64, h % 2 * 64 + 64)
                for m, j in enumerate((3, 2, 1, 0)):
                    n = 4 * h + m
                    if n >= 2:
                        pe.wait_ge(za, n - 1)
                    pe.matmul(bank(k, n % 2)[:, 0:512 - j * P], k.sbk[r, h // 2, j * P:(j + 1) * P], k.sbq[r, h // 2, j * P:512],
                              start=True, stop=True).then_inc(zf, 1)

            def tails(h):
                for m, j in enumerate((3, 2, 1, 0)):
                    n = 4 * h + m
                    pe.wait_ge(spr, n + 1)
                    if n >= 2:
                        pe.wait_ge(wr, n - 1)
                    b = bank(k, 2 + n % 2)
                    mm = pe.matmul(b[:, 0:512 - j * P], k.tril[:, :], sp_[h % 3][j], start=True, stop=(j == 3))
                    for jj in range(j + 1, 4):
                        mm = pe.matmul(b[:, (jj - j) * P:512 - j * P], k.ones[:, :], sp_[h % 3][jj], start=False, stop=(jj == 3))
                    mm.then_inc(tf, 1)

            def values(h):
                if h >= 2:
                    pe.wait_ge(oc, h - 1)
                pe.wait_ge(am, 4 * (h + 1))
                for j in range(4):
                    mm = pe.matmul(bank(k, 4 + h % 2)[:, j * P:512], k.sbv[:, j, (h // 2) * P:(h // 2 + 1) * P], z[h % 3][j],
                                   start=(j == 0), stop=(j == 3))
                mm.then_inc(of, 1)

            scores(0)
            for h in range(4):
                if h < 3:
                    scores(h + 1)
                tails(h)
                if h >= 1:
                    values(h - 1)
            values(3)

        @block.scalar
        def _(act):
            L = lambda ins: k.act_chain.link(act, ins)

            def logs(h):
                if h >= 3:
                    act.wait_ge(of, h - 2)
                for m, j in enumerate((3, 2, 1, 0)):
                    n = 4 * h + m
                    act.wait_ge(zf, n + 1)
                    src = bank(k, n % 2)[:, 0:512 - j * P]
                    act.copy(z[h % 3][j], src).then_inc(zc, 1)
                    act.activation(sp_[h % 3][j], src, ACT.Abs).then_inc(za, 1)
                act.wait_ge(za, 4 * (h + 1))
                for j in (3, 2, 1, 0):
                    L(act.activation(sp_[h % 3][j], sp_[h % 3][j], ACT.Exp, scale=-1.0))
                for j in (3, 2, 1, 0):
                    act.activation(sp_[h % 3][j], sp_[h % 3][j], ACT.Ln, bias=1.0).then_inc(zl, 1)

            value = lambda kk: k.catT[:, kk, :]

            def finish(h):
                act.wait_ge(of, h + 1)
                r = slice(h % 2 * 64, h % 2 * 64 + 64)
                act.copy(k.catT[r, 6 + h // 2, :], bank(k, 4 + h % 2)[r, :]).then_inc(oc, 1)
                if h % 2:
                    act.wait_ge(oc, h + 1)
                    act_split(k, act, value, None, tiles=[6 + h // 2])

            logs(0)
            for h in range(4):
                if h < 3:
                    logs(h + 1)
                for m, j in enumerate((3, 2, 1, 0)):
                    act.wait_ge(wr, 4 * h + m + 1)
                    act.activation(z[h % 3][j], z[h % 3][j], ACT.Exp).then_inc(ar, 1)
                split_hi(k, act, first + h + 1)
                if h >= 1:
                    finish(h - 1)
            finish(3)

        @block.vector
        def _(dve):
            L = lambda ins: k.dve_chain.link(dve, ins)

            def softplus(h):
                for m, j in enumerate((3, 2, 1, 0)):
                    n = 4 * h + m
                    dve.wait_ge(zl, n + 1)
                    dve.wait_ge(zc, n + 1)
                    s = sp_[h % 3][j]
                    L(dve.scalar_tensor_tensor(s, z[h % 3][j], 0.0, s, ALU.max, ALU.add))
                    dve.tensor_tensor(s[:, 0:P], s[:, 0:P], k.triu_strict[:, :], ALU.mult).then_inc(spr, 1)

            def exponents(h):
                for m, j in enumerate((3, 2, 1, 0)):
                    n = 4 * h + m
                    dve.wait_ge(tf, n + 1)
                    dve.wait_ge(zc, n + 1)
                    w = z[h % 3][j]
                    L(dve.tensor_tensor(w, w, bank(k, 2 + n % 2)[:, 0:512 - j * P], ALU.subtract))
                    dve.tensor_scalar(w[:, 0:P], w[:, 0:P], 0.0, None, ALU.min).then_inc(wr, 1)

            def mask(h):
                for m, j in enumerate((3, 2, 1, 0)):
                    dve.wait_ge(ar, 4 * h + m + 1)
                    w = z[h % 3][j][:, 0:P]
                    dve.tensor_tensor(w, w, k.triu_strict[:, :], ALU.mult).then_inc(am, 1)

            value = lambda kk: k.catT[:, kk, :]
            softplus(0)
            for h in range(4):
                exponents(h)
                if h < 3:
                    softplus(h + 1)
                mask(h)
                split_lo(k, dve, first + h + 1)
                if h == 3:
                    dve_split(k, dve, value, 0, tiles=[6])
            dve_split(k, dve, value, 1, tiles=[7])
    k.advance(h_rounded=2, h_ready=2)


def stage_final(k, out):
    rows = k.carve(4096, (4, 1024))
    turned, copied, stored = k.sem("final_turned"), k.sem("final_copied"), k.sem("final_stored")
    with k.nc.Block() as block:
        @block.scalar
        def _(act):
            act_rstd(k, act)
            for n in range(8):
                act.wait_ge(turned, n + 1)
                act.copy(rows[:, n // 2, (n % 2) * 512:(n % 2 + 1) * 512], bank(k, n)[:, :]).then_inc(copied, 1)

        @block.vector
        def _(dve):
            dve.wait_ge(k.rstd_ready.sem, k.rstd_ready.at(1))
            dve_normed(k, dve, lambda kk: k.sq[:, kk, :], lambda kk: k.xT[:, kk, :], VEC_ROWS["w_norm_final_2"], 512)

        @block.tensor
        def _(pe):
            pe_warm(k, pe, 5)
            for n in range(8):
                pe.wait_ge(k.normed.sem, k.normed.at(4 * (n % 2 + 1)))
                for m in range(4):
                    kk = (n % 2) * 4 + m
                    mm = pe.transpose(bank(k, n)[:, m * P:(m + 1) * P], k.sq[:, kk, (n // 2) * P:(n // 2 + 1) * P], k.ident[:, :])
                mm.then_inc(turned, 1)

        @block.sync
        def _(sp):
            for n in range(8):
                sp.wait_ge(copied, n + 1)
                half = slice((n % 2) * 512, (n % 2 + 1) * 512)
                sp.dma_start(out[0, (n // 2) * P:(n // 2 + 1) * P, half], rows[:, n // 2, half]).then_inc(stored, 16)
            sp.wait_ge(stored, 128)


KEEP = 15400
DENSE_SCRATCH = 4096
MIXER_SCRATCH = 16900


def program(k, a, out):
    conv = lambda name: (lambda j: VEC_ROWS[name] + j * FT)

    def plain(*args):
        c = chunks_of(k, *args)
        return c, [1] * len(c)

    def counted(c, n):
        return c, [n] * len(c)

    def paired_out(w):
        return [x for cols in (0, 512) for x in (counted(paired_out_chunks(k, w, cols), 2),
                                                 counted(chunks_of(k, w, cols)[2:], 1))]

    w_mem, w_in, w_mix = a["w_mem_kv"], a["a_w_in"][0], a["w_mix_in_2"][0]
    return [
        (True, [plain(w_mem[l], cols) for l in range(2) for cols in (0, 512)] +
               [plain(w_in, cols) for cols in (0, 512, 1024, 1552)],
         [lambda: stage_setup(k, a), lambda: stage_memory(k, a), lambda: stage_gla_in(k, a)]),
        (False, [], [lambda: stage_gla(k, a)]),
        (True, [plain(a["a_w_out"][0], cols) for cols in (0, 512)] + [ffn_chunks(k, a["w_up"][0], a["w_down"][0])] +
               [counted(kv_chunks(k, a["w_kv"]), 4), plain(a["w_kv"], 256), plain(a["w_ck1"], 0, 256, 4),
                plain(a["w_cv1"], 0, 256, 4), counted(paired_query_chunks(k, a["b_w_in"][0]), 4),
                plain(a["b_w_in"][0], 536)],
         [lambda: stage_mem_attention(k, 0), lambda: stage_out_projection(k),
          lambda: stage_ffn(k, a["w_up"][0], VEC_ROWS["g_ffn0"], conv("conv_w0"), VEC_ROWS["conv_b0"], False),
          lambda: stage_nsa_in(k, a)]),
        (False, [], [lambda: stage_nsa(k)]),
        (True, paired_out(a["b_w_out"][0]) + [ffn_chunks(k, a["w_up"][1], a["w_down"][1])] +
               [plain(w_mix, 0), counted(mixed_chunks(k, w_mix, (512, 3336)), 2)] +
               [plain(w_mix, cols) for cols in (768, 1280, 1792, 2304, 2824)],
         [lambda: stage_mem_attention(k, 1), lambda: stage_out_projection(k),
          lambda: stage_ffn(k, a["w_up"][1], VEC_ROWS["g_ffn1"], conv("conv_w1"), VEC_ROWS["conv_b1"], False),
          lambda: stage_mix_in(k, a)]),
        (False, [], [lambda: stage_delta(k, a)]),
        (True, [plain(a["w_mix_out_2"][0], cols) for cols in (0, 512)] +
               [ffn_chunks(k, a["w_ffn_up_2"][0], a["w_ffn_down_2"][0])],
         [lambda: stage_stick(k), lambda: stage_out_projection(k),
          lambda: stage_ffn(k, a["w_ffn_up_2"][0], VEC_ROWS["w_norm_ffn_2"], lambda j: VEC_ROWS[f"ffn_conv2_{j}"], None, True),
          lambda: stage_final(k, out)]),
    ]


def build(nc, a, out, until=99, debug=None):
    k = K()
    k.nc = nc
    ctx = ExitStack()
    with ctx:
        def sb(name, shape, dt=F32):
            return ctx.enter_context(nc.sbuf_tensor(name, shape, dt))

        k.sem = lambda name: ctx.enter_context(nc.semaphore(name))
        k.xT = sb("xT", [P, 8, 512])
        k.h_hi, k.h_lo = sb("h_hi", [P, 8, 512], F32R), sb("h_lo", [P, 8, 512], F32R)
        k.vecs = sb("vecs", [P, VEC_TILES * P])
        k.ident, k.ones, k.triu, k.triu_strict, k.tril = (sb(n, [P, P]) for n in ("ident", "ones", "triu", "triu_strict", "tril"))
        k.level = sb("level", [P, 7, P])
        k.eps, k.spare, k.valid = sb("eps", [P, 1]), sb("spare", [P, 1]), sb("valid", [P, 1])
        k.rstd = sb("rstd", [P, 512])
        k.dist, k.dist_cmp = sb("dist", [P, 512]), sb("dist_cmp", [P, 4 * 31])
        k.keep = sb("keep", [P, KEEP])
        k.psum = [ctx.enter_context(nc.psum_tensor(f"bank{i}", [P, 512], F32)) for i in range(8)]
        k.vec = lambda c: k.vecs[:, c:c + 1]

        def carved(tensor, size, at, shape):
            n = 1
            for s in shape:
                n *= s
            assert at + n <= size, (at, shape)
            ap = tensor[:, at:at + n]
            if len(shape) == 2:
                return ap.rearrange("p (a b) -> p a b", a=shape[0])
            if len(shape) == 3:
                return ap.rearrange("p (a b c) -> p a b c", a=shape[0], b=shape[1])
            return ap

        k.carve = lambda at, shape: carved(k.keep, KEEP, at, shape)
        k.sq = k.carve(0, (8, 512))
        k.mkT = k.carve(KEEP - 4096, (2, 4, 256))
        k.mv = k.carve(KEEP - 2048, (2, 2, 512))
        k.memT = k.carve(9216, (8, 256))
        scratch = sb("scratch", [P, DENSE_SCRATCH])
        k.catT = carved(scratch, DENSE_SCRATCH, 0, (8, 512))
        signals = {name: Signal(k.sem(name)) for name in
                   ("tile_full", "tile_free", "sq_ready", "sq_added", "sums_full", "rstd_ready", "normed", "h_rounded", "h_ready")}
        k.tile_full, k.tile_free = signals["tile_full"], signals["tile_free"]
        k.sq_ready, k.sq_added, k.sums_full, k.rstd_ready = signals["sq_ready"], signals["sq_added"], signals["sums_full"], signals["rstd_ready"]
        k.normed, k.h_rounded, k.h_ready = signals["normed"], signals["h_rounded"], signals["h_ready"]
        k.ma_sig = [Signal(k.sem("mem_" + n)) for n in ("scores", "lows", "exps", "probs", "turned", "turned_out", "full", "out")]
        k.ffn_sig = [Signal(k.sem("ffn_" + n)) for n in
                     ("padded", "conv_a", "conv_b", "silu", "done", "cleared", "product_hi", "product_lo")]

        def advance(**counts):
            for name, n in counts.items():
                signals[name].base += n

        k.advance = advance
        k.dve_chain, k.act_chain, k.pool_chain = (Chain(k.sem(n)) for n in ("vector_order", "scalar_order", "pool_order"))
        phases = program(k, a, out)
        k.plan, loads, ends = [], [], []
        for _, groups, _ in phases:
            for chunks, counts in groups:
                k.plan.extend(chunks)
                loads.extend(counts)
            ends.append(len(k.plan))
        k.ring = Ring([k.sem(f"weights_in{i}") for i in range(RING)], k.sem("weights_hi"), k.sem("weights_lo"),
                      k.sem("weights_used"), loads)
        ran = 0
        for number, (dense, _, stages) in enumerate(phases):
            k.phase_end = ends[number]
            with ExitStack() as phase:
                k.scope = lambda name, shape, dt: phase.enter_context(nc.sbuf_tensor(f"{name}_{number}", shape, dt))
                if dense:
                    k.raw = [k.scope(f"raw{i}", [P, SLOT], F32) for i in range(RING)]
                    k.w_hi = [k.scope(f"w_hi{i}", [P, SLOT], F32R) for i in range(RING)]
                    k.w_lo = [k.scope(f"w_lo{i}", [P, SLOT], F32R) for i in range(RING)]
                    k.scr = lambda at, shape: carved(scratch, DENSE_SCRATCH, at, shape)
                else:
                    more = k.scope("more_scratch", [P, MIXER_SCRATCH], F32)
                    k.scr = lambda at, shape: carved(more, MIXER_SCRATCH, at - DENSE_SCRATCH, shape)
                for stage in stages:
                    if ran < until:
                        stage()
                    ran += 1
                if debug and ran >= until:
                    debug(k, ctx)
                    debug = None
                    until = 0


_INS = ['x', 'mem', 'g_mix', 'g_ffn', 'g_mem', 'w_mem_kv', 'w_up', 'conv_w', 'conv_b', 'w_down', 'a_w_in', 'a_w_alpha',
        'a_b_alpha', 'a_g_head', 'a_w_out', 'g_kv', 'w_kv', 'pe_k', 'pe_v', 'w_ck1', 'w_ck2', 'w_cv1', 'w_cv2', 'b_w_in',
        'b_w_out', 'g_final', 'w_norm_mix_2', 'w_mix_in_2', 'w_sconv_2', 'w_gdn_conv_2', 'gdn_a_log_2', 'gdn_dt_bias_2',
        'w_gdn_norm_2', 'w_mix_out_2', 'w_norm_ffn_2', 'w_ffn_up_2', 'w_ffn_conv_2', 'w_ffn_down_2', 'w_norm_final_2']
_OUT = ((1, 512, 1024), 'float32')


def kernel(**inputs):
    import numpy as _np
    import concourse.bacc as _bacc
    from concourse import mybir as _mybir
    from concourse.bass_utils import run_bass_kernel_spmd as _run

    nc = _bacc.Bacc("TRN2", target_bir_lowering=False, num_devices=1)
    arrays, args = {}, {}
    for name in _INS:
        v = _np.ascontiguousarray(inputs[name])
        arrays[f"in_{name}"] = v
        args[name] = nc.dram_tensor(f"in_{name}", v.shape, _mybir.dt.from_np(v.dtype), kind="ExternalInput").ap()
    out = nc.dram_tensor("out", _OUT[0], _mybir.dt.from_np(_np.dtype(_OUT[1])), kind="ExternalOutput").ap()
    build(nc, args, out)
    r = _run(nc, [arrays], core_ids=[0])
    return r.results[0]["out"]
```
